# Optimizing a Trainium2 kernel written in Bass

```python
import jax, jax.numpy as jnp
from jax import lax
import numpy as np

D_MODEL = 1024
BATCH = 1
SEQ = 512
DEPTH = 2

GRID_W = 64
CTX_LEN = 256
FOUR_GROUPS = 4
FOUR_GC = D_MODEL // 8
FOUR_WIDTH = FOUR_GROUPS * FOUR_GC
NA_HEADS = 8
NA_HEAD_DIM = D_MODEL // 16
NA_WIDTH = NA_HEADS * NA_HEAD_DIM
NA_WIN_ROWS = 8
NA_WIN_COLS = 16
POOL_SIZES = (2, 4, 8, 16)
POOL_GC = D_MODEL // len(POOL_SIZES)
MLP_HIDDEN = 4 * D_MODEL
N_MOD = 6
RMS_EPS = 1e-6
N_EVEN = (DEPTH + 1) // 2
N_ODD = DEPTH // 2


def rms_norm(x, g):
    xf = x.astype(jnp.float32)
    y = xf * lax.rsqrt(jnp.mean(xf * xf, axis=-1, keepdims=True) + RMS_EPS)
    return (y * g.astype(jnp.float32)).astype(x.dtype)

def modulate(xn, shift, scale):
    return xn * (1.0 + scale) + shift

def sq_relu_mlp(u, w1, w2):
    a = jnp.maximum(u @ w1, 0.0)
    return (a * a) @ w2

def fourier_mix(f, w_four):
    B, N, _ = f.shape
    fg = f.reshape(B, N, FOUR_GROUPS, FOUR_GC).transpose(0, 2, 1, 3)
    mixed = jnp.fft.fft2(fg.astype(jnp.float32), norm="ortho").real.astype(f.dtype)
    out = jnp.einsum('bgnc,gcd->bngd', mixed, w_four)
    return out.reshape(B, N, FOUR_WIDTH)

def neighbourhood_attention(q, k, v, k_ctx, v_ctx, rpb):
    B, N, H, dh = q.shape
    rows = N // GRID_W
    wr = min(NA_WIN_ROWS, rows)

    def to_grid(a):
        return a.reshape(B, rows, GRID_W, H, dh).transpose(0, 3, 1, 2, 4)

    qg, kg, vg = to_grid(q), to_grid(k), to_grid(v)
    r = jnp.arange(rows)
    row_start = jnp.clip(r - wr // 2, 0, rows - wr)
    row_idx = row_start[:, None] + jnp.arange(wr)[None, :]
    kb = kg[:, :, row_idx]
    vb = vg[:, :, row_idx]
    cidx = jnp.arange(GRID_W)
    col_start = jnp.clip(cidx - NA_WIN_COLS // 2, 0, GRID_W - NA_WIN_COLS)
    col_mask = (cidx[None, :] >= col_start[:, None]) & (cidx[None, :] < col_start[:, None] + NA_WIN_COLS)
    dr = row_idx - r[:, None] + (NA_WIN_ROWS - 1)
    dc = jnp.clip(cidx[None, :] - cidx[:, None] + (NA_WIN_COLS - 1), 0, 2 * NA_WIN_COLS - 2)
    bias = rpb[:, dr[:, None, :, None], dc[None, :, None, :]]
    scale = dh ** -0.5
    s_win = jnp.einsum('bhrqd,bhrjkd->bhrqjk', qg, kb).astype(jnp.float32) * scale + bias.astype(jnp.float32)
    s_win = jnp.where(col_mask[:, None, :], s_win, -jnp.inf)
    s_win = s_win.reshape(B, H, rows, GRID_W, wr * GRID_W)
    s_ctx = jnp.einsum('bhrqd,blhd->bhrql', qg, k_ctx).astype(jnp.float32) * scale
    p = jax.nn.softmax(jnp.concatenate([s_win, s_ctx], axis=-1), axis=-1)
    p_win = p[..., :wr * GRID_W].reshape(B, H, rows, GRID_W, wr, GRID_W).astype(v.dtype)
    p_ctx = p[..., wr * GRID_W:].astype(v.dtype)
    o = jnp.einsum('bhrqjk,bhrjkd->bhrqd', p_win, vb) + jnp.einsum('bhrql,blhd->bhrqd', p_ctx, v_ctx)
    return o.transpose(0, 2, 3, 1, 4).reshape(B, N, H * dh)

def context_attention(qc, kc, vc):
    B, L, H, dh = qc.shape
    s = jnp.einsum('blhd,bmhd->bhlm', qc, kc).astype(jnp.float32) * (dh ** -0.5)
    p = jax.nn.softmax(s, axis=-1).astype(vc.dtype)
    return jnp.einsum('bhlm,bmhd->blhd', p, vc).reshape(B, L, H * dh)

def split_heads(a):
    return a.reshape(a.shape[0], a.shape[1], NA_HEADS, NA_HEAD_DIM)

def even_mixer(u, uc, w_in, w_four, q_g, k_g, rpb, w_out, update_ctx):
    p = u @ w_in
    f, q, k, v = jnp.split(p, [FOUR_WIDTH, FOUR_WIDTH + NA_WIDTH, FOUR_WIDTH + 2 * NA_WIDTH], axis=-1)
    q = rms_norm(split_heads(q), q_g)
    k = rms_norm(split_heads(k), k_g)
    v = split_heads(v)
    kvc = uc @ w_in[:, FOUR_WIDTH + NA_WIDTH:]
    kc, vc = jnp.split(kvc, [NA_WIDTH], axis=-1)
    kc = rms_norm(split_heads(kc), k_g)
    vc = split_heads(vc)
    o_four = fourier_mix(f, w_four)
    o_na = neighbourhood_attention(q, k, v, kc, vc, rpb)
    y = jnp.concatenate([o_four, o_na], axis=-1) @ w_out
    if not update_ctx:
        return y, None
    fc, qc = jnp.split(uc @ w_in[:, :FOUR_WIDTH + NA_WIDTH], [FOUR_WIDTH], axis=-1)
    qc = rms_norm(split_heads(qc), q_g)
    yc = jnp.concatenate([fourier_mix(fc, w_four), context_attention(qc, kc, vc)], axis=-1) @ w_out
    return y, yc

def multiscale_pool(u):
    N = u.shape[1]
    uf = u.astype(jnp.float32)
    zeros = jnp.zeros((uf.shape[0], 1, uf.shape[2]), jnp.float32)
    cs = jnp.concatenate([zeros, jnp.cumsum(uf, axis=1)], axis=1)
    t = jnp.arange(N)
    outs = []
    for gi, w in enumerate(POOL_SIZES):
        sl = slice(gi * POOL_GC, (gi + 1) * POOL_GC)
        lo = jnp.clip(t - w // 2, 0, N)
        hi = jnp.clip(t + w - w // 2, 0, N)
        csg = cs[..., sl]
        s = jnp.take(csg, hi, axis=1) - jnp.take(csg, lo, axis=1)
        cnt = (hi - lo).astype(jnp.float32)[None, :, None]
        outs.append(s / cnt - uf[..., sl])
    return jnp.concatenate(outs, axis=-1).astype(u.dtype)

def pool_mixer(u, w_pool, pool_scale):
    B, N, _ = u.shape
    pooled = multiscale_pool(u).reshape(B, N, len(POOL_SIZES), POOL_GC)
    y = jnp.einsum('bngc,gcd->bngd', pooled, w_pool).reshape(B, N, D_MODEL)
    return y * pool_scale

def first_inputs(seed: int = 0) -> dict:
    key = jax.random.key(seed)
    ks = jax.random.split(key, 20)
    f32 = jnp.float32
    n = lambda k, s: jax.random.normal(k, s, f32)
    return {
        "x": n(ks[0], (BATCH, SEQ, D_MODEL)),
        "c": n(ks[1], (BATCH, D_MODEL)),
        "ctx": n(ks[2], (BATCH, CTX_LEN, D_MODEL)),
        "c_ctx": n(ks[3], (D_MODEL,)),
        "w_mod": n(ks[4], (DEPTH, D_MODEL, N_MOD * D_MODEL)) * D_MODEL ** -0.5,
        "b_mod": n(ks[5], (DEPTH, N_MOD * D_MODEL)) * 0.02,
        "norm1_g": 1.0 + 0.02 * n(ks[6], (DEPTH, D_MODEL)),
        "norm2_g": 1.0 + 0.02 * n(ks[7], (DEPTH, D_MODEL)),
        "w_in_even": n(ks[8], (N_EVEN, D_MODEL, FOUR_WIDTH + 3 * NA_WIDTH)) * D_MODEL ** -0.5,
        "w_four": n(ks[9], (N_EVEN, FOUR_GROUPS, FOUR_GC, FOUR_GC)) * FOUR_GC ** -0.5,
        "q_norm_g": 1.0 + 0.02 * n(ks[10], (N_EVEN, NA_HEAD_DIM)),
        "k_norm_g": 1.0 + 0.02 * n(ks[11], (N_EVEN, NA_HEAD_DIM)),
        "rpb": 0.1 * n(ks[12], (N_EVEN, NA_HEADS, 2 * NA_WIN_ROWS - 1, 2 * NA_WIN_COLS - 1)),
        "w_out_even": n(ks[13], (N_EVEN, FOUR_WIDTH + NA_WIDTH, D_MODEL)) * (FOUR_WIDTH + NA_WIDTH) ** -0.5,
        "w_pool": n(ks[14], (N_ODD, len(POOL_SIZES), POOL_GC, POOL_GC)) * POOL_GC ** -0.5,
        "pool_scale": 1.0 + 0.1 * n(ks[15], (N_ODD, D_MODEL)),
        "w_mlp1": n(ks[16], (DEPTH, D_MODEL, MLP_HIDDEN)) * D_MODEL ** -0.5,
        "w_mlp2": n(ks[17], (DEPTH, MLP_HIDDEN, D_MODEL)) * MLP_HIDDEN ** -0.5,
    }

def first_block(x, c, ctx, c_ctx, w_mod, b_mod, norm1_g, norm2_g, w_in_even, w_four, q_norm_g, k_norm_g,
              rpb, w_out_even, w_pool, pool_scale, w_mlp1, w_mlp2):
    h, hc = x, ctx
    sc = jax.nn.silu(c)
    scc = jax.nn.silu(c_ctx)
    for l in range(DEPTH):
        update_ctx = any(j % 2 == 0 for j in range(l + 1, DEPTH))
        need_ctx_in = (l % 2 == 0) or update_ctx
        mod = (sc @ w_mod[l] + b_mod[l])[:, None, :]
        sh1, sc1, g1, sh2, sc2, g2 = jnp.split(mod, N_MOD, axis=-1)
        u = modulate(rms_norm(h, norm1_g[l]), sh1, sc1)
        if need_ctx_in:
            mod_c = scc @ w_mod[l] + b_mod[l]
            csh1, csc1, cg1, csh2, csc2, cg2 = jnp.split(mod_c, N_MOD, axis=-1)
            uc = modulate(rms_norm(hc, norm1_g[l]), csh1, csc1)
        if l % 2 == 0:
            e = l // 2
            y, yc = even_mixer(u, uc, w_in_even[e], w_four[e], q_norm_g[e], k_norm_g[e], rpb[e],
                               w_out_even[e], update_ctx)
        else:
            o = l // 2
            y = pool_mixer(u, w_pool[o], pool_scale[o])
            yc = pool_mixer(uc, w_pool[o], pool_scale[o]) if update_ctx else None
        h = h + g1 * y
        h = h + g2 * sq_relu_mlp(modulate(rms_norm(h, norm2_g[l]), sh2, sc2), w_mlp1[l], w_mlp2[l])
        if update_ctx:
            hc = hc + cg1 * yc
            hc = hc + cg2 * sq_relu_mlp(modulate(rms_norm(hc, norm2_g[l]), csh2, csc2), w_mlp1[l], w_mlp2[l])
    return h


DEPTH_2 = 1

MEM_LEN = 256

HEAD_DIM = 64
NSA_HEADS = D_MODEL // 128
NSA_KV_HEADS = NSA_HEADS // 4
NSA_GROUP = NSA_HEADS // NSA_KV_HEADS
NSA_WIDTH = NSA_HEADS * HEAD_DIM
NSA_KV_WIDTH = NSA_KV_HEADS * HEAD_DIM
CMP_BLOCK = 32
CMP_STRIDE = 16
CMP_HIDDEN = 2 * HEAD_DIM
SLC_BLOCK = 64
N_SELECT = 8
WINDOW = 256
NSA_QBLOCK = SLC_BLOCK

GLA_HEADS = 4
GLA_DK = 64
GLA_DV = 128
GLA_KEY_WIDTH = GLA_HEADS * GLA_DK
GLA_VAL_WIDTH = GLA_HEADS * GLA_DV
GLA_GATE_RANK = 16
GLA_TAU = 16.0
GLA_CHUNK = 64

XATTN_HEADS = 4
XATTN_HEAD_DIM = 128
XATTN_WIDTH = XATTN_HEADS * XATTN_HEAD_DIM

FFN_DIM = 2816
CONV_WIDTH = 3

NEG_INF = -1e30

IN_SPLITS = (NSA_WIDTH, 6 * NSA_KV_WIDTH, 3 * NSA_HEADS,
             GLA_KEY_WIDTH, GLA_KEY_WIDTH, GLA_VAL_WIDTH, GLA_VAL_WIDTH, GLA_GATE_RANK,
             2 * D_MODEL)
IN_WIDTH = (NSA_WIDTH + 6 * NSA_KV_WIDTH + 3 * NSA_HEADS + 2 * GLA_KEY_WIDTH
            + 2 * GLA_VAL_WIDTH + GLA_GATE_RANK + 2 * D_MODEL)


def rms_norm_2(x, g):
    x32 = x.astype(jnp.float32)
    y = x32 * lax.rsqrt(jnp.mean(x32 * x32, axis=-1, keepdims=True) + RMS_EPS)
    return (y * g.astype(jnp.float32)).astype(x.dtype)

def alibi_slopes(n):
    return 2.0 ** (-8.0 * jnp.arange(1, n + 1, dtype=jnp.float32) / n)

def masked_softmax(s, mask):
    s = jnp.where(mask, s, NEG_INF)
    return jnp.where(mask, jax.nn.softmax(s, axis=-1), 0.0)

def compress_blocks(kv, pos_emb, w1, w2):
    B, S, H, dh = kv.shape
    c = kv.reshape(B, S // CMP_STRIDE, CMP_STRIDE, H, dh)
    blocks = jnp.concatenate([c[:, :-1], c[:, 1:]], axis=2) + pos_emb[None, None, :, None, :]
    n_cmp = blocks.shape[1]
    flat = blocks.transpose(0, 1, 3, 2, 4).reshape(B, n_cmp, H, CMP_BLOCK * dh)
    return jax.nn.gelu(flat @ w1) @ w2

def nsa_attention(q, kc, vc, ks, vs, kw, vw, gate_logits,
                  cmp_pos_k, cmp_w1_k, cmp_w2_k, cmp_pos_v, cmp_w1_v, cmp_w2_v):
    B, S = q.shape[:2]
    f32 = jnp.float32
    q = q.reshape(B, S, NSA_KV_HEADS, NSA_GROUP, HEAD_DIM) * (HEAD_DIM ** -0.5)
    kv_shape = (B, S, NSA_KV_HEADS, HEAD_DIM)
    kc, vc, ks, vs, kw, vw = [a.reshape(kv_shape) for a in (kc, vc, ks, vs, kw, vw)]
    gates = jax.nn.sigmoid(gate_logits.astype(f32)).reshape(B, S, NSA_KV_HEADS, NSA_GROUP, 3)
    slopes = alibi_slopes(NSA_HEADS).reshape(NSA_KV_HEADS, NSA_GROUP)

    k_cmp = compress_blocks(kc, cmp_pos_k, cmp_w1_k, cmp_w2_k)
    v_cmp = compress_blocks(vc, cmp_pos_v, cmp_w1_v, cmp_w2_v)
    n_cmp = k_cmp.shape[1]
    cmp_end = jnp.arange(n_cmp) * CMP_STRIDE + CMP_BLOCK - 1

    n_slc = S // SLC_BLOCK
    n_sel = min(N_SELECT, n_slc)
    cmp_tok = jnp.arange(n_cmp)[:, None] * CMP_STRIDE + jnp.arange(CMP_BLOCK)[None, :]
    overlap = jax.nn.one_hot(cmp_tok // SLC_BLOCK, n_slc, dtype=f32).sum(axis=1) / CMP_BLOCK

    ks_blk = ks.reshape(B, n_slc, SLC_BLOCK, NSA_KV_HEADS, HEAD_DIM).transpose(0, 3, 1, 2, 4)
    vs_blk = vs.reshape(B, n_slc, SLC_BLOCK, NSA_KV_HEADS, HEAD_DIM).transpose(0, 3, 1, 2, 4)
    kw_pad = jnp.pad(kw, ((0, 0), (WINDOW, 0), (0, 0), (0, 0)))
    vw_pad = jnp.pad(vw, ((0, 0), (WINDOW, 0), (0, 0), (0, 0)))
    b_ix = jnp.arange(B)[:, None, None, None]
    h_ix = jnp.arange(NSA_KV_HEADS)[None, :, None, None]
    forced_score = float(NSA_GROUP + 1)

    def query_block(i):
        t0 = i * NSA_QBLOCK
        qb = lax.dynamic_slice_in_dim(q, t0, NSA_QBLOCK, axis=1)
        gb = lax.dynamic_slice_in_dim(gates, t0, NSA_QBLOCK, axis=1)
        t = t0 + jnp.arange(NSA_QBLOCK)

        dist = (t[:, None] - cmp_end[None, :]).astype(f32)
        s = jnp.einsum('bqhgd,bnhd->bhgqn', qb, k_cmp).astype(f32)
        s = s - slopes[:, :, None, None] * dist
        p_cmp = masked_softmax(s, dist >= 0)
        o_cmp = jnp.einsum('bhgqn,bnhd->bqhgd', p_cmp.astype(v_cmp.dtype), v_cmp)

        imp = jnp.einsum('bhgqn,nj->bhqj', p_cmp, overlap)
        cur = t // SLC_BLOCK
        j = jnp.arange(n_slc)
        forced = (j[None, :] == 0) | (j[None, :] == cur[:, None]) | (j[None, :] == cur[:, None] - 1)
        future = j[None, :] > cur[:, None]
        imp = jnp.where(forced, forced_score, jnp.where(future, -1.0, imp))
        _, idx = lax.top_k(imp, n_sel)
        kg = ks_blk[b_ix, h_ix, idx]
        vg = vs_blk[b_ix, h_ix, idx]
        kpos = idx[..., None] * SLC_BLOCK + jnp.arange(SLC_BLOCK)
        dist = (t[:, None, None] - kpos).astype(f32)[:, :, None]
        s = jnp.einsum('bqhgd,bhqnld->bhgqnl', qb, kg).astype(f32)
        s = s - slopes[None, :, :, None, None, None] * dist
        n_keys = n_sel * SLC_BLOCK
        s = s.reshape(B, NSA_KV_HEADS, NSA_GROUP, NSA_QBLOCK, n_keys)
        mask = (dist >= 0).reshape(B, NSA_KV_HEADS, 1, NSA_QBLOCK, n_keys)
        p_slc = masked_softmax(s, mask)
        vg = vg.reshape(B, NSA_KV_HEADS, NSA_QBLOCK, n_keys, HEAD_DIM)
        o_slc = jnp.einsum('bhgqk,bhqkd->bqhgd', p_slc.astype(vg.dtype), vg)

        kwb = lax.dynamic_slice_in_dim(kw_pad, t0, NSA_QBLOCK + WINDOW, axis=1)
        vwb = lax.dynamic_slice_in_dim(vw_pad, t0, NSA_QBLOCK + WINDOW, axis=1)
        kpos = t0 - WINDOW + jnp.arange(NSA_QBLOCK + WINDOW)
        dist_i = t[:, None] - kpos[None, :]
        mask = (dist_i >= 0) & (dist_i < WINDOW) & (kpos[None, :] >= 0)
        s = jnp.einsum('bqhgd,bkhd->bhgqk', qb, kwb).astype(f32)
        s = s - slopes[:, :, None, None] * dist_i.astype(f32)
        p_win = masked_softmax(s, mask)
        o_win = jnp.einsum('bhgqk,bkhd->bqhgd', p_win.astype(vwb.dtype), vwb)

        return gb[..., 0:1] * o_cmp + gb[..., 1:2] * o_slc + gb[..., 2:3] * o_win

    out = lax.map(query_block, jnp.arange(S // NSA_QBLOCK))
    out = out.transpose(1, 0, 2, 3, 4, 5).reshape(B, S, NSA_WIDTH)
    return out.astype(q.dtype)

def gla(q, k, v, r, a_low, w_alpha2, b_alpha, norm_g):
    B, S = q.shape[:2]
    f32 = jnp.float32
    nc = S // GLA_CHUNK
    shp_k = (B, nc, GLA_CHUNK, GLA_HEADS, GLA_DK)
    shp_v = (B, nc, GLA_CHUNK, GLA_HEADS, GLA_DV)
    q = q.reshape(shp_k).astype(f32) * (GLA_DK ** -0.5)
    k = k.reshape(shp_k).astype(f32)
    v = v.reshape(shp_v).astype(f32)
    log_a = jax.nn.log_sigmoid((a_low @ w_alpha2 + b_alpha).astype(f32)) / GLA_TAU
    b = jnp.cumsum(log_a.reshape(shp_k), axis=2)
    b_last = b[:, :, -1:]
    q_d = q * jnp.exp(b)
    k_d = k * jnp.exp(-b)
    k_s = k * jnp.exp(b_last - b)
    causal = jnp.tril(jnp.ones((GLA_CHUNK, GLA_CHUNK), dtype=bool))
    att = jnp.where(causal, jnp.einsum('bnihd,bnjhd->bnhij', q_d, k_d), 0.0)
    o_intra = jnp.einsum('bnhij,bnjhe->bnihe', att, v)
    state_inc = jnp.einsum('bnjhd,bnjhe->bnhde', k_s, v)
    decay = jnp.exp(b_last[:, :, 0])

    def step(state, xs):
        dec, inc = xs
        return dec[..., None] * state + inc, state

    init = jnp.zeros((B, GLA_HEADS, GLA_DK, GLA_DV), f32)
    _, states = lax.scan(step, init, (decay.swapaxes(0, 1), state_inc.swapaxes(0, 1)))
    states = states.swapaxes(0, 1)
    o_inter = jnp.einsum('bnihd,bnhde->bnihe', q_d, states)
    o = (o_intra + o_inter).reshape(B, S, GLA_HEADS, GLA_DV)
    o = o * lax.rsqrt(jnp.mean(o * o, axis=-1, keepdims=True) + RMS_EPS) * norm_g.astype(f32)
    o = o * jax.nn.silu(r.reshape(B, S, GLA_HEADS, GLA_DV).astype(f32))
    return o.reshape(B, S, GLA_VAL_WIDTH).astype(r.dtype)

def memory_cross_attention(h, mem_n, w_xq, w_xkv, w_xo):
    B, S = h.shape[:2]
    M = mem_n.shape[1]
    q = (h @ w_xq).reshape(B, S, XATTN_HEADS, XATTN_HEAD_DIM) * (XATTN_HEAD_DIM ** -0.5)
    k, v = jnp.split(mem_n @ w_xkv, 2, axis=-1)
    k = k.reshape(B, M, XATTN_HEADS, XATTN_HEAD_DIM)
    v = v.reshape(B, M, XATTN_HEADS, XATTN_HEAD_DIM)
    p = jax.nn.softmax(jnp.einsum('bshd,bmhd->bhsm', q, k).astype(jnp.float32), axis=-1)
    o = jnp.einsum('bhsm,bmhd->bshd', p.astype(v.dtype), v).reshape(B, S, XATTN_WIDTH)
    return o @ w_xo

def conv_ffn(h, w_up, conv_w, conv_b, w_down):
    S = h.shape[1]
    u, g = jnp.split(h @ w_up, 2, axis=-1)
    u_pad = jnp.pad(u, ((0, 0), (CONV_WIDTH - 1, 0), (0, 0)))
    u = sum(conv_w[tap] * u_pad[:, tap:tap + S] for tap in range(CONV_WIDTH)) + conv_b
    return (jax.nn.gelu(u) * g) @ w_down

def second_inputs(seed: int = 0) -> dict:
    key = jax.random.key(seed)
    ks = jax.random.split(key, 28)
    f32 = jnp.float32
    L = DEPTH_2

    def dense(k, shape, fan_in):
        return jax.random.normal(k, shape, f32) * fan_in ** -0.5

    def gain(k, shape):
        return 1.0 + 0.02 * jax.random.normal(k, shape, f32)

    def small(k, shape, scale):
        return scale * jax.random.normal(k, shape, f32)

    return {
        "x": jax.random.normal(ks[0], (BATCH, SEQ, D_MODEL), f32),
        "mem": jax.random.normal(ks[1], (BATCH, MEM_LEN, D_MODEL), f32),
        "ln_mix_g": gain(ks[2], (L, D_MODEL)),
        "w_in": dense(ks[3], (L, D_MODEL, IN_WIDTH), D_MODEL),
        "nsa_gate_b": small(ks[4], (L, 3 * NSA_HEADS), 0.1),
        "cmp_pos_k": small(ks[5], (L, CMP_BLOCK, HEAD_DIM), 0.1),
        "cmp_w1_k": dense(ks[6], (L, CMP_BLOCK * HEAD_DIM, CMP_HIDDEN), CMP_BLOCK * HEAD_DIM),
        "cmp_w2_k": dense(ks[7], (L, CMP_HIDDEN, HEAD_DIM), CMP_HIDDEN),
        "cmp_pos_v": small(ks[8], (L, CMP_BLOCK, HEAD_DIM), 0.1),
        "cmp_w1_v": dense(ks[9], (L, CMP_BLOCK * HEAD_DIM, CMP_HIDDEN), CMP_BLOCK * HEAD_DIM),
        "cmp_w2_v": dense(ks[10], (L, CMP_HIDDEN, HEAD_DIM), CMP_HIDDEN),
        "gla_w_alpha2": dense(ks[11], (L, GLA_GATE_RANK, GLA_KEY_WIDTH), GLA_GATE_RANK),
        "gla_b_alpha": small(ks[12], (L, GLA_KEY_WIDTH), 0.1),
        "gla_norm_g": gain(ks[13], (L, GLA_DV)),
        "w_branch_nsa": dense(ks[14], (L, NSA_WIDTH, D_MODEL), NSA_WIDTH),
        "w_branch_gla": dense(ks[15], (L, GLA_VAL_WIDTH, D_MODEL), GLA_VAL_WIDTH),
        "w_out": dense(ks[16], (L, D_MODEL, D_MODEL), D_MODEL),
        "ln_x_g": gain(ks[17], (L, D_MODEL)),
        "ln_mem_g": gain(ks[18], (L, D_MODEL)),
        "w_xq": dense(ks[19], (L, D_MODEL, XATTN_WIDTH), D_MODEL),
        "w_xkv": dense(ks[20], (L, D_MODEL, 2 * XATTN_WIDTH), D_MODEL),
        "w_xo": dense(ks[21], (L, XATTN_WIDTH, D_MODEL), XATTN_WIDTH),
        "ln_ffn_g": gain(ks[22], (L, D_MODEL)),
        "w_up": dense(ks[23], (L, D_MODEL, 2 * FFN_DIM), D_MODEL),
        "conv_w": dense(ks[24], (L, CONV_WIDTH, FFN_DIM), CONV_WIDTH),
        "conv_b": small(ks[25], (L, FFN_DIM), 0.02),
        "w_down": dense(ks[26], (L, FFN_DIM, D_MODEL), FFN_DIM),
        "ln_final_g": gain(ks[27], (D_MODEL,)),
    }

def second_block(x, mem, ln_mix_g, w_in, nsa_gate_b, cmp_pos_k, cmp_w1_k, cmp_w2_k,
              cmp_pos_v, cmp_w1_v, cmp_w2_v, gla_w_alpha2, gla_b_alpha, gla_norm_g,
              w_branch_nsa, w_branch_gla, w_out, ln_x_g, ln_mem_g, w_xq, w_xkv, w_xo,
              ln_ffn_g, w_up, conv_w, conv_b, w_down, ln_final_g):
    split_points = np.cumsum(IN_SPLITS)[:-1].tolist()
    for l in range(DEPTH_2):
        h = rms_norm_2(x, ln_mix_g[l])
        q_a, kv_a, gate_a, q_b, k_b, v_b, r_b, alpha_b, merge = jnp.split(h @ w_in[l], split_points, axis=-1)
        kc, vc, ks_, vs_, kw, vw = jnp.split(kv_a, 6, axis=-1)
        o_nsa = nsa_attention(q_a, kc, vc, ks_, vs_, kw, vw, gate_a + nsa_gate_b[l],
                              cmp_pos_k[l], cmp_w1_k[l], cmp_w2_k[l],
                              cmp_pos_v[l], cmp_w1_v[l], cmp_w2_v[l])
        o_gla = gla(q_b, k_b, v_b, r_b, alpha_b, gla_w_alpha2[l], gla_b_alpha[l], gla_norm_g[l])
        g_nsa, g_gla = jnp.split(jax.nn.sigmoid(merge), 2, axis=-1)
        mix = g_nsa * (o_nsa @ w_branch_nsa[l]) + g_gla * (o_gla @ w_branch_gla[l])
        x = x + (mix @ w_out[l]).astype(x.dtype)
        mem_n = rms_norm_2(mem, ln_mem_g[l])
        x = x + memory_cross_attention(rms_norm_2(x, ln_x_g[l]), mem_n, w_xq[l], w_xkv[l], w_xo[l]).astype(x.dtype)
        x = x + conv_ffn(rms_norm_2(x, ln_ffn_g[l]), w_up[l], conv_w[l], conv_b[l], w_down[l]).astype(x.dtype)
    return rms_norm_2(x, ln_final_g)


def setup_inputs(seed=0):
    out = dict(first_inputs(seed))
    for name, value in second_inputs(seed + 1).items():
        if name != "x":
            out[name + "_2"] = value
    return out


def reference(
    x, c, ctx, c_ctx, w_mod, b_mod, norm1_g, norm2_g, w_in_even, w_four, q_norm_g, k_norm_g,
    rpb, w_out_even, w_pool, pool_scale, w_mlp1, w_mlp2, mem_2, ln_mix_g_2, w_in_2,
    nsa_gate_b_2, cmp_pos_k_2, cmp_w1_k_2, cmp_w2_k_2, cmp_pos_v_2, cmp_w1_v_2, cmp_w2_v_2,
    gla_w_alpha2_2, gla_b_alpha_2, gla_norm_g_2, w_branch_nsa_2, w_branch_gla_2, w_out_2,
    ln_x_g_2, ln_mem_g_2, w_xq_2, w_xkv_2, w_xo_2, ln_ffn_g_2, w_up_2, conv_w_2, conv_b_2,
    w_down_2, ln_final_g_2,
):
    x = first_block(
        x, c, ctx, c_ctx, w_mod, b_mod, norm1_g, norm2_g, w_in_even, w_four, q_norm_g, k_norm_g,
        rpb, w_out_even, w_pool, pool_scale, w_mlp1, w_mlp2,
    )
    return second_block(
        x, mem_2, ln_mix_g_2, w_in_2, nsa_gate_b_2, cmp_pos_k_2, cmp_w1_k_2, cmp_w2_k_2,
        cmp_pos_v_2, cmp_w1_v_2, cmp_w2_v_2, gla_w_alpha2_2, gla_b_alpha_2, gla_norm_g_2,
        w_branch_nsa_2, w_branch_gla_2, w_out_2, ln_x_g_2, ln_mem_g_2, w_xq_2, w_xkv_2, w_xo_2,
        ln_ffn_g_2, w_up_2, conv_w_2, conv_b_2, w_down_2, ln_final_g_2,
    )


_drawn_inputs = setup_inputs


def setup_inputs(seed=0):
    import zlib

    import numpy as np

    out = dict(_drawn_inputs(seed))
    spreads = {}
    factors = {'norm1_g': 5.687,
     'q_norm_g': 8.0,
     'k_norm_g': 8.0,
     'rpb': 8.0,
     'ln_mix_g_2': 7.952,
     'nsa_gate_b_2': 8.0,
     'cmp_pos_k_2': 8.0,
     'cmp_w1_k_2': 6.755,
     'cmp_w2_k_2': 6.883,
     'cmp_pos_v_2': 7.015,
     'gla_b_alpha_2': 4.514,
     'gla_norm_g_2': 8.0,
     'ln_x_g_2': 8.0,
     'ln_mem_g_2': 8.0,
     'ln_ffn_g_2': 20.102,
     'conv_b_2': 26.399,
     'ln_final_g_2': 7.958}
    for name, (base, spread) in spreads.items():
        noise = np.random.default_rng([zlib.crc32(name.encode()), seed]).standard_normal(out[name].shape)
        drawn = base * np.exp(spread * noise) if base else spread * noise
        out[name] = __import__('jax').numpy.asarray(drawn.astype(out[name].dtype))
    for name, factor in factors.items():
        out[name] = (out[name] * factor).astype(out[name].dtype)
    return out
```

```python
from contextlib import ExitStack

import numpy as np
import concourse.bass as bass
from concourse import mybir

ALU = mybir.AluOpType
ACT = mybir.ActivationFunctionType
F32 = mybir.dt.float32
F32R = mybir.dt.float32r
I32 = mybir.dt.int32
X = mybir.AxisListType.X

P = 128
D = 1024
S = 512
L = 256
KT = D // P
TT = S // P
LT = L // P
HID = 4 * D
HD = 64
NH = 8
GRID = 64
ROWS = S // GRID
NCMP = 31
CHUNK = 64
NCH = S // CHUNK
FFN = 2816
FT = FFN // P
WINDOW = 256
NEG = -1e30
EPS = 1e-6
PW = 2048

ROWS0 = [("c", 8), ("c_ctx", 8), ("norm1", 16), ("norm2", 16), ("ln_mix", 8), ("ln_x", 8), ("ln_mem", 8),
         ("ln_ffn", 8), ("ln_final", 8), ("pool_scale", 8), ("b_alpha", 2), ("gla_norm", 1), ("qg", 1), ("kg", 1)]
ROWS1 = [("b_mod", 96)]
ROWS2 = [("conv_w", 66), ("conv_b", 22)]


def column_places():
    at, where = 0, {}
    for rows in (ROWS0, ROWS1, ROWS2):
        for name, n in rows:
            where[name] = at
            at += n
    return where, at


COL, NCOL = column_places()


def host_constants():
    n = np.arange(S)
    angle = 2 * np.pi * ((n[:, None] * n[None, :]) % S) / S
    scale = 1.0 / np.sqrt(S * P)
    c = np.arange(P)
    angle_c = 2 * np.pi * ((c[:, None] * c[None, :]) % P) / P
    dft = np.stack([np.cos(angle) * scale, -np.sin(angle) * scale]).astype(np.float32)
    dft_c = np.stack([np.cos(angle_c), np.sin(angle_c)]).astype(np.float32)
    ident = np.eye(P, dtype=np.float32)
    halves = np.kron(np.eye(2), np.ones((HD, HD))).astype(np.float32)
    col = np.arange(GRID)
    start = np.clip(col - 8, 0, GRID - 16)
    near = (col[None, :] >= start[:, None]) & (col[None, :] < start[:, None] + 16)
    near = np.where(near, 0.0, NEG).astype(np.float32)
    near = np.concatenate([near, near], 0)[:, ::-1]
    p = np.arange(P)[:, None]
    dist = p - np.arange(S)[None, :] + (S - P)
    causal = np.where(dist >= 0, -dist, NEG).astype(np.float32)
    window = np.where((dist >= 0) & (dist < WINDOW), -dist, NEG).astype(np.float32)
    end = np.arange(NCMP) * 16 + 31
    t = np.arange(S).reshape(TT, P, 1)
    dc = t - end[None, None, :]
    cmp_bias = np.where(dc >= 0, -dc, NEG).astype(np.float32).transpose(1, 0, 2)
    j, i = np.arange(P)[:, None], np.arange(P)[None, :]
    gla_mask = ((j // CHUNK == i // CHUNK) & (j <= i)).astype(np.int32)
    cnt = []
    for w in (2, 4, 8, 16):
        lo, hi = np.clip(n - w // 2, 0, S), np.clip(n + w - w // 2, 0, S)
        cnt.append(1.0 / (hi - lo))
    cnt = np.broadcast_to(np.stack(cnt)[None], (P, 4, S)).astype(np.float32)
    valid = (np.arange(S).reshape(TT, P).T >= 31).astype(np.float32)
    tab = np.concatenate([causal, window[:, P:], cmp_bias.reshape(P, TT * NCMP)], 1)
    arrays = {"k_dft": dft.reshape(2, TT, P, S).transpose(2, 0, 1, 3), "k_dft_c": dft_c.transpose(1, 0, 2),
              "k_ident": ident, "k_halves": halves, "k_near": near, "k_tab": tab, "k_valid": valid,
              "k_gla_mask": gla_mask, "k_cnt": cnt}
    return {name: np.ascontiguousarray(x) for name, x in arrays.items()}


class Plan:

    def __init__(self):
        self.panels = []
        self.groups = {}
        self.order = []

    def panel(self, src, kc, nc):
        self.panels.append((src, kc, nc))
        return len(self.panels) - 1

    def released(self):
        last = {}
        for name in self.order:
            for i, n in enumerate(self.groups[name]["panels"]):
                last[n] = (name, i)
        out, early = {}, 0
        for n in range(len(self.panels)):
            name, i = last[n]
            g = self.groups[name]
            if i == len(g["panels"]) - 1:
                out[n] = ("tile", g["tile0"] + g["tiles"])
            else:
                early += 1
                out[n] = ("early", early)
        return out

    def group(self, name, panels, tiles, by):
        last = self.order[-1] if self.order else None
        base = {"tile0": 0, "a": 0, "d": 0}
        if last:
            g = self.groups[last]
            base = {"tile0": g["tile0"] + g["tiles"], "a": g["a"], "d": g["d"]}
        prev = self.groups[self.order[-2]] if len(self.order) > 1 else {"a": 0, "d": 0}
        g = dict(base, panels=panels, tiles=tiles, by=by, bank0=4 * (len(self.order) % 2),
                 wait_a=prev["a"], wait_d=prev["d"], before=(base["a"], base["d"]))
        g[by] += tiles
        self.groups[name] = g
        self.order.append(name)


def build(nc, a, out):
    plan = Plan()

    def kview(w):
        return w.rearrange("(k p) n -> p k n", p=P)

    def panels(w, c0, ncols=512, k=KT, k0=0):
        v = kview(w)
        return [plan.panel(v[:, x:min(x + 4, k0 + k), c0:c0 + ncols], min(4, k0 + k - x), ncols)
                for x in range(k0, k0 + k, 4)]

    w_in = a["w_in_even"][0]
    plan.group("xk", panels(a["w_xkv_2"][0], 0), 4, "a")
    plan.group("xv", panels(a["w_xkv_2"][0], 512), 2, "a")
    plan.group("f", panels(w_in, 0), 4, "a")
    plan.group("q", panels(w_in, 512), 4, "a")
    pk = panels(w_in, 1024)
    plan.group("k", pk, 4, "a")
    plan.group("kc", pk, 4, "a")
    pv = panels(w_in, 1536)
    plan.group("v", pv, 4, "a")
    plan.group("vc", pv, 2, "a")
    for j in range(2):
        plan.group(f"o{j}", panels(a["w_out_even"][0], 512 * j), 4, "d")

    def mlp_groups(l):
        plan.group(f"m{l}a0", panels(a["w_mlp1"][l], 0), 4, "a")
        for c in range(8):
            if c < 7:
                plan.group(f"m{l}a{c + 1}", panels(a["w_mlp1"][l], 512 * (c + 1)), 4, "a")
            for j in range(2):
                plan.group(f"m{l}b{c}{j}", panels(a["w_mlp2"][l], 512 * j, k=4, k0=4 * c), 4, "d")

    mlp_groups(0)
    pp = [plan.panel(a["w_pool"][0].rearrange("g (k p) n -> p (g k) n", p=P), 8, 256)]
    plan.group("p0", pp, 4, "d")
    plan.group("p1", pp, 4, "d")
    mlp_groups(1)
    w2 = a["w_in_2"][0]
    plan.group("qa", panels(w2, 0), 4, "a")
    plan.group("kv1", panels(w2, 512), 4, "a")
    plan.group("kv2", panels(w2, 1024, 280), 3, "a")
    plan.group("qkb", panels(w2, 1304), 4, "a")
    plan.group("vb", panels(w2, 1816), 4, "a")
    plan.group("rb", panels(w2, 2328), 4, "a")
    plan.group("al", panels(w2, 2840, 128), 1, "a")
    for j in range(4):
        plan.group(f"mg{j}", panels(w2, 2856 + 512 * j), 4, "a")
    for j in range(2):
        plan.group(f"bn{j}", panels(a["w_branch_nsa_2"][0], 512 * j, k=4), 4, "d")
        plan.group(f"bg{j}", panels(a["w_branch_gla_2"][0], 512 * j, k=4), 4, "d")
    for j in range(2):
        plan.group(f"ow{j}", panels(a["w_out_2"][0], 512 * j), 4, "d")
    plan.group("xq", panels(a["w_xq_2"][0], 0), 4, "a")
    for j in range(2):
        plan.group(f"xo{j}", panels(a["w_xo_2"][0], 512 * j, k=4), 4, "d")
    FC = [4, 4, 4, 4, 4, 2]
    for c, n in enumerate(FC):
        plan.group(f"fu{c}", panels(a["w_up_2"][0], 512 * c, P * n), n, "d")
        plan.group(f"fg{c}", panels(a["w_up_2"][0], FFN + 512 * c, P * n), n, "d")
        for j in range(2):
            plan.group(f"fd{c}{j}", panels(a["w_down_2"][0], 512 * j, k=n, k0=4 * c), 4, "d")
    PAN, G = plan.panels, plan.groups
    NPAN = len(PAN)

    mod_src = [kview(a["w_mod"][l])[:, 4 * i:4 * i + 4, 512 * j:512 * j + 512]
               for l in range(2) for j in range(12) for i in range(2)]
    NMOD = 24
    RELEASED = plan.released()

    with ExitStack() as ctx:
        def at(name, shape, kb, dt=F32):
            return nc.alloc_sbuf_tensor_at(name, shape, dt, offset=int(kb * 1024))

        def sem(name):
            return ctx.enter_context(nc.semaphore(name))

        B0 = 16.25
        h = at("h", [P, KT, S], B0)
        u_hi = at("u_hi", [P, KT, S], B0 + 16, F32R)
        u_lo = at("u_lo", [P, KT, S], B0 + 32, F32R)
        w_raw = [at(f"w_raw{i}", [P, PW], B0 + 48 + 8 * i) for i in range(3)]
        w_hi = [at(f"w_hi{i}", [P, PW], B0 + 72 + 8 * i, F32R) for i in range(2)]
        w_lo = [at(f"w_lo{i}", [P, PW], B0 + 88 + 8 * i, F32R) for i in range(2)]
        xk = at("xk", [P, 4, L], B0 + 104)
        xv = at("xv", [P, LT, S], B0 + 108)
        sq = at("sq", [P, 2, S], B0 + 112)
        root = at("root", [P, S], B0 + 116)
        rstd = at("rstd", [P, S], B0 + 118)
        tmp = at("tmp", [P, 2, S], B0 + 120)
        col = at("col", [P, NCOL], B0 + 124)
        ident = at("ident", [P, P], B0 + 125.25)
        ones = at("ones", [P, P], B0 + 125.75)
        halves = at("halves", [P, P], B0 + 126.25)
        modc = at("modc", [P, 2, 48, 2], B0 + 126.75)
        gcol = at("gcol", [P, 8, 8], B0 + 127.5)
        silu = at("silu", [P, KT, 2], B0 + 127.75)
        stats = at("stats", [P, 8, 32], B0 + 127.875)
        eps = at("eps", [P, 1], B0 + 128.875)
        X0 = B0 + 129
        tok_in = [at(f"tok_in{i}", [P, D], X0 + 4 * i) for i in range(4)]
        mod_raw = [at(f"mod_raw{i}", [P, PW], X0 + 16 + 8 * i) for i in range(2)]
        uc_hi = at("uc_hi", [P, KT, L], X0 + 32, F32R)
        uc_lo = at("uc_lo", [P, KT, L], X0 + 40, F32R)
        mem_t = at("mem_t", [P, KT, L], X0 + 48)
        ctx_t = at("ctx_t", [P, KT, L], X0 + 56)
        rows = at("rows", [P, 3, P], X0 + 64)
        f_t = at("f_t", [P, 4, S], X0)
        q_t = at("q_t", [P, 4, S], X0 + 8)
        k_t = at("k_t", [P, 4, S], X0 + 16)
        kc_t = at("kc_t", [P, 4, L], X0 + 24)
        vc = at("vc", [P, LT, S], X0 + 28)
        v = at("v", [P, TT, S], X0 + 48)
        dft = at("dft", [P, 2, TT, S], X0 + 32)
        w_four = at("w_four", [P, 4, P], X0 + 56)
        dft_c = at("dft_c", [P, 2, P], X0 + 58)
        cw = at("cw", [P, 4, 2 * P], X0 + 59)
        z = [at(f"z{i}", [P, TT, 2 * P], X0 + 63 + 4 * i) for i in range(2)]
        gb = [at(f"gb{i}", [P, 14, GRID], X0 + 71 + 3.5 * i) for i in range(2)]
        near = at("near", [P, GRID], X0 + 78)
        pad = at("pad", [NH * 15, 127], X0 + 74.5)
        rpb_in = at("rpb_in", [NH * 15, 31], X0 + 75)
        p_na = [at(f"p_na{i}", [P, 768], X0 + 3 * i) for i in range(2)]
        pt_na = [at(f"pt_na{i}", [P, 6, P], X0 + 56 + 3 * i) for i in range(2)]
        o_na = at("o_na", [P, TT, S], X0 + 63)
        mod_raw1 = [at(f"mod_raw1{i}", [P, PW], X0 + 32 + 8 * i) for i in range(2)]
        a_hi = [at(f"a_hi{i}", [P, 4, S], X0 + 16 * i, F32R) for i in range(2)]
        a_lo = [at(f"a_lo{i}", [P, 4, S], X0 + 16 * i + 8, F32R) for i in range(2)]
        up = at("up", [P, KT, S + 16], X0 + 32)
        win = [at(f"win{i}", [P, 2, S + 16], X0 + 49 + 4.25 * i) for i in range(2)]
        cnt = at("cnt", [P, 4, S], X0 + 58)
        qa_t = at("qa_t", [P, 4, S], X0)
        kcv_t = at("kcv_t", [P, 2, S], X0 + 8)
        ks_t = at("ks_t", [P, S], X0 + 12)
        kw_t = at("kw_t", [P, S], X0 + 14)
        vs = at("vs", [P, TT, P], X0 + 16)
        vw = at("vw", [P, TT, P], X0 + 18)
        qkb = at("qkb", [P, 4, S], X0 + 20)
        vb = at("vb", [P, TT, S], X0 + 28)
        rb = at("rb", [P, 4, S], X0 + 36)
        al = at("al", [P, S], X0 + 44)
        w1 = at("w1", [P, 2, 32, P], X0 + 46)
        kpos = [sq, tmp]
        gate = at("gate", [P, TT, 24], X0 + 78)
        pos_rows = at("pos_rows", [32, 2, P], B0 + 116)
        pos = at("pos", [P, 2, 32], B0 + 117)
        w2 = at("w2", [P, 2, HD], B0 + 117.25)
        ghid = at("ghid", [P, 4, 32], B0 + 118)
        kcm = at("kcm", [P, NCMP + 1], B0 + 118.5)
        vcm = at("vcm", [NCMP, 2, HD], B0 + 118.75)
        gate_b = at("gate_b", [1, 24], B0 + 119.25)
        w_al = at("w_al", [16, 256], X0 + 74)
        valid = at("valid", [P, TT], X0 + 78.5)
        tab = at("tab", [P, 896 + 124], X0 + 46)
        ntab = [at("ntab0", [P, 896 + 124], B0 + 112), at("ntab1", [P, 896 + 124], B0 + 120)]
        p_nsa = [at(f"p_nsa{i}", [P, 928], X0 + 50 + 3.75 * i) for i in range(2)]
        pt_nsa = [at(f"pt_nsa{i}", [P, 8, P], X0 + 57.5 + 4 * i) for i in range(2)]
        o_nsa = at("o_nsa", [P, TT, S], X0 + 66)
        on_hi = at("on_hi", [P, 4, S], X0 + 50, F32R)
        on_lo = at("on_lo", [P, 4, S], X0 + 58, F32R)
        la = [at(f"la{i}", [P, 2, S], X0 + 4 * i) for i in range(2)]
        qd = at("qd", [P, 2, S], X0 + 8)
        kd = at("kd", [P, 2, S], X0 + 12)
        ks = at("ks", [P, 2, S], X0 + 16)
        ga = at("ga", [P, 2, S], B0 + 116)
        gt = at("gt", [P, 2, S], B0 + 112)
        kst = at("kst", [P, TT, 256], X0 + 46)
        att = [at(f"att{i}", [P, TT, P], X0 + 66 + 2 * i) for i in range(2)]
        st = at("st", [P, 2, NCH, P], X0 + 70)
        dec = at("dec", [P, 2, NCH], X0 + 78.375)
        gmask = at("gmask", [P, P], X0 + 44, I32)
        og_hi = at("og_hi", [P, 4, S], X0 + 20, F32R)
        og_lo = at("og_lo", [P, 4, S], X0, F32R)
        mg = [at(f"mg{i}", [P, S], X0 + (8 + 2 * i if i < 6 else 16 + 2 * i)) for i in range(16)]
        mixn = at("mixn", [P, 4, S], X0 + 66)
        xq_t = at("xq_t", [P, 4, S], X0)
        xo_hi = at("xo_hi", [P, 4, S], X0 + 8, F32R)
        xo_lo = at("xo_lo", [P, 4, S], X0 + 16, F32R)
        p_x = [at(f"p_x{i}", [P, L], X0 + 24 + i) for i in range(2)]
        pt_x = [at(f"pt_x{i}", [P, LT, P], X0 + 26 + i) for i in range(2)]
        o_x = at("o_x", [P, TT, S], X0 + 28)
        ub = at("ub", [P, 4, S], X0 + 32)
        cv = at("cv", [P, 4, S], X0 + 41)
        y = at("y", [P, KT, S], X0)
        y_out = [at(f"y_out{i}", [P, D], X0 + 16 + 4 * i) for i in range(2)]

        ps = ctx.enter_context(nc.psum_tensor("ps", [P, 8, S], F32))
        bias_pad = nc.dram_tensor("bias_pad", (NH, 15, 127), F32, kind="Internal").ap()

        tok_loaded = [sem(f"tok_loaded{i}") for i in range(4)]
        consts_loaded = sem("consts_loaded")
        rows_loaded = sem("rows_loaded")
        ones_set = sem("ones_set")
        tok_turned = sem("tok_turned")
        tok_kept = sem("tok_kept")
        rows_turned, col_ready = sem("rows_turned"), sem("col_ready")
        silu_ready = sem("silu_ready")
        mod_loaded = [sem(f"mod_loaded{i}") for i in range(2)]
        mod_used = sem("mod_used")
        mod_ready = sem("mod_ready")
        w_loaded = [sem(f"w_loaded{i}") for i in range(3)]
        w_hi_ready, w_lo_ready = sem("w_hi_ready"), sem("w_lo_ready")
        w_early = sem("w_early")
        tile_done = sem("tile_done")
        free_a, free_d = sem("free_a"), sem("free_d")
        sq_ready, sq_used = sem("sq_ready"), sem("sq_used")
        root_ready, rstd_ready = sem("root_ready"), sem("rstd_ready")
        t_ready, n_hi_ready = sem("t_ready"), sem("n_hi_ready")
        n_ready = sem("n_ready")
        act_chain, dve_chain, pool_chain = sem("act_chain"), sem("dve_chain"), sem("pool_chain")
        hn_sum, hn_root = sem("hn_sum"), sem("hn_root")
        hn_sq, qk_ready = sem("hn_sq"), sem("qk_ready")
        four_loaded, cw_done, cw_ready = sem("four_loaded"), sem("cw_done"), sem("cw_ready")
        z_done, z_ready = sem("z_done"), sem("z_ready")
        four_done, four_hi, four_kept = sem("four_done"), sem("four_hi"), sem("four_kept")
        pad_set, pad_loaded, pad_stored = sem("pad_set"), sem("pad_loaded"), sem("pad_stored")
        gb_loaded = [sem(f"gb_loaded{i}") for i in range(2)]
        gb_ready = sem("gb_ready")
        na_s, na_max, na_exp, na_t, na_pt, na_pv, na_o = [sem(f"na_{x}") for x in
                                                         ("s", "max", "exp", "t", "pt", "pv", "o")]
        ot_turned, ot_hi, ot_kept = sem("ot_turned"), sem("ot_hi"), sem("ot_kept")
        a_hi_ready, a_ready = sem("a_hi_ready"), sem("a_ready")
        cnt_loaded, pooled, pooled_hi, pooled_ready = [sem(f"pool_{x}") for x in ("cnt", "t", "hi", "ready")]
        cmp_loaded, pos_turned, pos_ready, kpos_ready = [sem(f"cmp_{x}") for x in
                                                        ("loaded", "turned", "pos", "kpos")]
        hid_done, hid_ready, cmp_done, cmp_ready = [sem(f"cmp_{x}") for x in
                                                   ("hid", "gelu", "done", "ready")]
        tab_loaded, tab_ready = sem("tab_loaded"), sem("tab_ready")
        ns_s, ns_max, ns_exp, ns_t, ns_pt, ns_pv, ns_o = [sem(f"ns_{x}") for x in
                                                         ("s", "max", "exp", "t", "pt", "pv", "o")]
        gla_loaded, gmask_loaded = sem("gla_loaded"), sem("gmask_loaded")
        gz_done, gz_log, gla_b, gla_e, gla_qk = [sem(f"gla_{x}") for x in ("z", "log", "b", "e", "qk")]
        kst_done, kst_ready, inc_done, st_ready = [sem(f"gla_{x}") for x in
                                                  ("kst_done", "kst", "inc", "st")]
        att_zero, att_done, att_ready, go_done, go_sq, go_root, go_t, go_hi, go_ready, go_sum = [
            sem(f"gla_{x}") for x in ("zero", "att_done", "att", "o", "sq", "root", "t", "hi", "ready", "sum")]
        mix_t, mix_hi, mix_ready = [sem(f"mix_{x}") for x in ("t", "hi", "ready")]
        xa_s, xa_max, xa_exp, xa_t, xa_pt, xa_pv, xa_o = [sem(f"xa_{x}") for x in
                                                         ("s", "max", "exp", "t", "pt", "pv", "o")]
        c_ready, c_gelu, f_hi, f_pair = [sem(f"ffn_{x}") for x in ("c", "gelu", "hi", "ready")]
        out_turned, out_kept = sem("out_turned"), sem("out_kept")
        out_stored = [sem(f"out_stored{i}") for i in range(2)]

        block = ctx.enter_context(nc.Block())

        MEM, CTX, X1, X2, Y1, Y2, MIX, XAT, FF, FIN = range(10)
        ncols = {MEM: L, CTX: L}

        def gain(n, k):
            if n in (MEM, MIX, XAT, FF, FIN):
                c0 = COL[{MEM: "ln_mem", MIX: "ln_mix", XAT: "ln_x", FF: "ln_ffn", FIN: "ln_final"}[n]]
                return col[:, c0 + k:c0 + k + 1]
            return gcol[:, n, k:k + 1]

        def shift(n, k):
            l, t0, src = {CTX: (0, 0, 1), X1: (0, 0, 0), X2: (0, 24, 0), Y1: (1, 0, 0), Y2: (1, 24, 0)}[n]
            return modc[:, l, t0 + k, src:src + 1]

        def g_mod(l, second, k):
            return modc[:, l, (40 if second else 16) + k, 0:1]

        def source(n, k):
            return {MEM: mem_t, CTX: ctx_t}.get(n, h)[:, k, :]

        def pair(n, k):
            return (uc_hi[:, k, :], uc_lo[:, k, :]) if n in (MEM, CTX) else (u_hi[:, k, :], u_lo[:, k, :])

        def group_end(name):
            return G[name]["a"], G[name]["d"]

        def raw_panel(n):
            _, kc, w = PAN[n]
            return w_raw[n % 3][:, 0:kc * w]

        def part_panel(part, n):
            _, kc, w = PAN[n]
            return part[n % 2][:, 0:kc * w]

        def after_panel(eng, n):
            kind, value = RELEASED[n]
            eng.wait_ge(tile_done if kind == "tile" else w_early, value)

        def after_groups(eng, name):
            fa, fd = group_end(name)
            if fa:
                eng.wait_ge(free_a, fa)
            if fd:
                eng.wait_ge(free_d, fd)

        NUNIT = NH * TT
        NROWDMA = 19
        LOADS = {}
        for n in range(NPAN):
            LOADS[n] = LOADS.get(n - 3, 0) + (8 if n in G["qa"]["panels"] else 1)
        SLOPES = [2.0 ** (-(i + 1)) for i in range(NH)]
        N_READY = {n: 8 * n for n in range(10)}
        PAIRED = {n: 8 * i for i, n in enumerate((MEM, CTX, X1, X2, Y2, MIX, XAT, FF))}
        RELEASER = {n: [name for name in plan.order if n in G[name]["panels"]][-1] for n in range(NPAN)}

        def computed(eng, name):
            eng.wait_ge(tile_done, G[name]["tile0"] + G[name]["tiles"])

        @block.sync
        def _(sp):
            for dst, src in ((ident, "k_ident"), (halves, "k_halves")):
                sp.dma_start(dst[:, :], a[src]).then_inc(consts_loaded, 16)
            for t, (names, tensor) in enumerate(((ROWS0, 0), (ROWS1, 1), (ROWS2, 2))):
                r = 0
                for name, n in names:
                    if name in ("qg", "kg"):
                        src = a["q_norm_g" if name == "qg" else "k_norm_g"]
                        sp.dma_start(rows[r:r + 1, t, 0:HD], src).then_inc(rows_loaded, 16)
                        sp.dma_start(rows[r:r + 1, t, HD:P], src).then_inc(rows_loaded, 16)
                    else:
                        src = {"c": a["c"], "c_ctx": a["c_ctx"].unsqueeze(0), "norm1": a["norm1_g"],
                               "norm2": a["norm2_g"], "ln_mix": a["ln_mix_g_2"], "ln_x": a["ln_x_g_2"],
                               "ln_mem": a["ln_mem_g_2"], "ln_ffn": a["ln_ffn_g_2"],
                               "ln_final": a["ln_final_g_2"].unsqueeze(0), "pool_scale": a["pool_scale"],
                               "b_alpha": a["gla_b_alpha_2"], "gla_norm": a["gla_norm_g_2"],
                               "b_mod": a["b_mod"], "conv_w": a["conv_w_2"][0], "conv_b": a["conv_b_2"]}[name]
                        src = src.rearrange("a (b p) -> (a b) p", p=P)
                        sp.dma_start(rows[r:r + n, t, :], src).then_inc(rows_loaded, 16)
                    r += n

            def load_panel(n):
                src, kc, w = PAN[n]
                if n >= 3:
                    sp.wait_ge(w_lo_ready, n - 2)
                if n in G["qa"]["panels"]:
                    dst = raw_panel(n).rearrange("p (k m a b) -> p k m a b", k=kc, m=4, a=2)
                    for x in range(2):
                        for k in range(kc):
                            sp.dma_start(dst[:, k, :, x, :],
                                         src[:, k, 256 * x:256 * x + 256].rearrange("p (m b) -> p m b", m=4))\
                              .then_inc(w_loaded[n % 3], 16)
                    return
                sp.dma_start(raw_panel(n).rearrange("p (k n) -> p k n", k=kc), src).then_inc(w_loaded[n % 3], 16)

            for i in range(8):
                if i >= 4:
                    sp.wait_ge(tok_kept, 2 * (i - 4) + 2)
                src = (a["mem_2"][0][P * i:P * i + P, :] if i < 2 else
                       a["ctx"][0][P * (i - 2):P * (i - 1), :] if i < 4 else a["x"][0][P * (i - 4):P * (i - 3), :])
                sp.dma_start(tok_in[i % 4][:, :], src).then_inc(tok_loaded[i % 4], 16)
                if i == 1:
                    for n in range(3):
                        load_panel(n)
            load_panel(3)
            load_panel(4)
            load_panel(5)
            for i in range(NMOD):
                if i >= 2:
                    sp.wait_ge(mod_used, i - 1)
                sp.dma_start(mod_raw[i % 2][:, :].rearrange("p (k n) -> p k n", k=4), mod_src[i])\
                  .then_inc(mod_loaded[i % 2], 16)
            last = G["vc"]["panels"][-1]
            for n in range(6, last + 1):
                load_panel(n)
            after_panel(sp, last)
            sp.dma_start(dft[:, :, :, :], a["k_dft"]).then_inc(four_loaded, 16)
            sp.dma_start(dft_c[:, :, :], a["k_dft_c"]).then_inc(four_loaded, 16)
            sp.dma_start(w_four[:, :, :], a["w_four"][0].rearrange("g c d -> c g d")).then_inc(four_loaded, 16)
            for n in range(last + 1, last + 4):
                load_panel(n)
            sp.dma_start(near[:, :], a["k_near"]).then_inc(pad_loaded, 16)
            sp.dma_start(rpb_in[:, :], a["rpb"][0].rearrange("h r c -> (h r) c")).then_inc(pad_loaded, 16)
            sp.wait_ge(pad_set, 2)
            sp.dma_start(bias_pad.rearrange("h r c -> (h r) c"), pad[:, :]).then_inc(pad_stored, 16)
            sp.wait_ge(pad_stored, 16)
            sp.wait_ge(four_kept, 4)
            mods = list(range(NMOD))

            def load_mod():
                i = mods.pop(0)
                if i >= 2:
                    sp.wait_ge(mod_used, NMOD + i - 1)
                sp.dma_start(mod_raw1[i % 2][:, :].rearrange("p (k n) -> p k n", k=4), mod_src[NMOD + i])\
                  .then_inc(mod_loaded[i % 2], 16)

            for hh in range(NH):
                if hh >= 2:
                    sp.wait_ge(na_max, 4 * (hh - 1))
                for ro in range(2):
                    src = bass.AP(tensor=bias_pad.tensor, offset=hh * 15 * 127 + (1 - ro) * 127,
                                  ap=[[1, GRID], [127, 14], [1, GRID]])
                    sp.dma_start(gb[hh % 2][GRID * ro:GRID * ro + GRID, :, :], src).then_inc(gb_loaded[hh % 2], 16)
                for _ in range(3):
                    load_mod()
            n0 = last + 4
            end = G["m0b71"]["panels"][-1]
            for n in range(n0, end + 2):
                load_panel(n)
            sp.dma_start(cnt[:, :, :], a["k_cnt"]).then_inc(cnt_loaded, 16)
            n1 = G["al"]["panels"][-1]
            second = G["qa"]["panels"][0]
            for n in range(end + 2, second):
                load_panel(n)
            for n in range(second, n1 + 1):
                load_panel(n)
                if n == G["kv1"]["panels"][0]:
                    sp.wait_ge(n_ready, 8 * (MIX + 1))
                    sp.dma_start(gate_b[:, :], a["nsa_gate_b_2"]).then_inc(cmp_loaded, 16)
                    for x, c in enumerate("kv"):
                        for half in range(2):
                            r = slice(HD * half, HD * half + HD)
                            sp.dma_start(w1[r, x, :, :], a[f"cmp_w1_{c}_2"][0].rearrange("(l d) n -> d l n", d=HD))\
                              .then_inc(cmp_loaded, 16)
                            sp.dma_start(pos_rows[:, x, r], a[f"cmp_pos_{c}_2"][0]).then_inc(cmp_loaded, 16)
                        sp.dma_start(w2[:, x, :], a[f"cmp_w2_{c}_2"][0]).then_inc(cmp_loaded, 16)
            for n in range(n1 + 1, n1 + 4):
                load_panel(n)
            sp.wait_ge(hid_done, 4)
            sp.dma_start(tab[:, :], a["k_tab"]).then_inc(tab_loaded, 16)
            sp.dma_start(valid[:, :], a["k_valid"]).then_inc(tab_loaded, 16)
            sp.dma_start(w_al[:, :], a["gla_w_alpha2_2"][0]).then_inc(gla_loaded, 16)
            sp.wait_ge(gz_done, 1)
            sp.dma_start(gmask[:, :], a["k_gla_mask"]).then_inc(gmask_loaded, 16)
            for n in range(n1 + 4, NPAN):
                load_panel(n)
            for i in range(TT):
                sp.wait_ge(out_kept, 2 * i + 2)
                sp.dma_start(out[0][P * i:P * i + P, :], y_out[i % 2][:, :]).then_inc(out_stored[i % 2], 16)
            for stored in out_stored:
                sp.wait_ge(stored, 16 * TT // 2)

        @block.tensor
        def _(pe):
            def norm_sum(n):
                t = ncols.get(n, S)
                for k in range(KT):
                    pe.wait_ge(sq_ready, 8 * n + k + 1)
                    nc.tensor.matmul(ps[:, 7, 0:t], ones[:, :], sq[:, k % 2, 0:t], start=(k == 0),
                                     stop=(k == KT - 1)).then_inc(sq_used, 1)

            def gemm(name, products, ready=None):
                g = G[name]
                if g["wait_a"]:
                    pe.wait_ge(free_a, g["wait_a"])
                if g["wait_d"]:
                    pe.wait_ge(free_d, g["wait_d"])
                for i, n in enumerate(g["panels"]):
                    _, kc, w = PAN[n]
                    pe.wait_ge(w_lo_ready, n + 1)
                    hi = part_panel(w_hi, n).rearrange("p (k n) -> p k n", k=kc)
                    lo = part_panel(w_lo, n).rearrange("p (k n) -> p k n", k=kc)
                    kl = 4 * (len(g["panels"]) - 1) + PAN[g["panels"][-1]][1]
                    for m in range(g["tiles"]):
                        for kk in range(kc):
                            k = 4 * i + kk
                            if ready and m == 0:
                                ready(k)
                            todo = products(m, k, hi[:, kk, :], lo[:, kk, :], g["bank0"])
                            for j, (dst, l, r) in enumerate(todo):
                                ins = nc.tensor.matmul(dst, l, r, start=(k == 0 and j == 0),
                                                       stop=(k == kl - 1 and j >= len(todo) - 3),
                                                       skip_group_check=True)
                        if i == len(g["panels"]) - 1:
                            ins.then_inc(tile_done, 1)
                    if RELEASED[n][0] == "early" and name == RELEASER[n]:
                        ins.then_inc(w_early, 1)

            def three_w(dst, whi, wlo, xhi, xlo):
                return [(dst, whi, xhi), (dst, whi, xlo), (dst, wlo, xhi)]

            def three_x(dst, whi, wlo, xhi, xlo):
                return [(dst, xhi, whi), (dst, xhi, wlo), (dst, xlo, whi)]

            def by_feature(x, t=S):
                def products(m, k, hi, lo, b):
                    c = slice(P * m, P * m + P)
                    return three_w(ps[:, b + m, 0:t], hi[:, c], lo[:, c], *x(k))
                return products

            def by_token(x):
                def products(m, k, hi, lo, b):
                    xh, xl = x(k)
                    c = slice(P * m, P * m + P)
                    return three_x(ps[:, b + m, :], hi, lo, xh[:, c], xl[:, c])
                return products

            def u(k):
                return u_hi[:, k, :], u_lo[:, k, :]

            def uc(k):
                return uc_hi[:, k, :], uc_lo[:, k, :]

            def when_normed(n):
                return lambda k: pe.wait_ge(n_ready, N_READY[n] + k + 1)

            def mod_panel(i, l):
                raw = (mod_raw, mod_raw1)[l][i % 2]
                bank = (6, 7)[l]
                j, half = i // 2, i % 2
                n = NMOD * l + i
                pe.wait_ge(mod_loaded[i % 2], 16 * (n // 2 + 1))
                wv = raw[:, :].rearrange("p (k n) -> p k n", k=4)
                for m in range(4):
                    t = 4 * j + m
                    for kk in range(4):
                        k = 4 * half + kk
                        ins = nc.tensor.matmul(ps[:, bank, 2 * t:2 * t + 2], wv[:, kk, P * m:P * m + P],
                                               silu[:, k, :], start=(i == 0 and m == 0 and kk == 0),
                                               stop=(k == KT - 1), skip_group_check=True)
                ins.then_inc(mod_used, 1)

            pe.wait_ge(consts_loaded, 32)
            for i in range(8):
                pe.wait_ge(tok_loaded[i % 4], 16 * (i // 4 + 1))
                for half in range(2):
                    n = 2 * i + half
                    if n >= 4:
                        pe.wait_ge(tok_kept, n - 3)
                    for j in range(4):
                        k = 4 * half + j
                        ins = nc.tensor.transpose(ps[:, n % 4, P * j:P * j + P], tok_in[i % 4][:, P * k:P * k + P],
                                                  ident[:, :])
                    ins.then_inc(tok_turned, 1)
                if i == 1:
                    pe.wait_ge(rows_loaded, 16 * NROWDMA)
                    at_ = 0
                    for t, rr in enumerate((ROWS0, ROWS1, ROWS2)):
                        r = sum(n for _, n in rr)
                        ins = nc.tensor.transpose(ps[:, 4, at_:at_ + r], rows[0:r, t, :], ident[0:r, 0:r])
                        at_ += r
                    ins.then_inc(rows_turned, 1)
                    pe.wait_ge(ones_set, 1)
            norm_sum(MEM)
            pe.wait_ge(tok_kept, 16)
            pe.wait_ge(col_ready, 1)
            gemm("xk", by_feature(uc, L), when_normed(MEM))
            gemm("xv", by_token(uc))
            pe.wait_ge(silu_ready, 2)
            for i in range(NMOD):
                mod_panel(i, 0)
            norm_sum(CTX)
            pe.wait_ge(root_ready, CTX + 1)
            norm_sum(X1)
            pe.wait_ge(root_ready, X1 + 1)
            gemm("f", by_feature(u), when_normed(X1))
            gemm("q", by_feature(u))
            gemm("k", by_feature(u))
            gemm("kc", by_feature(uc, L))
            gemm("v", by_token(u))
            gemm("vc", by_token(uc))

            after_groups(pe, "vc")
            for n in range(10):
                pe.wait_ge(hn_sq, n + 1)
                if n >= 2:
                    pe.wait_ge(hn_root, n - 1)
                nc.tensor.matmul(ps[:, 6 + n % 2, :], halves[:, :], sq[:, n % 2, :], start=True, stop=True)\
                  .then_inc(hn_sum, 1)

            pe.wait_ge(four_loaded, 48)
            for g in range(4):
                for x in range(2):
                    ins = nc.tensor.matmul(ps[:, g // 2, 256 * (g % 2) + P * x:256 * (g % 2) + P * x + P],
                                           dft_c[:, x, :], w_four[:, g, :], start=True, stop=True)
            ins.then_inc(cw_done, 1)
            pe.wait_ge(cw_ready, 1)
            for g in range(4):
                if g >= 1:
                    pe.wait_ge(z_ready, 2 * g)
                for m in range(TT):
                    ins = nc.tensor.matmul(ps[:, 2 + m // 2, 256 * (m % 2):256 * (m % 2) + 256],
                                           f_t[:, g, P * m:P * m + P], cw[:, g, :], start=True, stop=True)
                    if m % 2:
                        ins.then_inc(z_done, 1)
                pe.wait_ge(z_ready, 2 * g + 2)
                if g >= 2:
                    pe.wait_ge(four_kept, g - 1)
                for x in range(2):
                    for m in range(TT):
                        ins = nc.tensor.matmul(ps[:, 4 + g % 2, :], z[g % 2][:, m, P * x:P * x + P],
                                               dft[:, x, m, :], start=(x == 0 and m == 0), stop=(x == 1 and m == 3))
                ins.then_inc(four_done, 1)

            pe.wait_ge(qk_ready, 10)
            pe.wait_ge(four_kept, 4)

            def na_scores(n):
                hh, i = n // TT, n % TT
                r = slice(HD * (hh % 2), HD * (hh % 2) + HD)
                b = 2 * (n % 2)
                if n >= 2:
                    pe.wait_ge(na_exp, n - 1)
                q = q_t[r, hh // 2, P * i:P * i + P]
                nc.tensor.matmul(ps[:, b, :], q, k_t[r, hh // 2, :], start=True, stop=True)
                nc.tensor.matmul(ps[:, b + 1, 0:L], q, kc_t[r, hh // 2, :], start=True, stop=True).then_inc(na_s, 1)

            def na_turn(n):
                pe.wait_ge(na_exp, n + 1)
                if n >= 1:
                    pe.wait_ge(na_pt, n)
                for j in range(6):
                    ins = nc.tensor.transpose(ps[:, 4 + j // 4, P * (j % 4):P * (j % 4) + P],
                                              p_na[n % 2][:, P * j:P * j + P], ident[:, :])
                ins.then_inc(na_t, 1)

            def na_values(n):
                hh = n // TT
                pe.wait_ge(na_pt, n + 1)
                if n >= 1:
                    pe.wait_ge(na_o, n)
                for j in range(6):
                    val = v[:, j, HD * hh:HD * hh + HD] if j < TT else vc[:, j - TT, HD * hh:HD * hh + HD]
                    ins = nc.tensor.matmul(ps[:, 6, HD * (n % 8):HD * (n % 8) + HD], pt_na[n % 2][:, j, :], val,
                                           start=(j == 0), stop=(j == 5))
                ins.then_inc(na_pv, 1)

            na_scores(0)
            for n in range(NUNIT):
                if n + 1 < NUNIT:
                    na_scores(n + 1)
                na_turn(n)
                if n % TT < 3:
                    mod_panel(3 * (n // TT) + n % TT, 1)
                na_values(n)

            def turn_out(o, n0):
                for j in range(4):
                    for i in range(TT):
                        ins = nc.tensor.transpose(ps[:, j, P * i:P * i + P], o[:, i, P * j:P * j + P], ident[:, :])
                    ins.then_inc(ot_turned, 1)

            pe.wait_ge(na_o, NUNIT)
            turn_out(o_na, 0)
            pe.wait_ge(mod_ready, 2)
            pe.wait_ge(ot_kept, 4)
            for j in range(2):
                gemm(f"o{j}", by_feature(u))

            def mlp(l, n):
                after_groups(pe, "o1" if l == 0 else "p1")
                norm_sum(n)
                pe.wait_ge(root_ready, n + 1)

                def when_hidden(c):
                    return lambda k: pe.wait_ge(a_ready, 32 * l + 4 * c + k + 1)

                gemm(f"m{l}a0", by_feature(u), when_normed(n))
                for c in range(8):
                    if c < 7:
                        gemm(f"m{l}a{c + 1}", by_feature(u))
                    x = lambda k, c=c: (a_hi[c % 2][:, k, :], a_lo[c % 2][:, k, :])
                    gemm(f"m{l}b{c}0", by_feature(x), when_hidden(c))
                    gemm(f"m{l}b{c}1", by_feature(x))
            mlp(0, X2)
            after_groups(pe, "m0b71")
            norm_sum(Y1)
            pe.wait_ge(root_ready, Y1 + 1)
            n = G["p0"]["panels"][0]
            hi = part_panel(w_hi, n).rearrange("p (k n) -> p k n", k=8)
            lo = part_panel(w_lo, n).rearrange("p (k n) -> p k n", k=8)
            pe.wait_ge(w_lo_ready, n + 1)
            for j in range(2):
                for m in range(4):
                    g = 2 * j + m // 2
                    c = slice(P * (m % 2), P * (m % 2) + P)
                    pe.wait_ge(pooled_ready, g + 1)
                    for kk in range(2):
                        todo = three_w(ps[:, G[f"p{j}"]["bank0"] + m, :], hi[:, 2 * g + kk, c], lo[:, 2 * g + kk, c],
                                       *u(2 * g + kk))
                        for x, (dst, l_, r_) in enumerate(todo):
                            ins = nc.tensor.matmul(dst, l_, r_, start=(kk == 0 and x == 0), stop=(kk == 1 and x == 2))
                    ins.then_inc(tile_done, 1)
            mlp(1, Y2)

            after_groups(pe, "m1b71")
            norm_sum(MIX)
            pe.wait_ge(root_ready, MIX + 1)

            def keys_and_values(m, k, hi, lo, b):
                if m < 3:
                    c = slice(P * m, P * m + P)
                    return three_w(ps[:, b + m, :], hi[:, c], lo[:, c], *u(k))
                xh, xl = u(k)
                return [p for t in range(TT) for p in
                        three_x(ps[:, b + 3, P * t:P * t + P], hi[:, 384:512], lo[:, 384:512],
                                xh[:, P * t:P * t + P], xl[:, P * t:P * t + P])]

            def window_and_gates(m, k, hi, lo, b):
                xh, xl = u(k)
                if m == 0:
                    return three_w(ps[:, b, :], hi[:, 0:P], lo[:, 0:P], xh, xl)
                w, c = ((P, slice(P, 2 * P)), (24, slice(2 * P, 2 * P + 24)))[m - 1]
                todo = [p for t in range(TT) for p in
                        three_x(ps[:, b + m, w * t:w * t + w], hi[:, c], lo[:, c],
                                xh[:, P * t:P * t + P], xl[:, P * t:P * t + P])]
                if m == 2 and k == KT - 1:
                    todo += [(ps[:, b + m, w * t:w * t + w], ones[0:1, :], gate_b[0:1, :]) for t in range(TT)]
                return todo

            gemm("qa", by_feature(u), when_normed(MIX))
            gemm("kv1", keys_and_values)
            pe.wait_ge(cmp_loaded, 16 * 11)
            gemm("kv2", window_and_gates)
            gemm("qkb", by_feature(u))
            gemm("vb", by_token(u))
            gemm("rb", by_feature(u))
            gemm("al", by_feature(u))

            after_groups(pe, "al")
            for x in range(2):
                ins = nc.tensor.transpose(ps[:, 6, 32 * x:32 * x + 32], pos_rows[:, x, :], ident[0:32, 0:32])
            ins.then_inc(pos_turned, 1)
            for x in range(2):
                for half in range(2):
                    if half == 0:
                        pe.wait_ge(kpos_ready, x + 1)
                    r = slice(HD * half, HD * half + HD)
                    for l in range(32):
                        ins = nc.tensor.matmul(ps[:, 2 * x + half, 0:NCMP], w1[r, x, l, :],
                                               kpos[x][r, l // 16, l:l + 16 * (NCMP - 1) + 1:16] if l < 16 else
                                               kpos[x][r, 1, l:l + 16 * (NCMP - 1) + 1:16],
                                               start=(l == 0), stop=(l == 31))
                    ins.then_inc(hid_done, 1)
            pe.wait_ge(hid_ready, 4)
            for half in range(2):
                r = slice(HD * half, HD * half + HD)
                nc.tensor.matmul(ps[r, 4, 0:NCMP], w2[:, 0, :], ghid[:, half, 0:NCMP], start=True, stop=True)
                ins = nc.tensor.matmul(ps[0:NCMP, 5, r], ghid[:, 2 + half, 0:NCMP], w2[:, 1, :],
                                       start=True, stop=True)
            ins.then_inc(cmp_done, 1)

            pe.wait_ge(cmp_ready, 1)

            def ns_scores(n):
                hh, i = n // TT, n % TT
                kv = hh // 4
                r = slice(HD * kv, HD * kv + HD)
                b = 2 * (n % 2)
                if n >= 2:
                    pe.wait_ge(ns_max, n - 1)
                q = qa_t[r, hh % 4, P * i:P * i + P]
                ws, ww = P * (i + 1), P * min(i + 1, 3)
                nc.tensor.matmul(ps[:, b, 0:ws], q, ks_t[r, 0:ws], start=True, stop=True)
                nc.tensor.matmul(ps[:, b + 1, 0:ww], q, kw_t[r, ws - ww:ws], start=True, stop=True)
                nc.tensor.matmul(ps[:, b + 1, 384:384 + NCMP], q, kcm[r, 0:NCMP], start=True, stop=True)\
                  .then_inc(ns_s, 1)

            def ns_turn(n):
                i = n % TT
                pe.wait_ge(ns_exp, n + 1)
                if n >= 1:
                    pe.wait_ge(ns_pt, n)
                pr = p_nsa[n % 2]
                for j in range(i + 1):
                    nc.tensor.transpose(ps[:, 4, P * j:P * j + P], pr[:, P * j:P * j + P], ident[:, :])
                for j in range(min(i + 1, 3)):
                    nc.tensor.transpose(ps[:, 5, P * j:P * j + P], pr[:, S + P * j:S + P * j + P], ident[:, :])
                nc.tensor.transpose(ps[0:NCMP, 5, 384:512], pr[:, 896:896 + NCMP], ident[:, :]).then_inc(ns_t, 1)

            def ns_values(n):
                hh, i = n // TT, n % TT
                c = slice(HD * (hh // 4), HD * (hh // 4) + HD)
                b = 6 + n % 2
                pt = pt_nsa[n % 2]
                pe.wait_ge(ns_pt, n + 1)
                if n >= 2:
                    pe.wait_ge(ns_o, n - 1)
                for j in range(i + 1):
                    nc.tensor.matmul(ps[:, b, 0:HD], pt[:, j, :], vs[:, j, c], start=(j == 0), stop=(j == i))
                nw = min(i + 1, 3)
                for j in range(nw):
                    nc.tensor.matmul(ps[:, b, HD:2 * HD], pt[:, 4 + j, :], vw[:, i + 1 - nw + j, c],
                                     start=(j == 0), stop=(j == nw - 1))
                nc.tensor.matmul(ps[:, b, 2 * HD:3 * HD], pt[0:NCMP, 7, :], vcm[:, hh // 4, :],
                                 start=True, stop=True).then_inc(ns_pv, 1)

            ns_scores(0)
            for n in range(NUNIT):
                if n + 1 < NUNIT:
                    ns_scores(n + 1)
                ns_turn(n)
                ns_values(n)
            pe.wait_ge(ns_o, NUNIT)
            turn_out(o_nsa, 1)

            pe.wait_ge(gla_loaded, 16)
            pe.wait_ge(ot_kept, 8)
            for p in range(2):
                ins = nc.tensor.matmul(ps[:, p, :], w_al[:, P * p:P * p + P], al[0:16, :], start=True, stop=True)
            ins.then_inc(gz_done, 1)
            pe.wait_ge(gla_qk, 3)
            for i in range(TT):
                for p in range(2):
                    ins = nc.tensor.transpose(ps[:, 2 + i // 2, 256 * (i % 2) + P * p:256 * (i % 2) + P * p + P],
                                              ks[:, p, P * i:P * i + P], ident[:, :])
            ins.then_inc(kst_done, 1)
            pe.wait_ge(kst_ready, 1)

            def gla_head(hh):
                p, r = hh // 2, slice(HD * (hh % 2), HD * (hh % 2) + HD)
                e = slice(P * hh, P * hh + P)
                if hh == 0:
                    pe.wait_ge(st_ready, 1)
                pe.wait_ge(att_ready, hh + 1)
                if hh >= 2:
                    pe.wait_ge(go_t, hh - 1)
                o = ps[:, 6 + hh % 2, :]
                for i in range(TT):
                    nc.tensor.matmul(o[:, P * i:P * i + P], vb[:, i, e], att[hh % 2][:, i, :], start=(i == 0),
                                     stop=False, skip_group_check=True)
                for c in range(1, NCH):
                    t = slice(CHUNK * c, CHUNK * c + CHUNK)
                    ins = nc.tensor.matmul(o[:, t], st[r, p, c, :], qd[r, p, t], start=False, stop=True,
                                           skip_group_check=True)
                ins.then_inc(go_done, 1)
                pe.wait_ge(go_sq, hh + 1)
                if hh >= 2:
                    pe.wait_ge(go_root, hh - 1)
                nc.tensor.matmul(ps[:, hh % 2, :], ones[:, :], gt[:, hh % 2, :], start=True, stop=True)\
                  .then_inc(go_sum, 1)

            for c in range(NCH - 1):
                for hh in range(4):
                    p, half = hh // 2, hh % 2
                    r = slice(CHUNK * (c % 2), CHUNK * (c % 2) + CHUNK)
                    ins = nc.tensor.matmul(ps[HD * half:HD * half + HD, 2 * p + c % 2, P * (c // 2):P * (c // 2) + P],
                                           kst[r, c // 2, HD * hh:HD * hh + HD], vb[r, c // 2, P * hh:P * hh + P],
                                           start=True, stop=True)
            ins.then_inc(inc_done, 1)
            for hh in range(4):
                p, r = hh // 2, slice(HD * (hh % 2), HD * (hh % 2) + HD)
                if hh == 0:
                    pe.wait_ge(gla_qk, 3)
                if hh >= 2:
                    pe.wait_ge(att_ready, hh - 1)
                for i in range(TT):
                    ins = nc.tensor.matmul(ps[:, 4 + hh % 2, P * i:P * i + P], kd[r, p, P * i:P * i + P],
                                           qd[r, p, P * i:P * i + P], start=True, stop=True)
                ins.then_inc(att_done, 1)
                if hh >= 1:
                    gla_head(hh - 1)
            gla_head(3)
            pe.wait_ge(go_ready, 4)

            for j in range(4):
                gemm(f"mg{j}", by_feature(u))
            for j in range(2):
                gemm(f"bn{j}", by_feature(lambda k: (on_hi[:, k, :], on_lo[:, k, :])))
                gemm(f"bg{j}", by_feature(lambda k: (og_hi[:, k, :], og_lo[:, k, :])))
            for j in range(2):
                gemm(f"ow{j}", by_feature(u), (lambda k: pe.wait_ge(mix_ready, k + 1)) if j == 0 else None)

            after_groups(pe, "ow1")
            norm_sum(XAT)
            pe.wait_ge(root_ready, XAT + 1)
            gemm("xq", by_feature(u), when_normed(XAT))
            after_groups(pe, "xq")

            def xa_scores(n):
                hh, i = n // TT, n % TT
                if n >= 2:
                    pe.wait_ge(xa_exp, n - 1)
                nc.tensor.matmul(ps[:, n % 2, 0:L], xq_t[:, hh, P * i:P * i + P], xk[:, hh, :],
                                 start=True, stop=True).then_inc(xa_s, 1)

            def xa_turn(n):
                pe.wait_ge(xa_exp, n + 1)
                if n >= 2:
                    pe.wait_ge(xa_pt, n - 1)
                for j in range(LT):
                    ins = nc.tensor.transpose(ps[:, 2 + n % 2, P * j:P * j + P], p_x[n % 2][:, P * j:P * j + P],
                                              ident[:, :])
                ins.then_inc(xa_t, 1)

            def xa_values(n):
                hh = n // TT
                pe.wait_ge(xa_pt, n + 1)
                if n >= 2:
                    pe.wait_ge(xa_o, n - 1)
                for j in range(LT):
                    ins = nc.tensor.matmul(ps[:, 4 + n % 2, 0:P], pt_x[n % 2][:, j, :], xv[:, j, P * hh:P * hh + P],
                                           start=(j == 0), stop=(j == LT - 1))
                ins.then_inc(xa_pv, 1)

            xa_scores(0)
            for n in range(4 * TT):
                if n + 1 < 4 * TT:
                    xa_scores(n + 1)
                xa_turn(n)
                xa_values(n)
            pe.wait_ge(xa_o, 4 * TT)
            turn_out(o_x, 2)
            pe.wait_ge(ot_kept, 12)
            for j in range(2):
                gemm(f"xo{j}", by_feature(lambda k: (xo_hi[:, k, :], xo_lo[:, k, :])))

            after_groups(pe, "xo1")
            norm_sum(FF)
            pe.wait_ge(root_ready, FF + 1)
            for c, nt in enumerate(FC):
                gemm(f"fu{c}", by_feature(u), when_normed(FF) if c == 0 else None)
                gemm(f"fg{c}", by_feature(u))
                for j in range(2):
                    gemm(f"fd{c}{j}", by_feature(lambda k, c=c: (a_hi[c % 2][:, k, :], a_lo[c % 2][:, k, :])),
                         (lambda k, c=c: pe.wait_ge(f_pair, 4 * c + k + 1)) if j == 0 else None)
            after_groups(pe, "fd51")
            norm_sum(FIN)
            pe.wait_ge(n_ready, N_READY[FIN] + 8)
            for n in range(2 * TT):
                i, half = n // 2, n % 2
                if n >= 4:
                    pe.wait_ge(out_kept, n - 3)
                for j in range(4):
                    ins = nc.tensor.transpose(ps[:, n % 4, P * j:P * j + P], y[:, 4 * half + j, P * i:P * i + P],
                                              ident[:, :])
                ins.then_inc(out_turned, 1)

        @block.scalar
        def _(act):
            chain = [0]

            def link(ins):
                chain[0] += 1
                ins.then_inc(act_chain, 1)
                act.wait_ge(act_chain, chain[0])

            def split(n):
                if n >= NPAN:
                    return
                act.wait_ge(w_loaded[n % 3], 16 * LOADS[n])
                if n >= 2:
                    after_panel(act, n - 2)
                nc.scalar.copy(part_panel(w_hi, n), raw_panel(n)).then_inc(w_hi_ready, 1)

            def group(name, evacuate=None):
                g = G[name]
                for i, n in enumerate(g["panels"]):
                    if i == len(g["panels"]) - 1 and evacuate:
                        for m in range(g["tiles"]):
                            if g["by"] == "a":
                                act.wait_ge(tile_done, g["tile0"] + m + 1)
                            evacuate(m, ps[:, g["bank0"] + m, :])
                    if RELEASER[n] == name:
                        split(n + 2)

            def copy_to(dst, t=S, scale=None):
                def evacuate(m, src):
                    if scale is None:
                        nc.scalar.copy(dst(m), src[:, 0:t]).then_inc(free_a, 1)
                    else:
                        nc.scalar.mul(dst(m), src[:, 0:t], scale).then_inc(free_a, 1)
                return evacuate

            def norm(n, ready, free):
                t = ncols.get(n, S)
                ready()
                for k in range(KT):
                    if n or k >= 2:
                        act.wait_ge(sq_used, 8 * n + k - 1)
                    nc.scalar.activation(sq[:, k % 2, 0:t], source(n, k), ACT.Square).then_inc(sq_ready, 1)
                act.wait_ge(sq_used, 8 * n + 8)
                if n:
                    act.wait_ge(rstd_ready, n)
                nc.scalar.activation(root[:, 0:t], ps[:, 7, 0:t], ACT.Sqrt, bias=eps[:, :], scale=1.0 / D)\
                  .then_inc(root_ready, 1)
                if n not in PAIRED:
                    return
                if free:
                    computed(act, free)
                for k in range(KT):
                    act.wait_ge(t_ready, PAIRED[n] + k + 1)
                    if n in (MEM, MIX, XAT, FF):
                        ins = nc.scalar.copy(pair(n, k)[0], tmp[:, k % 2, 0:t])
                    else:
                        ins = nc.scalar.activation(pair(n, k)[0], tmp[:, k % 2, 0:t], ACT.Identity, bias=shift(n, k))
                    ins.then_inc(n_hi_ready, 1)

            act.wait_ge(ones_set, 1)
            norm(MEM, lambda: act.wait_ge(tok_kept, 4), None)
            split(0)
            split(1)
            group("xk", copy_to(lambda m: xk[:, m, :], L))
            group("xv", copy_to(lambda m: xv[:, m, :]))
            act.wait_ge(col_ready, 1)
            for i, name in enumerate(("c", "c_ctx")):
                nc.scalar.activation(silu[:, :, i], col[:, COL[name]:COL[name] + KT], ACT.Silu)\
                  .then_inc(silu_ready, 1)
            norm(CTX, lambda: act.wait_ge(tok_kept, 8), "xv")
            norm(X1, lambda: act.wait_ge(tok_kept, 16), None)
            group("f", copy_to(lambda m: f_t[:, m, :]))
            group("q", copy_to(lambda m: q_t[:, m, :]))
            group("k", copy_to(lambda m: k_t[:, m, :]))
            group("kc", copy_to(lambda m: kc_t[:, m, :], L))
            group("v", copy_to(lambda m: v[:, m, :]))
            group("vc", copy_to(lambda m: vc[:, m, :]))

            act.wait_ge(free_a, G["vc"]["a"])

            def head_square(n):
                src = q_t[:, n, :] if n < 4 else k_t[:, n - 4, :] if n < 8 else kc_t[:, 2 * n - 16:2 * n - 14, :]
                if n >= 2:
                    act.wait_ge(hn_sum, n - 1)
                dst = sq[:, n % 2, :]
                if n >= 8:
                    dst = dst.rearrange("p (a b) -> p a b", a=2)
                nc.scalar.activation(dst, src, ACT.Square).then_inc(hn_sq, 1)

            def head_root(n):
                act.wait_ge(hn_sum, n + 1)
                if n >= 2:
                    act.wait_ge(qk_ready, n - 1)
                nc.scalar.activation(ga[:, n % 2, :], ps[:, 6 + n % 2, :], ACT.Sqrt, bias=eps[:, :], scale=1.0 / HD)\
                  .then_inc(hn_root, 1)

            for n in range(10):
                head_square(n)
                head_root(n)
            for g in range(4):
                for x in range(2):
                    act.wait_ge(z_done, 2 * g + x + 1)
                    if g >= 2:
                        act.wait_ge(four_done, g - 1)
                    nc.scalar.copy(z[g % 2][:, 2 * x:2 * x + 2, :],
                                   ps[:, 2 + x, :].rearrange("p (a b) -> p a b", a=2)).then_inc(z_ready, 1)
                act.wait_ge(four_done, g + 1)
                nc.scalar.copy(u_hi[:, g, :], ps[:, 4 + g % 2, :]).then_inc(four_hi, 1)

            def na_exp_of(n):
                act.wait_ge(na_max, n + 1)
                nc.scalar.activation(p_na[n % 2][:, 0:S], p_na[n % 2][:, 0:S], ACT.Exp, bias=stats[:, 4, n:n + 1],
                                     accum_out=stats[:, 2, n:n + 1])
                nc.scalar.activation(p_na[n % 2][:, S:S + L], ps[:, 2 * (n % 2) + 1, 0:L], ACT.Exp,
                                     bias=stats[:, 4, n:n + 1], accum_out=stats[:, 3, n:n + 1]).then_inc(na_exp, 1)

            def na_keep(n):
                act.wait_ge(na_t, n + 1)
                if n >= 2:
                    act.wait_ge(na_pv, n - 1)
                nc.scalar.copy(pt_na[n % 2][:, :, :].rearrange("p a b -> p (a b)"),
                               ps[:, 4:6, :].rearrange("p a b -> p (a b)")[:, 0:768]).then_inc(na_pt, 1)

            act.wait_ge(four_kept, 4)
            act.wait_ge(z_ready, 8)
            na_exp_of(0)
            for n in range(NUNIT):
                if n + 1 < NUNIT:
                    na_exp_of(n + 1)
                na_keep(n)

            def turned_hi(which, dst, free):
                if free:
                    computed(act, free)
                for j in range(4):
                    act.wait_ge(ot_turned, 4 * which + j + 1)
                    nc.scalar.copy(dst(j), ps[:, j, :]).then_inc(ot_hi, 1)

            turned_hi(0, lambda j: u_hi[:, 4 + j, :], None)
            group("o0")
            group("o1")

            def mlp(l, n):
                prev = "o1" if l == 0 else "p1"
                norm(n, lambda: after_groups(act, prev), prev)

                def hidden(c):
                    g = G[f"m{l}a{c}"]

                    def evacuate(m, src):
                        t = 32 * l + 4 * c + m
                        if t >= 2:
                            act.wait_ge(a_ready, t - 1)
                        nc.scalar.activation(tmp[:, m % 2, :], src, ACT.Relu).then_inc(free_a, 1)
                        act.wait_ge(free_a, g["a"] - 4 + m + 1)
                        if m == 0 and c >= 2:
                            computed(act, f"m{l}b{c - 2}1")
                        nc.scalar.activation(a_hi[c % 2][:, m, :], tmp[:, m % 2, :], ACT.Square).then_inc(a_hi_ready, 1)
                    return evacuate

                group(f"m{l}a0", hidden(0))
                for c in range(8):
                    if c < 7:
                        group(f"m{l}a{c + 1}", hidden(c + 1))
                    group(f"m{l}b{c}0")
                    group(f"m{l}b{c}1")
            mlp(0, X2)
            norm(Y1, lambda: after_groups(act, "m0b71"), None)
            computed(act, "m0a7")
            for g in range(4):
                act.wait_ge(pooled, g + 1)
                nc.scalar.copy(u_hi[:, 2 * g:2 * g + 2, :], tmp[:, :, :]).then_inc(pooled_hi, 1)
            group("p0")
            group("p1")
            mlp(1, Y2)
            norm(MIX, lambda: after_groups(act, "m1b71"), "m1a7")
            group("qa", copy_to(lambda m: qa_t[:, m, :], scale=HD ** -0.5))
            group("kv1", copy_to(lambda m: (kcv_t[:, 0, :], kcv_t[:, 1, :], ks_t[:, :],
                                            vs[:, :, :].rearrange("p a b -> p (a b)"))[m]))

            def window_and_gates(m, src):
                if m < 2:
                    dst = (kw_t[:, :], vw[:, :, :].rearrange("p a b -> p (a b)"))[m]
                    nc.scalar.copy(dst, src).then_inc(free_a, 1)
                else:
                    nc.scalar.activation(gate[:, :, :].rearrange("p a b -> p (a b)"), src[:, 0:96], ACT.Sigmoid)\
                      .then_inc(free_a, 1)
            group("kv2", window_and_gates)
            group("qkb", copy_to(lambda m: qkb[:, m, :]))
            group("vb", copy_to(lambda m: vb[:, m, :]))
            group("rb", lambda m, src: nc.scalar.activation(rb[:, m, :], src, ACT.Silu).then_inc(free_a, 1))
            group("al", copy_to(lambda m: al[:, :]))
            for j in range(4):
                act.wait_ge(hid_done, j + 1)
                nc.scalar.activation(ghid[:, j, 0:NCMP], ps[:, j, 0:NCMP], ACT.Gelu_apprx_tanh).then_inc(hid_ready, 1)

            def parts(i):
                ws, ww = P * (i + 1), P * min(i + 1, 3)
                return (slice(896, 896 + NCMP), slice(0, ws), slice(S, S + ww))

            def ns_exp_of(n):
                act.wait_ge(ns_max, n + 1)
                pr = p_nsa[n % 2]
                for x, c in enumerate(parts(n % TT)):
                    ins = nc.scalar.activation(pr[:, c], pr[:, c], ACT.Exp, bias=stats[:, x, n:n + 1],
                                               accum_out=stats[:, 3 + x, n:n + 1])
                ins.then_inc(ns_exp, 1)

            def ns_keep(n):
                i = n % TT
                act.wait_ge(ns_t, n + 1)
                if n >= 2:
                    act.wait_ge(ns_pv, n - 1)
                pt = pt_nsa[n % 2][:, :, :].rearrange("p a b -> p (a b)")
                ws, ww = P * (i + 1), P * min(i + 1, 3)
                nc.scalar.copy(pt[:, 0:ws], ps[:, 4, 0:ws])
                nc.scalar.copy(pt[:, 512:512 + ww], ps[:, 5, 0:ww])
                nc.scalar.copy(pt[0:NCMP, 896:1024], ps[0:NCMP, 5, 384:512]).then_inc(ns_pt, 1)

            ns_exp_of(0)
            for n in range(NUNIT):
                if n + 1 < NUNIT:
                    ns_exp_of(n + 1)
                ns_keep(n)
            turned_hi(1, lambda j: on_hi[:, j, :], None)

            act.wait_ge(gz_done, 1)
            act.wait_ge(tab_ready, 8)
            for p in range(2):
                nc.scalar.activation(gt[:, p, :], ps[:, p, :], ACT.Abs,
                                     bias=col[:, COL["b_alpha"] + p:COL["b_alpha"] + p + 1]).then_inc(act_chain, 1)
            chain[0] += 2
            act.wait_ge(act_chain, chain[0])
            link(nc.scalar.activation(gt[:, :, :], gt[:, :, :], ACT.Exp, scale=-1.0))
            nc.scalar.activation(gt[:, :, :], gt[:, :, :], ACT.Ln, bias=ones[:, 0:1]).then_inc(gz_log, 1)
            act.wait_ge(gla_b, 1)
            nc.scalar.activation(ga[:, :, :], la[0][:, :, :], ACT.Exp, scale=1.0 / 16).then_inc(gla_e, 1)
            nc.scalar.activation(gt[:, :, :], la[0][:, :, :], ACT.Exp, scale=-1.0 / 16).then_inc(gla_e, 1)
            act.wait_ge(gla_b, 2)
            act.wait_ge(gla_qk, 1)
            nc.scalar.activation(ga[:, :, :], la[1][:, :, :], ACT.Exp, scale=1.0 / 16).then_inc(gla_e, 1)
            nc.scalar.activation(dec[:, :, :], la[0][:, :, CHUNK - 1::CHUNK], ACT.Exp, scale=1.0 / 16)\
              .then_inc(gla_e, 1)
            act.wait_ge(gla_qk, 3)
            for hh in range(4):
                act.wait_ge(go_done, hh + 1)
                if hh >= 2:
                    act.wait_ge(go_sum, hh - 1)
                nc.scalar.activation(gt[:, hh % 2, :], ps[:, 6 + hh % 2, :], ACT.Square).then_inc(go_sq, 1)
                act.wait_ge(go_sum, hh + 1)
                if hh:
                    act.wait_ge(go_t, hh)
                nc.scalar.activation(root[:, :], ps[:, hh % 2, :], ACT.Sqrt, bias=eps[:, :], scale=1.0 / P)\
                  .then_inc(go_root, 1)
                act.wait_ge(go_t, hh + 1)
                nc.scalar.copy(og_hi[:, hh, :], tmp[:, hh % 2, :]).then_inc(go_hi, 1)

            act.wait_ge(go_ready, 4)
            for j in range(4):
                group(f"mg{j}", lambda m, src, j=j: nc.scalar.activation(mg[4 * j + m][:, :], src, ACT.Sigmoid)
                      .then_inc(free_a, 1))

            def mixed(j):
                def evacuate(m, src):
                    act.wait_ge(mix_t, 4 * j + m + 1)
                    nc.scalar.copy(u_hi[:, 4 * j + m, :], tmp[:, m % 2, :]).then_inc(mix_hi, 1)
                return evacuate
            for j in range(2):
                group(f"bn{j}")
                group(f"bg{j}", mixed(j))
            group("ow0")
            group("ow1")

            norm(XAT, lambda: after_groups(act, "ow1"), "ow1")
            group("xq", copy_to(lambda m: xq_t[:, m, :], scale=float(np.float32(P ** -0.5))))

            def xa_exp_of(n):
                act.wait_ge(xa_max, n + 1)
                if n >= 2:
                    act.wait_ge(xa_t, n - 1)
                nc.scalar.activation(p_x[n % 2][:, :], ps[:, n % 2, 0:L], ACT.Exp, bias=stats[:, 1, n:n + 1],
                                     accum_out=stats[:, 2, n:n + 1]).then_inc(xa_exp, 1)

            def xa_keep(n):
                act.wait_ge(xa_t, n + 1)
                if n >= 2:
                    act.wait_ge(xa_pv, n - 1)
                nc.scalar.copy(pt_x[n % 2][:, :, :].rearrange("p a b -> p (a b)"), ps[:, 2 + n % 2, 0:L])\
                  .then_inc(xa_pt, 1)

            xa_exp_of(0)
            for n in range(4 * TT):
                if n + 1 < 4 * TT:
                    xa_exp_of(n + 1)
                xa_keep(n)
            turned_hi(2, lambda j: xo_hi[:, j, :], None)
            group("xo0")
            group("xo1")

            norm(FF, lambda: after_groups(act, "xo1"), "xq")
            for c, nt in enumerate(FC):
                def conv(m, src, c=c):
                    t = 4 * c + m
                    act.wait_ge(tile_done, G[f"fu{c}"]["tile0"] + m + 1)
                    w0 = COL["conv_w"] + 2 * FT + t
                    nc.scalar.activation(cv[:, m, :], src, ACT.Identity, scale=col[:, w0:w0 + 1],
                                         bias=col[:, COL["conv_b"] + t:COL["conv_b"] + t + 1]).then_inc(c_ready, 1)

                group(f"fu{c}", conv)
                for m in range(nt):
                    act.wait_ge(free_d, G[f"fu{c}"]["d"] - nt + m + 1)
                    nc.scalar.activation(ub[:, m, :], cv[:, m, :], ACT.Gelu_apprx_tanh).then_inc(c_gelu, 1)

                def gated(m, src, c=c, nt=nt):
                    act.wait_ge(free_d, G[f"fg{c}"]["d"] - nt + m + 1)
                    if m == 0 and c >= 2:
                        computed(act, f"fd{c - 2}1")
                    nc.scalar.copy(a_hi[c % 2][:, m, :], tmp[:, m % 2, :]).then_inc(f_hi, 1)
                group(f"fg{c}", gated)
                group(f"fd{c}0")
                group(f"fd{c}1")
            norm(FIN, lambda: after_groups(act, "fd51"), None)

        @block.gpsimd
        def _(pool):
            nc.gpsimd.memset(eps[:, :], EPS)
            nc.gpsimd.memset(ones[:, :], 1.0).then_inc(ones_set, 1)

            def split(n):
                pool.wait_ge(w_hi_ready, n + 1)
                nc.gpsimd.tensor_tensor(part_panel(w_lo, n), raw_panel(n), part_panel(w_hi, n).bitcast(F32),
                                        ALU.subtract).then_inc(w_lo_ready, 1)

            def through(name, n0):
                n1 = min(G[name]["panels"][-1] + 3, NPAN)
                for n in range(n0, n1):
                    split(n)
                return n1

            n0 = through("vc", 0)
            pool.wait_ge(ones_set, 1)
            nc.gpsimd.memset(pad[:, :], 0.0).then_inc(pad_set, 1)
            n0 = through("m0b71", n0)
            n0 = through("p1", n0)
            n0 = through("m1b71", n0)
            n0 = through("al", n0)
            pool.wait_ge(tab_loaded, 32)
            for hh in range(NH):
                if hh >= 2:
                    pool.wait_ge(ns_max, 4 * (hh - 1))
                nc.gpsimd.tensor_scalar(ntab[hh % 2][:, :], tab[:, :], SLOPES[hh], 1.0, ALU.mult, ALU.mult)\
                  .then_inc(tab_ready, 1)
            pool.wait_ge(ot_turned, 8)
            for i in range(2):
                nc.gpsimd.memset(att[i][:, :, :], 0.0).then_inc(att_zero, 1)
            through("fd51", n0)

        @block.vector
        def _(dve):
            chain = [0]

            def link(ins):
                chain[0] += 1
                ins.then_inc(dve_chain, 1)
                dve.wait_ge(dve_chain, chain[0])

            for n in range(16):
                i, half = n // 2, n % 2
                dve.wait_ge(tok_turned, n + 1)
                dst, t = ((mem_t, i) if i < 2 else (ctx_t, i - 2) if i < 4 else (h, i - 4))
                nc.vector.tensor_copy(dst[:, 4 * half:4 * half + 4, P * t:P * t + P],
                                      ps[:, n % 4, :].rearrange("p (a b) -> p a b", a=4)).then_inc(tok_kept, 1)
                if n == 3:
                    dve.wait_ge(rows_turned, 1)
                    nc.vector.tensor_copy(col[:, :], ps[:, 4, 0:NCOL]).then_inc(col_ready, 1)
            dve.wait_ge(col_ready, 1)
            dve.wait_ge(tok_kept, 16)

            def norm(n, dst=None):
                t = ncols.get(n, S)
                dve.wait_ge(root_ready, n + 1)
                nc.vector.reciprocal(rstd[:, 0:t], root[:, 0:t]).then_inc(rstd_ready, 1)
                dve.wait_ge(rstd_ready, n + 1)

                def lower(k):
                    hi, lo = pair(n, k)
                    dve.wait_ge(n_hi_ready, PAIRED[n] + k + 1)
                    if n in (MEM, MIX, XAT, FF):
                        ins = nc.vector.tensor_tensor(lo, tmp[:, k % 2, 0:t], hi.bitcast(F32), ALU.subtract)
                    else:
                        ins = nc.vector.scalar_tensor_tensor(lo, tmp[:, k % 2, 0:t], shift(n, k), hi.bitcast(F32),
                                                             ALU.add, ALU.subtract)
                    ins.then_inc(n_ready, 1)

                if n == FIN:
                    for k in range(KT):
                        nc.vector.scalar_tensor_tensor(y[:, k, :], h[:, k, :], gain(n, k), rstd[:, :], ALU.mult,
                                                       ALU.mult).then_inc(n_ready, 1)
                    return
                if n == Y1:
                    for k in range(KT):
                        if k >= 2:
                            dve.wait_ge(n_ready, 8 * n + k - 1)
                        link(nc.vector.scalar_tensor_tensor(tmp[:, k % 2, :], h[:, k, :], gain(n, k), rstd[:, :],
                                                            ALU.mult, ALU.mult))
                        nc.vector.tensor_scalar(up[:, k, 8:8 + S], tmp[:, k % 2, :], shift(n, k), None, ALU.add)\
                          .then_inc(n_ready, 1)
                    return
                for k in range(KT):
                    if k >= 2:
                        dve.wait_ge(n_ready, 8 * n + k - 1)
                    nc.vector.scalar_tensor_tensor(tmp[:, k % 2, 0:t], source(n, k), gain(n, k), rstd[:, 0:t],
                                                   ALU.mult, ALU.mult).then_inc(t_ready, 1)
                    if k:
                        lower(k - 1)
                lower(KT - 1)

            def modulation(l):
                bank = (6, 7)[l]
                b0 = COL["b_mod"] + 48 * l
                dve.wait_ge(mod_used, NMOD * (l + 1))
                link(nc.vector.tensor_tensor(modc[:, l, :, :],
                                             ps[:, bank, 0:96].rearrange("p (a b) -> p a b", b=2),
                                             col[:, b0:b0 + 48].unsqueeze(2).broadcast_to([P, 48, 2]), ALU.add))
                jobs = [(CTX, 8, 1, "norm1"), (X1, 8, 0, "norm1"), (X2, 32, 0, "norm2")] if l == 0 else \
                       [(Y1, 8, 0, "norm1"), (Y2, 32, 0, "norm2")]
                for n, t0, src, name in jobs:
                    c0 = COL[name] + 8 * l
                    ins = nc.vector.scalar_tensor_tensor(gcol[:, n, :], modc[:, l, t0:t0 + 8, src], 1.0,
                                                         col[:, c0:c0 + 8], ALU.add, ALU.mult)
                if l == 1:
                    c0 = COL["pool_scale"]
                    ins = nc.vector.tensor_tensor(gcol[:, 6, :], modc[:, 1, 16:24, 0], col[:, c0:c0 + 8], ALU.mult)
                ins.then_inc(mod_ready, 1)
                dve.wait_ge(mod_ready, l + 1)

            def residual(name, j, gate_of=None):
                g = G[name]
                if g["d"] > 4:
                    dve.wait_ge(free_d, g["d"] - 4)
                for m in range(4):
                    dve.wait_ge(tile_done, g["tile0"] + m + 1)
                    k = 4 * j + m
                    src = ps[:, g["bank0"] + m, :]
                    if gate_of:
                        ins = nc.vector.scalar_tensor_tensor(h[:, k, :], src, gate_of(k), h[:, k, :], ALU.mult, ALU.add)
                    else:
                        ins = nc.vector.tensor_tensor(h[:, k, :], src, h[:, k, :], ALU.add)
                    ins.then_inc(free_d, 1)

            norm(MEM)
            modulation(0)
            norm(CTX)
            norm(X1)

            link(nc.vector.tensor_scalar(gcol[:, 7, 0:1], col[:, COL["qg"]:COL["qg"] + 1], HD ** -0.5, None, ALU.mult))
            for n in range(10):
                dve.wait_ge(hn_root, n + 1)
                link(nc.vector.reciprocal(tmp[:, n % 2, :], ga[:, n % 2, :]))
                x = q_t[:, n, :] if n < 4 else k_t[:, n - 4, :] if n < 8 else kc_t[:, 2 * n - 16:2 * n - 14, :]
                g = gcol[:, 7, 0:1] if n < 4 else col[:, COL["kg"]:COL["kg"] + 1]
                r = tmp[:, n % 2, :]
                if n >= 8:
                    r = r.rearrange("p (a b) -> p a b", a=2)
                nc.vector.scalar_tensor_tensor(x, x, g, r, ALU.mult, ALU.mult).then_inc(qk_ready, 1)
            dve.wait_ge(cw_done, 1)
            nc.vector.tensor_copy(cw[:, :, :].rearrange("p a b -> p (a b)"),
                                  ps[:, 0:2, :].rearrange("p a b -> p (a b)")).then_inc(cw_ready, 1)
            for g in range(4):
                dve.wait_ge(four_hi, g + 1)
                nc.vector.tensor_tensor(u_lo[:, g, :], ps[:, 4 + g % 2, :], u_hi[:, g, :].bitcast(F32), ALU.subtract)\
                   .then_inc(four_kept, 1)

            dve.wait_ge(pad_loaded, 32)
            dve.wait_ge(pad_set, 1)
            nc.vector.tensor_copy(pad[:, 48:79], rpb_in[:, ::-1]).then_inc(pad_set, 1)

            def bias_ready(hh):
                dve.wait_ge(gb_loaded[hh % 2], 32 * (hh // 2 + 1))
                nc.vector.tensor_tensor(gb[hh % 2][:, :, :], gb[hh % 2][:, :, :],
                                        near[:, :].unsqueeze(1).broadcast_to([P, 14, GRID]), ALU.add)\
                   .then_inc(gb_ready, 1)

            def na_scores(n):
                hh, i, b = n // TT, n % TT, 2 * (n % 2)
                dve.wait_ge(na_s, n + 1)
                dve.wait_ge(gb_ready, hh + 1)
                if n >= 2:
                    dve.wait_ge(na_t, n - 1)
                nc.vector.tensor_tensor_reduce(p_na[n % 2][:, 0:S].rearrange("p (a b) -> p a b", b=GRID),
                                               ps[:, b, :].rearrange("p (a b) -> p a b", b=GRID),
                                               gb[hh % 2][:, 6 - 2 * i:14 - 2 * i, ::-1],
                                               1.0, NEG, ALU.add, ALU.max, stats[:, 0, n:n + 1])
                link(nc.vector.reduce_max(stats[:, 1, n:n + 1], ps[:, b + 1, 0:L], X))
                nc.vector.tensor_scalar(stats[:, 4, n:n + 1], stats[:, 0, n:n + 1], stats[:, 1, n:n + 1], -1.0,
                                        ALU.max, ALU.mult).then_inc(na_max, 1)

            def na_out(n):
                hh, i = n // TT, n % TT
                dve.wait_ge(na_pv, n + 1)
                link(nc.vector.tensor_tensor(stats[:, 5, n:n + 1], stats[:, 2, n:n + 1], stats[:, 3, n:n + 1], ALU.add))
                link(nc.vector.reciprocal(stats[:, 6, n:n + 1], stats[:, 5, n:n + 1]))
                nc.vector.tensor_scalar(o_na[:, i, HD * hh:HD * hh + HD], ps[:, 6, HD * (n % 8):HD * (n % 8) + HD],
                                        stats[:, 6, n:n + 1], None, ALU.mult).then_inc(na_o, 1)

            bias_ready(0)
            for n in range(NUNIT + 1):
                if n < NUNIT:
                    na_scores(n)
                    if n % TT == 2 and n // TT + 1 < NH:
                        bias_ready(n // TT + 1)
                if n:
                    na_out(n - 1)
            modulation(1)

            def turned_lo(which, hi, lo):
                for j in range(4):
                    dve.wait_ge(ot_hi, 4 * which + j + 1)
                    nc.vector.tensor_tensor(lo(j), ps[:, j, :], hi(j).bitcast(F32), ALU.subtract).then_inc(ot_kept, 1)

            turned_lo(0, lambda j: u_hi[:, 4 + j, :], lambda j: u_lo[:, 4 + j, :])
            for j in range(2):
                residual(f"o{j}", j, lambda k: g_mod(0, False, k))

            def mlp(l, n):
                norm(n)

                def hidden(c):
                    g = G[f"m{l}a{c}"]
                    for m in range(4):
                        t = 32 * l + 4 * c + m
                        dve.wait_ge(free_a, g["a"] - 4 + m + 1)
                        link(nc.vector.tensor_tensor(sq[:, m % 2, :], tmp[:, m % 2, :], tmp[:, m % 2, :], ALU.mult))
                        dve.wait_ge(a_hi_ready, t + 1)
                        nc.vector.tensor_tensor(a_lo[c % 2][:, m, :], sq[:, m % 2, :],
                                                a_hi[c % 2][:, m, :].bitcast(F32), ALU.subtract).then_inc(a_ready, 1)

                hidden(0)
                for c in range(8):
                    if c < 7:
                        hidden(c + 1)
                    for j in range(2):
                        residual(f"m{l}b{c}{j}", j, lambda k: g_mod(l, True, k))

            mlp(0, X2)

            for k in range(KT):
                nc.vector.memset(up[:, k, 0:8], 0.0)
                nc.vector.memset(up[:, k, 8 + S:16 + S], 0.0)
            norm(Y1)
            dve.wait_ge(n_ready, 8 * Y1 + 8)
            dve.wait_ge(cnt_loaded, 16)
            for g in range(4):
                src, reach = up[:, 2 * g:2 * g + 2, :], 1
                a0, a1 = 1, S + 16
                link(nc.vector.tensor_tensor(win[0][:, :, a0:a1], src[:, :, a0 - 1:a1 - 1], src[:, :, a0:a1], ALU.add))
                now = 0
                for _ in range(g):
                    a0, a1 = a0 + reach, a1 - reach
                    link(nc.vector.tensor_tensor(win[1 - now][:, :, a0:a1], win[now][:, :, a0 - reach:a1 - reach],
                                                 win[now][:, :, a0 + reach:a1 + reach], ALU.add))
                    now, reach = 1 - now, 2 * reach
                link(nc.vector.tensor_tensor(win[1 - now][:, :, 0:S], win[now][:, :, 8:8 + S],
                                             cnt[:, g:g + 1, :].broadcast_to([P, 2, S]), ALU.mult))
                if g:
                    dve.wait_ge(pooled_hi, g)
                nc.vector.tensor_tensor(tmp[:, :, :], win[1 - now][:, :, 0:S], src[:, :, 8:8 + S], ALU.subtract)\
                   .then_inc(pooled, 1)
                dve.wait_ge(pooled_hi, g + 1)
                nc.vector.tensor_tensor(u_lo[:, 2 * g:2 * g + 2, :], tmp[:, :, :],
                                        u_hi[:, 2 * g:2 * g + 2, :].bitcast(F32), ALU.subtract).then_inc(pooled_ready, 1)
            for j in range(2):
                residual(f"p{j}", j, lambda k: gcol[:, 6, k:k + 1])
            mlp(1, Y2)
            norm(MIX)

            dve.wait_ge(pos_turned, 1)
            link(nc.vector.tensor_copy(pos[:, :, :].rearrange("p a b -> p (a b)"), ps[:, 6, 0:64]))
            dve.wait_ge(free_a, G["al"]["a"])
            for x in range(2):
                for half in range(2):
                    ins = nc.vector.tensor_tensor(
                        kpos[x][:, half, :].rearrange("p (n l) -> p n l", l=16),
                        kcv_t[:, x, :].rearrange("p (n l) -> p n l", l=16),
                        pos[:, x, 16 * half:16 * half + 16].unsqueeze(1).broadcast_to([P, 32, 16]), ALU.add)
                ins.then_inc(kpos_ready, 1)
            dve.wait_ge(cmp_done, 1)
            nc.vector.tensor_copy(kcm[:, 0:NCMP], ps[:, 4, 0:NCMP])
            nc.vector.tensor_copy(vcm[:, :, :].rearrange("p a b -> p (a b)"), ps[0:NCMP, 5, 0:P])
            dve.wait_ge(tab_loaded, 32)
            for i in range(TT):
                ins = nc.vector.tensor_scalar(gate[:, i, 0:24:3], gate[:, i, 0:24:3], valid[:, i:i + 1], None, ALU.mult)
            ins.then_inc(cmp_ready, 1)
            dve.wait_ge(cmp_ready, 1)

            def ns_scores(n):
                hh, i, b = n // TT, n % TT, 2 * (n % 2)
                ws, ww = P * (i + 1), P * min(i + 1, 3)
                t = ntab[hh % 2]
                pr = p_nsa[n % 2]
                dve.wait_ge(ns_s, n + 1)
                dve.wait_ge(tab_ready, hh + 1)
                if n >= 2:
                    dve.wait_ge(ns_t, n - 1)
                for x, (dst, src, bias) in enumerate((
                        (pr[:, 896:896 + NCMP], ps[:, b + 1, 384:384 + NCMP],
                         t[:, 896 + NCMP * i:896 + NCMP * i + NCMP]),
                        (pr[:, 0:ws], ps[:, b, 0:ws], t[:, S - ws:S]),
                        (pr[:, S:S + ww], ps[:, b + 1, 0:ww], t[:, 896 - ww:896]))):
                    ins = nc.vector.tensor_tensor_reduce(dst, src, bias, 1.0, 3.0e38 * -1, ALU.add, ALU.max,
                                                         stats[:, x, n:n + 1])
                link(ins)
                nc.vector.tensor_scalar(stats[:, 0:3, n], stats[:, 0:3, n], -1.0, None, ALU.mult).then_inc(ns_max, 1)

            def ns_out(n):
                hh, i, b = n // TT, n % TT, 6 + n % 2
                dve.wait_ge(ns_pv, n + 1)
                c = stats[:, 3:6, n]
                link(nc.vector.reciprocal(c, c))
                link(nc.vector.tensor_tensor(c, c, gate[:, i, 3 * hh:3 * hh + 3], ALU.mult))
                o = o_nsa[:, i, HD * hh:HD * hh + HD]
                link(nc.vector.tensor_scalar(o, ps[:, b, 0:HD], stats[:, 4, n:n + 1], None, ALU.mult))
                link(nc.vector.scalar_tensor_tensor(o, ps[:, b, HD:2 * HD], stats[:, 5, n:n + 1], o, ALU.mult, ALU.add))
                nc.vector.scalar_tensor_tensor(o, ps[:, b, 2 * HD:3 * HD], stats[:, 3, n:n + 1], o, ALU.mult, ALU.add)\
                   .then_inc(ns_o, 1)

            for n in range(NUNIT + 1):
                if n < NUNIT:
                    ns_scores(n)
                if n:
                    ns_out(n - 1)
            turned_lo(1, lambda j: on_hi[:, j, :], lambda j: on_lo[:, j, :])

            dve.wait_ge(gz_log, 1)
            for p in range(2):
                ins = nc.vector.tensor_scalar(ga[:, p, :], ps[:, p, :],
                                              col[:, COL["b_alpha"] + p:COL["b_alpha"] + p + 1], 0.0, ALU.add, ALU.min)
            link(ins)
            link(nc.vector.tensor_tensor(la[0][:, :, :], ga[:, :, :], gt[:, :, :], ALU.subtract))

            def chunks(t):
                return t[:, :, :].rearrange("p a (c j) -> p (a c) j", j=CHUNK)

            now, reach = 0, 1
            while reach < CHUNK:
                x, y_ = chunks(la[now]), chunks(la[1 - now])
                nc.vector.tensor_copy(y_[:, :, 0:reach], x[:, :, 0:reach])
                ins = nc.vector.tensor_tensor(y_[:, :, reach:], x[:, :, reach:], x[:, :, :CHUNK - reach], ALU.add)
                now, reach = 1 - now, 2 * reach
                if reach < CHUNK:
                    link(ins)
            ins.then_inc(gla_b, 1)
            dve.wait_ge(gla_b, 1)
            b = chunks(la[0])
            nc.vector.tensor_tensor(chunks(la[1]), b[:, :, CHUNK - 1:CHUNK].broadcast_to([P, 2 * NCH, CHUNK]), b,
                                    ALU.subtract).then_inc(gla_b, 1)
            dve.wait_ge(gla_e, 1)
            nc.vector.scalar_tensor_tensor(qd[:, :, :], qkb[:, 0:2, :], HD ** -0.5, ga[:, :, :], ALU.mult, ALU.mult)\
               .then_inc(gla_qk, 1)
            dve.wait_ge(gla_e, 2)
            nc.vector.tensor_tensor(kd[:, :, :], qkb[:, 2:4, :], gt[:, :, :], ALU.mult).then_inc(gla_qk, 1)
            dve.wait_ge(gla_e, 3)
            nc.vector.tensor_tensor(ks[:, :, :], qkb[:, 2:4, :], ga[:, :, :], ALU.mult).then_inc(gla_qk, 1)
            dve.wait_ge(kst_done, 1)
            nc.vector.tensor_copy(kst[:, :, :].rearrange("p a b -> p (a b)"),
                                  ps[:, 2:4, :].rearrange("p a b -> p (a b)")).then_inc(kst_ready, 1)
            dve.wait_ge(inc_done, 1)
            dve.wait_ge(gla_e, 4)
            for c in range(NCH - 1):
                for p in range(2):
                    inc = ps[:, 2 * p + c % 2, P * (c // 2):P * (c // 2) + P]
                    if c == 0:
                        ins = nc.vector.tensor_copy(st[:, p, 1, :], inc)
                    else:
                        ins = nc.vector.scalar_tensor_tensor(st[:, p, c + 1, :], st[:, p, c, :], dec[:, p, c:c + 1],
                                                             inc, ALU.mult, ALU.add)
                if c < NCH - 2:
                    link(ins)
            ins.then_inc(st_ready, 1)
            dve.wait_ge(att_zero, 2)
            dve.wait_ge(gmask_loaded, 16)

            def gla_attention(hh):
                dve.wait_ge(att_done, hh + 1)
                if hh >= 2:
                    dve.wait_ge(go_done, hh - 1)
                nc.vector.copy_predicated(att[hh % 2][:, :, :], gmask[:, :].unsqueeze(1).broadcast_to([P, TT, P]),
                                          ps[:, 4 + hh % 2, :].rearrange("p (a b) -> p a b", a=TT))\
                   .then_inc(att_ready, 1)

            def gla_norm(hh):
                o = ps[:, 6 + hh % 2, :]
                t = tmp[:, hh % 2, :]
                dve.wait_ge(go_root, hh + 1)
                link(nc.vector.reciprocal(rstd[:, :], root[:, :]))
                link(nc.vector.scalar_tensor_tensor(t, o, col[:, COL["gla_norm"]:COL["gla_norm"] + 1], rstd[:, :],
                                                    ALU.mult, ALU.mult))
                nc.vector.tensor_tensor(t, t, rb[:, hh, :], ALU.mult).then_inc(go_t, 1)
                dve.wait_ge(go_hi, hh + 1)
                nc.vector.tensor_tensor(og_lo[:, hh, :], t, og_hi[:, hh, :].bitcast(F32), ALU.subtract)\
                   .then_inc(go_ready, 1)

            gla_attention(0)
            for hh in range(4):
                if hh < 3:
                    gla_attention(hh + 1)
                gla_norm(hh)

            for j in range(2):
                gn, gg = G[f"bn{j}"], G[f"bg{j}"]
                for m in range(4):
                    dve.wait_ge(tile_done, gn["tile0"] + m + 1)
                    nc.vector.tensor_tensor(mixn[:, m, :], ps[:, gn["bank0"] + m, :], mg[4 * j + m][:, :], ALU.mult)\
                       .then_inc(free_d, 1)
                for m in range(4):
                    dve.wait_ge(tile_done, gg["tile0"] + m + 1)
                    k = 4 * j + m
                    nc.vector.tensor_tensor(tmp[:, m % 2, :], ps[:, gg["bank0"] + m, :], mg[8 + k][:, :], ALU.mult)\
                       .then_inc(free_d, 1)
                    dve.wait_ge(free_d, gg["d"] - 4 + m + 1)
                    nc.vector.tensor_tensor(tmp[:, m % 2, :], tmp[:, m % 2, :], mixn[:, m, :], ALU.add)\
                       .then_inc(mix_t, 1)
                    dve.wait_ge(mix_hi, k + 1)
                    nc.vector.tensor_tensor(u_lo[:, k, :], tmp[:, m % 2, :], u_hi[:, k, :].bitcast(F32), ALU.subtract)\
                       .then_inc(mix_ready, 1)
            for j in range(2):
                residual(f"ow{j}", j)
            norm(XAT)

            def xa_max_of(n):
                dve.wait_ge(xa_s, n + 1)
                link(nc.vector.reduce_max(stats[:, 0, n:n + 1], ps[:, n % 2, 0:L], X))
                nc.vector.tensor_scalar(stats[:, 1, n:n + 1], stats[:, 0, n:n + 1], -1.0, None, ALU.mult)\
                   .then_inc(xa_max, 1)

            def xa_out(n):
                hh, i = n // TT, n % TT
                dve.wait_ge(xa_pv, n + 1)
                link(nc.vector.reciprocal(stats[:, 3, n:n + 1], stats[:, 2, n:n + 1]))
                nc.vector.tensor_scalar(o_x[:, i, P * hh:P * hh + P], ps[:, 4 + n % 2, 0:P], stats[:, 3, n:n + 1],
                                        None, ALU.mult).then_inc(xa_o, 1)

            for n in range(4 * TT + 1):
                if n < 4 * TT:
                    xa_max_of(n)
                if n:
                    xa_out(n - 1)
            turned_lo(2, lambda j: xo_hi[:, j, :], lambda j: xo_lo[:, j, :])
            for j in range(2):
                residual(f"xo{j}", j)

            norm(FF)
            for c, nt in enumerate(FC):
                gu, gg = G[f"fu{c}"], G[f"fg{c}"]
                for m in range(nt):
                    t = 4 * c + m
                    src = ps[:, gu["bank0"] + m, :]
                    w0 = COL["conv_w"] + t
                    dve.wait_ge(c_ready, t + 1)
                    link(nc.vector.scalar_tensor_tensor(cv[:, m, 1:], src[:, :S - 1], col[:, w0 + FT:w0 + FT + 1],
                                                        cv[:, m, 1:], ALU.mult, ALU.add))
                    nc.vector.scalar_tensor_tensor(cv[:, m, 2:], src[:, :S - 2], col[:, w0:w0 + 1], cv[:, m, 2:],
                                                   ALU.mult, ALU.add).then_inc(free_d, 1)
                for m in range(nt):
                    t = 4 * c + m
                    dve.wait_ge(tile_done, gg["tile0"] + m + 1)
                    dve.wait_ge(c_gelu, t + 1)
                    nc.vector.tensor_tensor(tmp[:, m % 2, :], ps[:, gg["bank0"] + m, :], ub[:, m, :], ALU.mult)\
                       .then_inc(free_d, 1)
                    dve.wait_ge(f_hi, t + 1)
                    nc.vector.tensor_tensor(a_lo[c % 2][:, m, :], tmp[:, m % 2, :],
                                            a_hi[c % 2][:, m, :].bitcast(F32), ALU.subtract).then_inc(f_pair, 1)
                for j in range(2):
                    residual(f"fd{c}{j}", j)
            norm(FIN)
            for n in range(2 * TT):
                i, half = n // 2, n % 2
                dve.wait_ge(out_turned, n + 1)
                if i >= 2 and half == 0:
                    dve.wait_ge(out_stored[i % 2], 16 * (i // 2))
                nc.vector.tensor_copy(y_out[i % 2][:, 512 * half:512 * half + 512], ps[:, n % 4, :]).then_inc(out_kept, 1)


_OUT = (1, S, D)


def kernel(**inputs):
    import concourse.bacc as _bacc
    from concourse.bass_utils import run_bass_kernel_spmd as _run

    nc = _bacc.Bacc("TRN2", target_bir_lowering=False, num_devices=1)
    arrays, aps = {}, {}
    for name, value in {**inputs, **host_constants()}.items():
        value = np.ascontiguousarray(value)
        arrays[f"in_{name}"] = value
        aps[name] = nc.dram_tensor(f"in_{name}", value.shape, mybir.dt.from_np(value.dtype), kind="ExternalInput").ap()
    out = nc.dram_tensor("out_y", _OUT, F32, kind="ExternalOutput").ap()
    build(nc, aps, out)
    r = _run(nc, [arrays], core_ids=[0])
    return r.results[0]["out_y"]
```

```python
from contextlib import ExitStack

import numpy as np
import concourse.bass as bass
from concourse import mybir

ALU = mybir.AluOpType
ACT = mybir.ActivationFunctionType
F32 = mybir.dt.float32
F32R = mybir.dt.float32r
I32 = mybir.dt.int32
X = mybir.AxisListType.X

P = 128
D = 1024
S = 512
L = 256
KT = D // P
TT = S // P
LT = L // P
HD = 64
NH = 8
GRID = 64
NCMP = 31
CHUNK = 64
NCH = S // CHUNK
FFN = 2816
FT = FFN // P
WINDOW = 256
NEG = -1e30
EPS = 1e-6
PW = 2048

ROWS0 = [("c", 8), ("c_ctx", 8), ("norm1", 16), ("norm2", 16), ("ln_mix", 8), ("ln_x", 8), ("ln_mem", 8),
         ("ln_ffn", 8), ("ln_final", 8), ("pool_scale", 8), ("b_alpha", 2), ("gla_norm", 1), ("qg", 1), ("kg", 1)]
ROWS1 = [("b_mod", 96)]
ROWS2 = [("conv_w", 66), ("conv_b", 22)]


def column_places():
    at, where = 0, {}
    for rows in (ROWS0, ROWS1, ROWS2):
        for name, n in rows:
            where[name] = at
            at += n
    return where, at


COL, NCOL = column_places()


def host_constants():
    n = np.arange(S)
    angle = 2 * np.pi * ((n[:, None] * n[None, :]) % S) / S
    scale = 1.0 / np.sqrt(S * P)
    c = np.arange(P)
    angle_c = 2 * np.pi * ((c[:, None] * c[None, :]) % P) / P
    dft = np.stack([np.cos(angle) * scale, -np.sin(angle) * scale]).astype(np.float32)
    dft_c = np.stack([np.cos(angle_c), np.sin(angle_c)]).astype(np.float32)
    ident = np.eye(P, dtype=np.float32)
    halves = np.kron(np.eye(2), np.ones((HD, HD))).astype(np.float32)
    col = np.arange(GRID)
    start = np.clip(col - 8, 0, GRID - 16)
    near = (col[None, :] >= start[:, None]) & (col[None, :] < start[:, None] + 16)
    near = np.where(near, 0.0, NEG).astype(np.float32)
    near = np.concatenate([near, near], 0)[:, ::-1]
    p = np.arange(P)[:, None]
    dist = p - np.arange(S)[None, :] + (S - P)
    causal = np.where(dist >= 0, -dist, NEG).astype(np.float32)
    window = np.where((dist >= 0) & (dist < WINDOW), -dist, NEG).astype(np.float32)
    end = np.arange(NCMP) * 16 + 31
    t = np.arange(S).reshape(TT, P, 1)
    dc = t - end[None, None, :]
    cmp_bias = np.where(dc >= 0, -dc, NEG).astype(np.float32).transpose(1, 0, 2)
    j, i = np.arange(P)[:, None], np.arange(P)[None, :]
    gla_mask = ((j // CHUNK == i // CHUNK) & (j <= i)).astype(np.int32)
    cnt = []
    for w in (2, 4, 8, 16):
        lo, hi = np.clip(n - w // 2, 0, S), np.clip(n + w - w // 2, 0, S)
        cnt.append(1.0 / (hi - lo))
    cnt = np.broadcast_to(np.stack(cnt)[None], (P, 4, S)).astype(np.float32)
    valid = (np.arange(S).reshape(TT, P).T >= 31).astype(np.float32)
    tab = np.concatenate([causal, window[:, P:], cmp_bias.reshape(P, TT * NCMP)], 1)
    arrays = {"k_dft": dft.reshape(2, TT, P, S).transpose(2, 0, 1, 3), "k_dft_c": dft_c.transpose(1, 0, 2),
              "k_ident": ident, "k_halves": halves, "k_near": near, "k_tab": tab, "k_valid": valid,
              "k_gla_mask": gla_mask, "k_cnt": cnt}
    return {name: np.ascontiguousarray(x) for name, x in arrays.items()}


class Plan:

    def __init__(self):
        self.panels = []
        self.groups = {}
        self.order = []

    def panel(self, src, kc, nc):
        self.panels.append((src, kc, nc))
        return len(self.panels) - 1

    def released(self):
        last = {}
        for name in self.order:
            for i, n in enumerate(self.groups[name]["panels"]):
                last[n] = (name, i)
        out, early = {}, 0
        for n in range(len(self.panels)):
            name, i = last[n]
            g = self.groups[name]
            if i == len(g["panels"]) - 1:
                out[n] = ("tile", g["tile0"] + g["tiles"])
            else:
                early += 1
                out[n] = ("early", early)
        return out

    def group(self, name, panels, tiles, by):
        last = self.order[-1] if self.order else None
        base = {"tile0": 0, "a": 0, "d": 0}
        if last:
            g = self.groups[last]
            base = {"tile0": g["tile0"] + g["tiles"], "a": g["a"], "d": g["d"]}
        prev = self.groups[self.order[-2]] if len(self.order) > 1 else {"a": 0, "d": 0}
        g = dict(base, panels=panels, tiles=tiles, by=by, bank0=4 * (len(self.order) % 2),
                 wait_a=prev["a"], wait_d=prev["d"], before=(base["a"], base["d"]))
        g[by] += tiles
        self.groups[name] = g
        self.order.append(name)


def build(nc, a, out):
    plan = Plan()

    def kview(w):
        return w.rearrange("(k p) n -> p k n", p=P)

    def panels(w, c0, ncols=512, k=KT, k0=0):
        v = kview(w)
        return [plan.panel(v[:, x:min(x + 4, k0 + k), c0:c0 + ncols], min(4, k0 + k - x), ncols)
                for x in range(k0, k0 + k, 4)]

    w_in = a["w_in_even"][0]
    plan.group("xk", panels(a["w_xkv_2"][0], 0), 4, "a")
    plan.group("xv", panels(a["w_xkv_2"][0], 512), 2, "a")
    plan.group("f", panels(w_in, 0), 4, "a")
    plan.group("q", panels(w_in, 512), 4, "a")
    pk = panels(w_in, 1024)
    plan.group("k", pk, 4, "a")
    plan.group("kc", pk, 4, "a")
    pv = panels(w_in, 1536)
    plan.group("v", pv, 4, "a")
    plan.group("vc", pv, 2, "a")
    for j in range(2):
        plan.group(f"o{j}", panels(a["w_out_even"][0], 512 * j), 4, "d")

    MOD_AFTER = {"m0b21": "mc0", "m0b41": "mc1", "m0b61": "mc2"}

    def mlp_groups(l):
        plan.group(f"m{l}a0", panels(a["w_mlp1"][l], 0), 4, "a")
        for c in range(8):
            if c < 7:
                plan.group(f"m{l}a{c + 1}", panels(a["w_mlp1"][l], 512 * (c + 1)), 4, "a")
            for j in range(2):
                plan.group(f"m{l}b{c}{j}", panels(a["w_mlp2"][l], 512 * j, k=4, k0=4 * c), 4, "d")
                if f"m{l}b{c}{j}" in MOD_AFTER:
                    plan.group(MOD_AFTER[f"m{l}b{c}{j}"], [], 4, "d")

    mlp_groups(0)
    pp = [plan.panel(a["w_pool"][0].rearrange("g (k p) n -> p (g k) n", p=P), 8, 256)]
    plan.group("p0", pp, 4, "d")
    plan.group("p1", pp, 4, "d")
    mlp_groups(1)
    w2 = a["w_in_2"][0]
    plan.group("qa", panels(w2, 0), 4, "a")
    plan.group("kv1", panels(w2, 512), 4, "a")
    plan.group("kv2", panels(w2, 1024, 280), 3, "a")
    plan.group("qkb", panels(w2, 1304), 4, "a")
    plan.group("vb", panels(w2, 1816), 4, "a")
    plan.group("rb", panels(w2, 2328), 4, "a")
    plan.group("al", panels(w2, 2840, 128), 1, "a")
    for j in range(4):
        plan.group(f"mg{j}", panels(w2, 2856 + 512 * j), 4, "a")
    for j in range(2):
        plan.group(f"bn{j}", panels(a["w_branch_nsa_2"][0], 512 * j, k=4), 4, "d")
        plan.group(f"bg{j}", panels(a["w_branch_gla_2"][0], 512 * j, k=4), 4, "d")
    for j in range(2):
        plan.group(f"ow{j}", panels(a["w_out_2"][0], 512 * j), 4, "d")
    plan.group("xq", panels(a["w_xq_2"][0], 0), 4, "a")
    for j in range(2):
        plan.group(f"xo{j}", panels(a["w_xo_2"][0], 512 * j, k=4), 4, "d")
    FC = [4, 4, 4, 4, 4, 2]
    for c, n in enumerate(FC):
        plan.group(f"fu{c}", panels(a["w_up_2"][0], 512 * c, P * n), n, "d")
        plan.group(f"fg{c}", panels(a["w_up_2"][0], FFN + 512 * c, P * n), n, "d")
        for j in range(2):
            plan.group(f"fd{c}{j}", panels(a["w_down_2"][0], 512 * j, k=n, k0=4 * c), 4, "d")
    PAN, G = plan.panels, plan.groups
    NPAN = len(PAN)

    MOD_PARTS = 12
    MOD_FIRST = 4
    PIECES = (MOD_PARTS - MOD_FIRST) * 2

    def mod_source(c, k0, nk):
        return kview(a["w_mod"][c // MOD_PARTS])[:, k0:k0 + nk, 512 * (c % MOD_PARTS):512 * (c % MOD_PARTS) + 512]
    RELEASED = plan.released()

    with ExitStack() as ctx:
        def at(name, shape, kb, dt=F32):
            return nc.alloc_sbuf_tensor_at(name, shape, dt, offset=int(kb * 1024))

        def sem(name):
            return ctx.enter_context(nc.semaphore(name))

        B0 = 16.25
        h = at("h", [P, KT, S], B0)
        u_hi = at("u_hi", [P, KT, S], B0 + 16, F32R)
        u_lo = at("u_lo", [P, KT, S], B0 + 32, F32R)
        w_raw = [at(f"w_raw{i}", [P, PW], B0 + 48 + 8 * i) for i in range(3)]
        w_hi = [at(f"w_hi{i}", [P, PW], B0 + 72 + 8 * i, F32R) for i in range(2)]
        w_lo = [at(f"w_lo{i}", [P, PW], B0 + 88 + 8 * i, F32R) for i in range(2)]
        xk = at("xk", [P, 4, L], B0 + 104)
        xv = at("xv", [P, LT, S], B0 + 108)
        sq = at("sq", [P, 2, S], B0 + 112)
        root = at("root", [P, S], B0 + 116)
        rstd = at("rstd", [P, S], B0 + 118)
        tmp = at("tmp", [P, 2, S], B0 + 120)
        col = at("col", [P, NCOL], B0 + 124)
        ident = at("ident", [P, P], B0 + 125.25)
        ones = at("ones", [P, P], B0 + 125.75)
        halves = at("halves", [P, P], B0 + 126.25)
        modc = at("modc", [P, 2, 48, 2], B0 + 126.75)
        gcol = at("gcol", [P, 8, 8], B0 + 127.5)
        silu = at("silu", [P, KT, 2], B0 + 127.75)
        stats = at("stats", [P, 8, 32], B0 + 127.875)
        eps = at("eps", [P, 1], B0 + 128.875)
        X0 = B0 + 129
        tok_in = [at(f"tok_in{i}", [P, D], X0 + 4 * i) for i in range(4)]
        mod_raw = [at(f"mod_raw{i}", [P, PW], X0 + 16 + 8 * i) for i in range(2)]
        mod_acc = [at(f"mod_acc{i}", [P, 2, S], X0 + 66 + 4 * i) for i in range(2)]
        mod_prod = [at(f"mod_prod{i}", [P, S], X0 + 74 + 2 * i) for i in range(2)]
        uc_hi = at("uc_hi", [P, KT, L], X0 + 32, F32R)
        uc_lo = at("uc_lo", [P, KT, L], X0 + 40, F32R)
        mem_t = at("mem_t", [P, KT, L], X0 + 48)
        ctx_t = at("ctx_t", [P, KT, L], X0 + 56)
        rows = at("rows", [P, 3, P], X0 + 64)
        f_t = at("f_t", [P, 4, S], X0)
        q_t = at("q_t", [P, 4, S], X0 + 8)
        k_t = at("k_t", [P, 4, S], X0 + 16)
        kc_t = at("kc_t", [P, 4, L], X0 + 24)
        vc = at("vc", [P, LT, S], X0 + 28)
        v = at("v", [P, TT, S], X0 + 48)
        dft = at("dft", [P, 2, TT, S], X0 + 32)
        w_four = at("w_four", [P, 4, P], X0 + 56)
        dft_c = at("dft_c", [P, 2, P], X0 + 58)
        cw = at("cw", [P, 4, 2 * P], X0 + 59)
        z = [at(f"z{i}", [P, TT, 2 * P], X0 + 63 + 4 * i) for i in range(2)]
        gb = [at(f"gb{i}", [P, 14, GRID], X0 + 71 + 3.5 * i) for i in range(2)]
        near = at("near", [P, GRID], X0 + 78)
        pad = at("pad", [NH * 15, 127], X0 + 74.5)
        rpb_in = at("rpb_in", [NH * 15, 31], X0 + 75)
        p_na = [at(f"p_na{i}", [P, 768], X0 + 3 * i) for i in range(2)]
        pt_na = [at(f"pt_na{i}", [P, 6, P], X0 + 56 + 3 * i) for i in range(2)]
        o_na = at("o_na", [P, TT, S], X0 + 63)
        piece_raw = [[at(f"piece_raw{e}{i}", [P, 2, S], X0 + 32 + 8 * e + 4 * i) for i in range(2)] for e in range(2)]
        piece_acc = [[at(f"piece_acc{e}{i}", [P, S], B0 + 112 + 8 * e + 2 * i) for i in range(2)] for e in range(2)]
        piece_prod = [at(f"piece_prod{i}", [P, S], B0 + 116 + 2 * i) for i in range(2)]
        q_o = at("q_o", [P, 4, S], B0 + 24)
        a_hi = [at(f"a_hi{i}", [P, 4, S], X0 + 16 * i, F32R) for i in range(2)]
        a_lo = [at(f"a_lo{i}", [P, 4, S], X0 + 16 * i + 8, F32R) for i in range(2)]
        mod_sums = at("mod_sums", [P, MOD_PARTS, S], X0 + 32)
        mod_panels = [at(f"mod_panels{i}", [P, 4, S], X0 + 56 + 8 * i) for i in range(2)]
        up = at("up", [P, KT, S + 16], X0 + 32)
        win = [at(f"win{i}", [P, 2, S + 16], X0 + 49 + 4.25 * i) for i in range(2)]
        cnt = at("cnt", [P, 4, S], X0 + 58)
        qa_t = at("qa_t", [P, 4, S], X0)
        kcv_t = at("kcv_t", [P, 2, S], X0 + 8)
        ks_t = at("ks_t", [P, S], X0 + 12)
        kw_t = at("kw_t", [P, S], X0 + 14)
        vs = at("vs", [P, TT, P], X0 + 16)
        vw = at("vw", [P, TT, P], X0 + 18)
        qkb = at("qkb", [P, 4, S], X0 + 20)
        vb = at("vb", [P, TT, S], X0 + 28)
        rb = at("rb", [P, 4, S], X0 + 36)
        al = at("al", [P, S], X0 + 44)
        w1 = at("w1", [P, 2, 16, P], X0 + 46)
        kpos = [sq, tmp]
        gate = at("gate", [P, TT, 24], X0 + 78)
        pos_rows = at("pos_rows", [32, 2, P], B0 + 116)
        pos = at("pos", [P, 2, 32], B0 + 117)
        w2 = at("w2", [P, 2, HD], B0 + 117.25)
        ghid = at("ghid", [P, 4, 32], B0 + 118)
        kcm = at("kcm", [P, NCMP + 1], B0 + 118.5)
        vcm = at("vcm", [NCMP, 2, HD], B0 + 118.75)
        gate_b = at("gate_b", [3 * NH, 1], B0 + 119.25)
        v_t = at("v_t", [P, 2, S], X0 + 62)
        gate_t = at("gate_t", [3 * NH, S], X0 + 66)
        w_al = at("w_al", [16, 256], X0 + 73.25)
        valid = at("valid", [P, TT], X0 + 78.5)
        tab = at("tab", [P, 896 + 124], X0 + 46)
        ntab = [at("ntab0", [P, 896 + 124], B0 + 112), at("ntab1", [P, 896 + 124], B0 + 120)]
        p_nsa = [at(f"p_nsa{i}", [P, 928], X0 + 50 + 3.625 * i) for i in range(2)]
        pt_nsa = [at(f"pt_nsa{i}", [P, 8, P], X0 + 57.25 + 4 * i) for i in range(2)]
        o_nsa = at("o_nsa", [P, TT, S], X0 + 65.25)
        ks_o = at("ks_o", [P, S], X0 + 73.25)
        kw_o = at("kw_o", [P, S], X0 + 75.25)
        kcm_o = at("kcm_o", [P, NCMP + 1], X0 + 77.25)
        on_hi = at("on_hi", [P, 4, S], X0 + 50, F32R)
        on_lo = at("on_lo", [P, 4, S], X0 + 58, F32R)
        la = [at(f"la{i}", [P, 2, S], X0 + 4 * i) for i in range(2)]
        qd = at("qd", [P, 2, S], X0 + 8)
        kd = at("kd", [P, 2, S], X0 + 12)
        ks = at("ks", [P, 2, S], X0 + 16)
        ga = at("ga", [P, 2, S], B0 + 116)
        gt = at("gt", [P, 2, S], B0 + 112)
        kst = at("kst", [P, TT, 256], X0 + 46)
        att = [at(f"att{i}", [P, TT, P], X0 + 66 + 2 * i) for i in range(2)]
        st = at("st", [P, 2, NCH, P], X0 + 70)
        dec = at("dec", [P, 2, NCH], X0 + 78.375)
        gmask = at("gmask", [P, P], X0 + 44, I32)
        og_hi = at("og_hi", [P, 4, S], X0 + 20, F32R)
        og_lo = at("og_lo", [P, 4, S], X0, F32R)
        mg = [at(f"mg{i}", [P, S], X0 + (8 + 2 * i if i < 6 else 16 + 2 * i)) for i in range(16)]
        mixn = at("mixn", [P, 4, S], X0 + 66)
        xq_t = at("xq_t", [P, 4, S], X0)
        xo_hi = at("xo_hi", [P, 4, S], X0 + 8, F32R)
        xo_lo = at("xo_lo", [P, 4, S], X0 + 16, F32R)
        p_x = [at(f"p_x{i}", [P, L], X0 + 24 + i) for i in range(2)]
        pt_x = [at(f"pt_x{i}", [P, LT, P], X0 + 26 + i) for i in range(2)]
        o_x = at("o_x", [P, TT, S], X0 + 28)
        ub = at("ub", [P, 4, S], X0 + 32)
        cv = at("cv", [P, 4, S], X0 + 41)
        y = at("y", [P, KT, S], X0)
        y_out = [at(f"y_out{i}", [P, D], X0 + 16 + 4 * i) for i in range(2)]

        ps = ctx.enter_context(nc.psum_tensor("ps", [P, 8, S], F32))
        bias_pad = nc.dram_tensor("bias_pad", (NH, 15, 127), F32, kind="Internal").ap()

        tok_loaded = [sem(f"tok_loaded{i}") for i in range(4)]
        consts_loaded = sem("consts_loaded")
        rows_loaded = sem("rows_loaded")
        ones_set = sem("ones_set")
        tok_turned = sem("tok_turned")
        tok_kept = sem("tok_kept")
        rows_turned, col_ready = sem("rows_turned"), sem("col_ready")
        silu_ready = sem("silu_ready")
        mod_loaded = [sem(f"mod_loaded{i}") for i in range(2)]
        mod_added = sem("mod_added")
        mod_scaled = sem("mod_scaled")
        mod_pooled = sem("mod_pooled")
        piece_loaded = [[sem(f"piece_loaded{e}{i}") for i in range(2)] for e in range(2)]
        mod1_loaded = [sem(f"mod1_loaded{i}") for i in range(2)]
        mod1_added = sem("mod1_added")
        mod_summed = sem("mod_summed")
        mod_ready = sem("mod_ready")
        w_loaded = [sem(f"w_loaded{i}") for i in range(3)]
        w_hi_ready, w_lo_ready = sem("w_hi_ready"), sem("w_lo_ready")
        w_early = sem("w_early")
        tile_done = sem("tile_done")
        free_a, free_d = sem("free_a"), sem("free_d")
        sq_ready, sq_used = sem("sq_ready"), sem("sq_used")
        root_ready, rstd_ready = sem("root_ready"), sem("rstd_ready")
        t_ready, n_hi_ready = sem("t_ready"), sem("n_hi_ready")
        n_ready = sem("n_ready")
        act_chain, dve_chain, pool_chain = sem("act_chain"), sem("dve_chain"), sem("pool_chain")
        hn_sum, hn_root = sem("hn_sum"), sem("hn_root")
        hn_sq, qk_ready = sem("hn_sq"), sem("qk_ready")
        four_loaded, cw_done, cw_ready = sem("four_loaded"), sem("cw_done"), sem("cw_ready")
        z_done, z_ready = sem("z_done"), sem("z_ready")
        four_done, four_hi, four_kept = sem("four_done"), sem("four_hi"), sem("four_kept")
        pad_set, pad_loaded, pad_stored = sem("pad_set"), sem("pad_loaded"), sem("pad_stored")
        gb_loaded = [sem(f"gb_loaded{i}") for i in range(2)]
        gb_ready = sem("gb_ready")
        na_s, na_max, na_exp, na_t, na_pt, na_pv, na_o = [sem(f"na_{x}") for x in
                                                         ("s", "max", "exp", "t", "pt", "pv", "o")]
        ot_turned, ot_hi, ot_kept = sem("ot_turned"), sem("ot_hi"), sem("ot_kept")
        a_hi_ready, a_ready = sem("a_hi_ready"), sem("a_ready")
        cnt_loaded, pooled, pooled_hi, pooled_ready = [sem(f"pool_{x}") for x in ("cnt", "t", "hi", "ready")]
        cmp_loaded, pos_turned, kpos_ready = [sem(f"cmp_{x}") for x in ("loaded", "turned", "kpos")]
        hid_done, hid_ready, cmp_done, cmp_ready = [sem(f"cmp_{x}") for x in
                                                   ("hid", "gelu", "done", "ready")]
        gate_loaded = sem("gate_loaded")
        v_turned, v_kept = sem("v_turned"), sem("v_kept")
        keys_apart = sem("keys_apart")
        tab_loaded, tab_ready = sem("tab_loaded"), sem("tab_ready")
        ns_s, ns_max, ns_exp, ns_t, ns_pt, ns_pv, ns_o = [sem(f"ns_{x}") for x in
                                                         ("s", "max", "exp", "t", "pt", "pv", "o")]
        gla_loaded, gmask_loaded = sem("gla_loaded"), sem("gmask_loaded")
        gz_done, gz_log, gla_b, gla_e, gla_qk = [sem(f"gla_{x}") for x in ("z", "log", "b", "e", "qk")]
        kst_done, kst_ready, inc_done, st_ready = [sem(f"gla_{x}") for x in
                                                  ("kst_done", "kst", "inc", "st")]
        att_zero, att_done, att_ready, go_done, go_sq, go_root, go_t, go_hi, go_ready, go_sum = [
            sem(f"gla_{x}") for x in ("zero", "att_done", "att", "o", "sq", "root", "t", "hi", "ready", "sum")]
        mix_t, mix_hi, mix_ready = [sem(f"mix_{x}") for x in ("t", "hi", "ready")]
        xa_s, xa_max, xa_exp, xa_t, xa_pt, xa_pv, xa_o = [sem(f"xa_{x}") for x in
                                                         ("s", "max", "exp", "t", "pt", "pv", "o")]
        c_ready, c_gelu, f_hi, f_pair = [sem(f"ffn_{x}") for x in ("c", "gelu", "hi", "ready")]
        out_turned, out_kept = sem("out_turned"), sem("out_kept")
        out_stored = [sem(f"out_stored{i}") for i in range(2)]

        block = ctx.enter_context(nc.Block())

        MEM, CTX, X1, X2, Y1, Y2, MIX, XAT, FF, FIN = range(10)
        ncols = {MEM: L, CTX: L}

        def gain(n, k):
            if n in (MEM, MIX, XAT, FF, FIN):
                c0 = COL[{MEM: "ln_mem", MIX: "ln_mix", XAT: "ln_x", FF: "ln_ffn", FIN: "ln_final"}[n]]
                return col[:, c0 + k:c0 + k + 1]
            return gcol[:, n, k:k + 1]

        def shift(n, k):
            l, t0, src = {CTX: (0, 0, 1), X1: (0, 0, 0), X2: (0, 24, 0), Y1: (1, 0, 0), Y2: (1, 24, 0)}[n]
            return modc[:, l, t0 + k, src:src + 1]

        def g_mod(l, second, k):
            return modc[:, l, (40 if second else 16) + k, 0:1]

        def source(n, k):
            return {MEM: mem_t, CTX: ctx_t}.get(n, h)[:, k, :]

        def pair(n, k):
            return (uc_hi[:, k, :], uc_lo[:, k, :]) if n in (MEM, CTX) else (u_hi[:, k, :], u_lo[:, k, :])

        def group_end(name):
            return G[name]["a"], G[name]["d"]

        def raw_panel(n):
            _, kc, w = PAN[n]
            return w_raw[n % 3][:, 0:kc * w]

        def part_panel(part, n):
            _, kc, w = PAN[n]
            return part[n % 2][:, 0:kc * w]

        def after_panel(eng, n):
            kind, value = RELEASED[n]
            eng.wait_ge(tile_done if kind == "tile" else w_early, value)

        def after_groups(eng, name):
            fa, fd = group_end(name)
            if fa:
                eng.wait_ge(free_a, fa)
            if fd:
                eng.wait_ge(free_d, fd)

        NUNIT = NH * TT
        NROWDMA = 19
        LOADS = {}
        for n in range(NPAN):
            LOADS[n] = LOADS.get(n - 3, 0) + (8 if n in G["qa"]["panels"] else 1)
        SLOPES = [2.0 ** (-(i + 1)) for i in range(NH)]
        N_READY = {n: 8 * n for n in range(10)}
        PAIRED = {n: 8 * i for i, n in enumerate((MEM, CTX, X1, X2, Y2, MIX, XAT, FF))}
        RELEASER = {n: [name for name in plan.order if n in G[name]["panels"]][-1] for n in range(NPAN)}

        FIRST_K = 8 * MOD_FIRST

        def piece_part(e, x):
            return MOD_FIRST + 2 * (x // 4) + e

        def pieces_after(n):
            return range(PIECES * n // NUNIT, PIECES * (n + 1) // NUNIT)

        def columns_after(n):
            return [piece_part(e, x) for x in pieces_after(n) if x % 4 == 3 for e in range(2)] if n >= 0 else []

        def mod_tile(e, y):
            if y < FIRST_K:
                i, c, k = y // 4, y // 8, y % 8
                raw, loaded = mod_raw[i % 2][:, S * (y % 4):S * (y % 4) + S], (mod_loaded[i % 2], 16 * (i // 2 + 1))
                return raw, k, loaded, mod_acc[c % 2][:, e, :], c - 1
            y -= FIRST_K
            x, k = y // 2, y % 8
            c = piece_part(e, x)
            return (piece_raw[e][x % 2][:, y % 2, :], k, (piece_loaded[e][x % 2], 16 * (x // 2 + 1)),
                    piece_acc[e][y // 8 % 2][:, :], c - 3 if y >= 16 else 0)

        def mod_product(y):
            return (mod_prod if y < FIRST_K else piece_prod)[y % 2][:, :]

        MADE_BY = {X2: ("o0", "o1"), Y1: ("m0b70", "m0b71"), Y2: ("p0", "p1"), MIX: ("m1b70", "m1b71"),
                   XAT: ("ow0", "ow1"), FF: ("xo0", "xo1"), FIN: ("fd50", "fd51")}
        SUM_BANK = {n: 7 if G[names[1]]["bank0"] == 0 else 3 for n, names in MADE_BY.items()}
        SUM_BANK.update({MEM: 7, CTX: 7, X1: 7})

        def residual_tile(eng, n, k):
            eng.wait_ge(free_d, G[MADE_BY[n][k // 4]]["d"] - 3 + k % 4)

        def computed(eng, name):
            eng.wait_ge(tile_done, G[name]["tile0"] + G[name]["tiles"])

        @block.sync
        def _(sp):
            for dst, src in ((ident, "k_ident"), (halves, "k_halves")):
                sp.dma_start(dst[:, :], a[src]).then_inc(consts_loaded, 16)
            for t, (names, tensor) in enumerate(((ROWS0, 0), (ROWS1, 1), (ROWS2, 2))):
                r = 0
                for name, n in names:
                    if name in ("qg", "kg"):
                        src = a["q_norm_g" if name == "qg" else "k_norm_g"]
                        sp.dma_start(rows[r:r + 1, t, 0:HD], src).then_inc(rows_loaded, 16)
                        sp.dma_start(rows[r:r + 1, t, HD:P], src).then_inc(rows_loaded, 16)
                    else:
                        src = {"c": a["c"], "c_ctx": a["c_ctx"].unsqueeze(0), "norm1": a["norm1_g"],
                               "norm2": a["norm2_g"], "ln_mix": a["ln_mix_g_2"], "ln_x": a["ln_x_g_2"],
                               "ln_mem": a["ln_mem_g_2"], "ln_ffn": a["ln_ffn_g_2"],
                               "ln_final": a["ln_final_g_2"].unsqueeze(0), "pool_scale": a["pool_scale"],
                               "b_alpha": a["gla_b_alpha_2"], "gla_norm": a["gla_norm_g_2"],
                               "b_mod": a["b_mod"], "conv_w": a["conv_w_2"][0], "conv_b": a["conv_b_2"]}[name]
                        src = src.rearrange("a (b p) -> (a b) p", p=P)
                        sp.dma_start(rows[r:r + n, t, :], src).then_inc(rows_loaded, 16)
                    r += n

            def load_panel(n):
                src, kc, w = PAN[n]
                if n >= 3:
                    sp.wait_ge(w_lo_ready, n - 2)
                if n in G["qa"]["panels"]:
                    dst = raw_panel(n).rearrange("p (k m a b) -> p k m a b", k=kc, m=4, a=2)
                    for x in range(2):
                        for k in range(kc):
                            sp.dma_start(dst[:, k, :, x, :],
                                         src[:, k, 256 * x:256 * x + 256].rearrange("p (m b) -> p m b", m=4))\
                              .then_inc(w_loaded[n % 3], 16)
                    return
                sp.dma_start(raw_panel(n).rearrange("p (k n) -> p k n", k=kc), src).then_inc(w_loaded[n % 3], 16)

            def load_mod(i):
                if i >= 2:
                    sp.wait_ge(mod_added, 4 * (i - 1))
                    sp.wait_ge(mod_scaled, 4 * (i - 1))
                sp.dma_start(mod_raw[i % 2][:, :].rearrange("p (k n) -> p k n", k=4),
                             mod_source(i // 2, 4 * (i % 2), 4)).then_inc(mod_loaded[i % 2], 16)

            for i in range(8):
                if i >= 4:
                    sp.wait_ge(tok_kept, 2 * (i - 4) + 2)
                src = (a["mem_2"][0][P * i:P * i + P, :] if i < 2 else
                       a["ctx"][0][P * (i - 2):P * (i - 1), :] if i < 4 else a["x"][0][P * (i - 4):P * (i - 3), :])
                sp.dma_start(tok_in[i % 4][:, :], src).then_inc(tok_loaded[i % 4], 16)
                if i in (3, 5):
                    load_panel(i // 2 - 1)
                    load_mod(i // 2 - 1)
            load_panel(2)
            for i in range(2, 5):
                load_mod(i)
            load_panel(3)
            for i in range(5, 2 * MOD_FIRST):
                load_mod(i)
            load_panel(4)
            load_panel(5)
            last = G["vc"]["panels"][-1]
            for n in range(6, last + 1):
                load_panel(n)
            after_panel(sp, last)
            sp.dma_start(dft[:, :, :, :], a["k_dft"]).then_inc(four_loaded, 16)
            sp.dma_start(dft_c[:, :, :], a["k_dft_c"]).then_inc(four_loaded, 16)
            sp.dma_start(w_four[:, :, :], a["w_four"][0].rearrange("g c d -> c g d")).then_inc(four_loaded, 16)
            for n in range(last + 1, last + 4):
                load_panel(n)
            sp.dma_start(near[:, :], a["k_near"]).then_inc(pad_loaded, 16)
            sp.dma_start(rpb_in[:, :], a["rpb"][0].rearrange("h r c -> (h r) c")).then_inc(pad_loaded, 16)
            sp.wait_ge(pad_set, 2)
            sp.dma_start(bias_pad.rearrange("h r c -> (h r) c"), pad[:, :]).then_inc(pad_stored, 16)
            sp.wait_ge(pad_stored, 16)
            sp.wait_ge(four_kept, 4)
            per_head = PIECES // NH

            def load_bias(hh):
                for ro in range(2):
                    src = bass.AP(tensor=bias_pad.tensor, offset=hh * 15 * 127 + (1 - ro) * 127,
                                  ap=[[1, GRID], [127, 14], [1, GRID]])
                    sp.dma_start(gb[hh % 2][GRID * ro:GRID * ro + GRID, :, :], src).then_inc(gb_loaded[hh % 2], 16)

            load_bias(0)
            load_bias(1)
            for hh in range(NH):
                for x in range(per_head * hh, per_head * (hh + 1)):
                    for e in range(2):
                        if x >= 2:
                            sp.wait_ge((mod_added, mod_scaled)[e], FIRST_K + 2 * (x - 1))
                        sp.dma_start(piece_raw[e][x % 2][:, :, :], mod_source(piece_part(e, x), 2 * (x % 4), 2))\
                          .then_inc(piece_loaded[e][x % 2], 16)
                if hh + 2 < NH:
                    sp.wait_ge(na_max, 4 * (hh + 1))
                    load_bias(hh + 2)
            n0 = last + 4
            end = G["m0b71"]["panels"][-1]
            mod_after = {}
            for c in range(6):
                first, second = (G[f"m0b{c}{j}"]["panels"][0] for j in range(2))
                for j, n in enumerate((first, second, second + 1, second + 2)):
                    mod_after.setdefault(n, []).append(4 * c + j)
            for n in range(n0, end + 2):
                load_panel(n)
                for i in sorted(mod_after.get(n, [])):
                    if i >= 2:
                        sp.wait_ge(mod1_added, 4 * (i - 1))
                    sp.dma_start(mod_panels[i % 2][:, :, :], mod_source(MOD_PARTS + i // 2, 4 * (i % 2), 4))\
                      .then_inc(mod1_loaded[i % 2], 16)
            sp.wait_ge(mod1_added, 8 * MOD_PARTS)
            sp.dma_start(cnt[:, :, :], a["k_cnt"]).then_inc(cnt_loaded, 16)
            n1 = G["al"]["panels"][-1]
            second = G["qa"]["panels"][0]
            for n in range(end + 2, second):
                load_panel(n)
            for n in range(second, n1 + 1):
                load_panel(n)
                if n == G["kv1"]["panels"][0]:
                    sp.wait_ge(n_ready, 8 * (MIX + 1))
                    sp.dma_start(gate_b[:, :], a["nsa_gate_b_2"].rearrange("a b -> b a")).then_inc(gate_loaded, 16)
                if n == G["vb"]["panels"][0]:
                    for x, c in enumerate("kv"):
                        for half in range(2):
                            r = slice(HD * half, HD * half + HD)
                            sp.dma_start(w1[r, x, :, :],
                                         a[f"cmp_w1_{c}_2"][0].rearrange("(g l d) n -> g d l n", g=2, d=HD)[half])\
                              .then_inc(cmp_loaded, 16)
                            sp.dma_start(pos_rows[:, x, r], a[f"cmp_pos_{c}_2"][0]).then_inc(cmp_loaded, 16)
                        sp.dma_start(w2[:, x, :], a[f"cmp_w2_{c}_2"][0]).then_inc(cmp_loaded, 16)
            for n in range(n1 + 1, n1 + 4):
                load_panel(n)
            sp.wait_ge(hid_done, 4)
            sp.dma_start(tab[:, :], a["k_tab"]).then_inc(tab_loaded, 16)
            sp.dma_start(valid[:, :], a["k_valid"]).then_inc(tab_loaded, 16)
            sp.wait_ge(ns_s, NUNIT)
            sp.dma_start(w_al[:, :], a["gla_w_alpha2_2"][0]).then_inc(gla_loaded, 16)
            sp.wait_ge(gz_done, 1)
            sp.dma_start(gmask[:, :], a["k_gla_mask"]).then_inc(gmask_loaded, 16)
            for n in range(n1 + 4, NPAN):
                load_panel(n)
            for i in range(TT):
                sp.wait_ge(out_kept, 2 * i + 2)
                sp.dma_start(out[0][P * i:P * i + P, :], y_out[i % 2][:, :]).then_inc(out_stored[i % 2], 16)
            for stored in out_stored:
                sp.wait_ge(stored, 16 * TT // 2)

        @block.tensor
        def _(pe):
            def norm_sum(n, first=0, last=KT):
                t = ncols.get(n, S)
                for k in range(first, last):
                    pe.wait_ge(sq_ready, 8 * n + k + 1)
                    nc.tensor.matmul(ps[:, SUM_BANK[n], 0:t], ones[:, :], sq[:, k % 2, 0:t], start=(k == 0),
                                     stop=(k == KT - 1)).then_inc(sq_used, 1)

            def early_sums(n):
                after_groups(pe, MADE_BY[n][0])
                norm_sum(n, 0, KT // 2)

            def gemm(name, products, ready=None, norm_next=None):
                g = G[name]
                if g["wait_a"]:
                    pe.wait_ge(free_a, g["wait_a"])
                if g["wait_d"]:
                    pe.wait_ge(free_d, g["wait_d"])
                for i, n in enumerate(g["panels"]):
                    _, kc, w = PAN[n]
                    pe.wait_ge(w_lo_ready, n + 1)
                    hi = part_panel(w_hi, n).rearrange("p (k n) -> p k n", k=kc)
                    lo = part_panel(w_lo, n).rearrange("p (k n) -> p k n", k=kc)
                    kl = 4 * (len(g["panels"]) - 1) + PAN[g["panels"][-1]][1]
                    for m in range(g["tiles"]):
                        for kk in range(kc):
                            k = 4 * i + kk
                            if ready and m == 0:
                                ready(k)
                            todo = products(m, k, hi[:, kk, :], lo[:, kk, :], g["bank0"])
                            for j, (dst, l, r) in enumerate(todo):
                                ins = nc.tensor.matmul(dst, l, r, start=(k == 0 and j == 0),
                                                       stop=(k == kl - 1 and j >= len(todo) - 3),
                                                       skip_group_check=True)
                        if i == len(g["panels"]) - 1:
                            ins.then_inc(tile_done, 1)
                            if m == 1 and norm_next is not None:
                                early_sums(norm_next)
                    if RELEASED[n][0] == "early" and name == RELEASER[n]:
                        ins.then_inc(w_early, 1)

            def three_w(dst, whi, wlo, xhi, xlo):
                return [(dst, whi, xhi), (dst, whi, xlo), (dst, wlo, xhi)]

            def three_x(dst, whi, wlo, xhi, xlo):
                return [(dst, xhi, whi), (dst, xhi, wlo), (dst, xlo, whi)]

            def by_feature(x, t=S):
                def products(m, k, hi, lo, b):
                    c = slice(P * m, P * m + P)
                    return three_w(ps[:, b + m, 0:t], hi[:, c], lo[:, c], *x(k))
                return products

            def by_token(x):
                def products(m, k, hi, lo, b):
                    xh, xl = x(k)
                    c = slice(P * m, P * m + P)
                    return three_x(ps[:, b + m, :], hi, lo, xh[:, c], xl[:, c])
                return products

            def u(k):
                return u_hi[:, k, :], u_lo[:, k, :]

            def uc(k):
                return uc_hi[:, k, :], uc_lo[:, k, :]

            def when_normed(n):
                return lambda k: pe.wait_ge(n_ready, N_READY[n] + k + 1)

            def mod_columns(c):
                if c < MOD_FIRST:
                    for added in (mod_added, mod_pooled):
                        pe.wait_ge(added, 8 * c + 8)
                    bank, t0, sums = 6, 8 * c, [mod_acc[c % 2][:, 0, :], mod_acc[c % 2][:, 1, :]]
                else:
                    e, j = (c - MOD_FIRST) % 2, (c - MOD_FIRST) // 2
                    pe.wait_ge((mod_added, mod_pooled)[e], FIRST_K + 8 * j + 8)
                    bank, t0, sums = 7, 4 * (c - MOD_FIRST), [piece_acc[e][j % 2][:, :]]
                for m in range(4):
                    for x, acc in enumerate(sums):
                        t = t0 + len(sums) * m + x
                        ins = nc.tensor.matmul(ps[:, bank, t:t + 1], acc[:, P * m:P * m + P], ones[:, 0:1],
                                               start=True, stop=True)
                ins.then_inc(mod_summed, 1)

            pe.wait_ge(consts_loaded, 32)
            for i in range(8):
                pe.wait_ge(tok_loaded[i % 4], 16 * (i // 4 + 1))
                for half in range(2):
                    n = 2 * i + half
                    if n >= 4:
                        pe.wait_ge(tok_kept, n - 3)
                    for j in range(4):
                        k = 4 * half + j
                        ins = nc.tensor.transpose(ps[:, n % 4, P * j:P * j + P], tok_in[i % 4][:, P * k:P * k + P],
                                                  ident[:, :])
                    ins.then_inc(tok_turned, 1)
                if i == 1:
                    pe.wait_ge(rows_loaded, 16 * NROWDMA)
                    at_ = 0
                    for t, rr in enumerate((ROWS0, ROWS1, ROWS2)):
                        r = sum(n for _, n in rr)
                        ins = nc.tensor.transpose(ps[:, 4, at_:at_ + r], rows[0:r, t, :], ident[0:r, 0:r])
                        at_ += r
                    ins.then_inc(rows_turned, 1)
                    pe.wait_ge(ones_set, 1)
            norm_sum(MEM)
            pe.wait_ge(tok_kept, 16)
            pe.wait_ge(col_ready, 1)
            gemm("xk", by_feature(uc, L), when_normed(MEM))
            mod_columns(0)
            mod_columns(1)
            gemm("xv", by_token(uc))
            mod_columns(2)
            mod_columns(3)
            norm_sum(CTX)
            pe.wait_ge(root_ready, CTX + 1)
            norm_sum(X1)
            pe.wait_ge(root_ready, X1 + 1)
            gemm("f", by_feature(u), when_normed(X1))
            gemm("q", by_feature(u))
            gemm("k", by_feature(u))
            gemm("kc", by_feature(uc, L))
            gemm("v", by_token(u))
            gemm("vc", by_token(uc))

            def head_sum(n):
                pe.wait_ge(hn_sq, n + 1)
                if n >= 2:
                    pe.wait_ge(hn_root, n - 1)
                nc.tensor.matmul(ps[:, 6 + n % 2, :], halves[:, :], sq[:, n % 2, :], start=True, stop=True)\
                  .then_inc(hn_sum, 1)

            after_groups(pe, "vc")
            head_sum(0)
            head_sum(1)
            pe.wait_ge(four_loaded, 48)
            for g in range(4):
                for x in range(2):
                    ins = nc.tensor.matmul(ps[:, g // 2, 256 * (g % 2) + P * x:256 * (g % 2) + P * x + P],
                                           dft_c[:, x, :], w_four[:, g, :], start=True, stop=True)
            ins.then_inc(cw_done, 1)
            pe.wait_ge(cw_ready, 1)
            for g in range(4):
                if g >= 1:
                    pe.wait_ge(z_ready, 2 * g)
                for m in range(TT):
                    ins = nc.tensor.matmul(ps[:, 2 + m // 2, 256 * (m % 2):256 * (m % 2) + 256],
                                           f_t[:, g, P * m:P * m + P], cw[:, g, :], start=True, stop=True)
                    if m % 2:
                        ins.then_inc(z_done, 1)
                head_sum(2 * g + 2)
                head_sum(2 * g + 3)
                pe.wait_ge(z_ready, 2 * g + 2)
                if g >= 2:
                    pe.wait_ge(four_kept, g - 1)
                for x in range(2):
                    for m in range(TT):
                        ins = nc.tensor.matmul(ps[:, 4 + g % 2, :], z[g % 2][:, m, P * x:P * x + P],
                                               dft[:, x, m, :], start=(x == 0 and m == 0), stop=(x == 1 and m == 3))
                ins.then_inc(four_done, 1)

            pe.wait_ge(qk_ready, 10)
            pe.wait_ge(four_kept, 4)

            def na_scores(n):
                hh, i = n // TT, n % TT
                b = 2 * (n % 2)
                if n >= 2:
                    pe.wait_ge(na_exp, n - 1)
                q = (q_t, q_o)[hh % 2][:, hh // 2, P * i:P * i + P]
                nc.tensor.matmul(ps[:, b, :], q, k_t[:, hh // 2, :], start=True, stop=True)
                nc.tensor.matmul(ps[:, b + 1, 0:L], q, kc_t[:, hh // 2, :], start=True, stop=True).then_inc(na_s, 1)

            def na_turn(n):
                pe.wait_ge(na_exp, n + 1)
                if n >= 1:
                    pe.wait_ge(na_pt, n)
                for j in range(6):
                    ins = nc.tensor.transpose(ps[:, 4 + j // 4, P * (j % 4):P * (j % 4) + P],
                                              p_na[n % 2][:, P * j:P * j + P], ident[:, :])
                ins.then_inc(na_t, 1)

            def na_values(n):
                hh = n // TT
                pe.wait_ge(na_pt, n + 1)
                if n >= 2:
                    pe.wait_ge(na_o, n - 1)
                for j in range(6):
                    val = v[:, j, HD * hh:HD * hh + HD] if j < TT else vc[:, j - TT, HD * hh:HD * hh + HD]
                    ins = nc.tensor.matmul(ps[:, 6 + n % 2, 256:256 + HD], pt_na[n % 2][:, j, :], val,
                                           start=(j == 0), stop=(j == 5))
                ins.then_inc(na_pv, 1)

            na_scores(0)
            na_scores(1)
            for n in range(NUNIT):
                if n + 2 < NUNIT:
                    na_scores(n + 2)
                na_turn(n)
                for c in columns_after(n - 1):
                    read = n - 3 + n % 2
                    if read > 0:
                        pe.wait_ge(na_o, read + 1)
                    mod_columns(c)
                if n:
                    na_values(n - 1)
            na_values(NUNIT - 1)
            pe.wait_ge(na_o, NUNIT)
            for c in columns_after(NUNIT - 1):
                mod_columns(c)

            def turn_out(o):
                for j in range(4):
                    for i in range(TT):
                        ins = nc.tensor.transpose(ps[:, j, P * i:P * i + P], o[:, i, P * j:P * j + P], ident[:, :])
                    ins.then_inc(ot_turned, 1)

            pe.wait_ge(na_o, NUNIT)
            turn_out(o_na)
            pe.wait_ge(mod_ready, 2)
            pe.wait_ge(ot_kept, 4)
            gemm("o0", by_feature(u))
            gemm("o1", by_feature(u), norm_next=X2)

            def turn_mod(name):
                g, x = G[name], int(name[2])
                if g["wait_a"]:
                    pe.wait_ge(free_a, g["wait_a"])
                pe.wait_ge(free_d, g["wait_d"])
                pe.wait_ge(mod1_added, 32 * (x + 1))
                for m in range(4):
                    for t in range(4):
                        ins = nc.tensor.transpose(ps[:, g["bank0"] + m, P * t:P * t + P],
                                                  mod_sums[:, 4 * x + m, P * t:P * t + P], ident[:, :])
                    ins.then_inc(tile_done, 1)

            def mlp(l, n):
                if l == 0:
                    norm_sum(n, KT // 2)
                else:
                    after_groups(pe, MADE_BY[n][0])
                    norm_sum(n)
                pe.wait_ge(root_ready, n + 1)

                def when_hidden(c):
                    return lambda k: pe.wait_ge(a_ready, 32 * l + 4 * c + k + 1)

                gemm(f"m{l}a0", by_feature(u), when_normed(n))
                for c in range(8):
                    if c < 7:
                        gemm(f"m{l}a{c + 1}", by_feature(u))
                    x = lambda k, c=c: (a_hi[c % 2][:, k, :], a_lo[c % 2][:, k, :])
                    gemm(f"m{l}b{c}0", by_feature(x), when_hidden(c))
                    gemm(f"m{l}b{c}1", by_feature(x), norm_next=(Y1, MIX)[l] if c == 7 else None)
                    if f"m{l}b{c}1" in MOD_AFTER:
                        turn_mod(MOD_AFTER[f"m{l}b{c}1"])
            mlp(0, X2)
            norm_sum(Y1, KT // 2)
            pe.wait_ge(root_ready, Y1 + 1)
            n = G["p0"]["panels"][0]
            hi = part_panel(w_hi, n).rearrange("p (k n) -> p k n", k=8)
            lo = part_panel(w_lo, n).rearrange("p (k n) -> p k n", k=8)
            pe.wait_ge(w_lo_ready, n + 1)
            for j in range(2):
                for m in range(4):
                    g = 2 * j + m // 2
                    c = slice(P * (m % 2), P * (m % 2) + P)
                    pe.wait_ge(pooled_ready, g + 1)
                    for kk in range(2):
                        todo = three_w(ps[:, G[f"p{j}"]["bank0"] + m, :], hi[:, 2 * g + kk, c], lo[:, 2 * g + kk, c],
                                       *u(2 * g + kk))
                        for x, (dst, l_, r_) in enumerate(todo):
                            ins = nc.tensor.matmul(dst, l_, r_, start=(kk == 0 and x == 0), stop=(kk == 1 and x == 2))
                    ins.then_inc(tile_done, 1)
            mlp(1, Y2)

            norm_sum(MIX, KT // 2)
            pe.wait_ge(root_ready, MIX + 1)

            def window_and_gates(m, k, hi, lo, b):
                w = P if m < 2 else 3 * NH
                c = slice(P * m, P * m + w)
                return three_w(ps[0:w, b + m, :], hi[:, c], lo[:, c], *u(k))

            gemm("qa", by_feature(u), when_normed(MIX))
            gemm("kv1", by_feature(u))
            gemm("kv2", window_and_gates)
            gemm("qkb", by_feature(u))
            gemm("vb", by_token(u))
            gemm("rb", by_feature(u))
            gemm("al", by_feature(u))

            after_groups(pe, "al")
            pe.wait_ge(cmp_loaded, 16 * 10)
            for x in range(2):
                ins = nc.tensor.transpose(ps[:, 6, 32 * x:32 * x + 32], pos_rows[:, x, :], ident[0:32, 0:32])
            ins.then_inc(pos_turned, 1)
            for x in range(2):
                for i in range(TT):
                    nc.tensor.transpose(ps[:, (7, 4)[x], P * i:P * i + P], v_t[:, x, P * i:P * i + P], ident[:, :])
            for i in range(TT):
                ins = nc.tensor.transpose(ps[:, 5, 24 * i:24 * i + 24], gate_t[:, P * i:P * i + P],
                                          ident[0:3 * NH, 0:3 * NH])
            ins.then_inc(v_turned, 1)
            for x in range(2):
                for hh in range(2):
                    pe.wait_ge(kpos_ready, 2 * x + hh + 1)
                    for l in range(16):
                        ins = nc.tensor.matmul(ps[:, 2 * x + hh, 0:NCMP], w1[:, x, l, :],
                                               kpos[x][:, hh, l:l + 16 * (NCMP - 1) + 1:16],
                                               start=(l == 0), stop=(l == 15))
                    ins.then_inc(hid_done, 1)
            pe.wait_ge(hid_ready, 4)
            pe.wait_ge(v_kept, 1)
            for half in range(2):
                r = slice(HD * half, HD * half + HD)
                nc.tensor.matmul(ps[r, 4, 0:NCMP], w2[:, 0, :], ghid[:, half, 0:NCMP], start=True, stop=True)
                ins = nc.tensor.matmul(ps[0:NCMP, 5, r], ghid[:, 2 + half, 0:NCMP], w2[:, 1, :],
                                       start=True, stop=True)
            ins.then_inc(cmp_done, 1)

            pe.wait_ge(cmp_ready, 1)
            pe.wait_ge(keys_apart, 6)

            def ns_scores(n):
                hh, i = n // TT, n % TT
                kv = hh // 4
                b = 2 * (n % 2)
                if n >= 2:
                    pe.wait_ge(ns_max, n - 1)
                q = qa_t[:, hh % 4, P * i:P * i + P]
                k_s, k_w, k_c = ((ks_t, kw_t, kcm), (ks_o, kw_o, kcm_o))[kv]
                ws, ww = P * (i + 1), P * min(i + 1, 3)
                nc.tensor.matmul(ps[:, b, 0:ws], q, k_s[:, 0:ws], start=True, stop=True)
                nc.tensor.matmul(ps[:, b + 1, 0:ww], q, k_w[:, ws - ww:ws], start=True, stop=True)
                nc.tensor.matmul(ps[:, b + 1, 384:384 + NCMP], q, k_c[:, 0:NCMP], start=True, stop=True)\
                  .then_inc(ns_s, 1)

            def ns_turn(n):
                i = n % TT
                pe.wait_ge(ns_exp, n + 1)
                if n >= 1:
                    pe.wait_ge(ns_pt, n)
                pr = p_nsa[n % 2]
                for j in range(i + 1):
                    nc.tensor.transpose(ps[:, 4, P * j:P * j + P], pr[:, P * j:P * j + P], ident[:, :])
                for j in range(min(i + 1, 3)):
                    nc.tensor.transpose(ps[:, 5, P * j:P * j + P], pr[:, S + P * j:S + P * j + P], ident[:, :])
                nc.tensor.transpose(ps[0:NCMP, 5, 384:512], pr[:, 896:896 + NCMP], ident[:, :]).then_inc(ns_t, 1)

            def ns_values(n):
                hh, i = n // TT, n % TT
                c = slice(HD * (hh // 4), HD * (hh // 4) + HD)
                b = 6 + n % 2
                pt = pt_nsa[n % 2]
                pe.wait_ge(ns_pt, n + 1)
                if n >= 2:
                    pe.wait_ge(ns_o, n - 1)
                for j in range(i + 1):
                    nc.tensor.matmul(ps[:, b, 0:HD], pt[:, j, :], vs[:, j, c], start=(j == 0), stop=(j == i))
                nw = min(i + 1, 3)
                for j in range(nw):
                    nc.tensor.matmul(ps[:, b, HD:2 * HD], pt[:, 4 + j, :], vw[:, i + 1 - nw + j, c],
                                     start=(j == 0), stop=(j == nw - 1))
                nc.tensor.matmul(ps[:, b, 2 * HD:3 * HD], pt[0:NCMP, 7, :], vcm[:, hh // 4, :],
                                 start=True, stop=True).then_inc(ns_pv, 1)

            ns_scores(0)
            ns_scores(1)
            for n in range(NUNIT):
                if n + 2 < NUNIT:
                    ns_scores(n + 2)
                ns_turn(n)
                if n:
                    ns_values(n - 1)
            ns_values(NUNIT - 1)
            pe.wait_ge(ns_o, NUNIT)
            turn_out(o_nsa)

            pe.wait_ge(gla_loaded, 16)
            pe.wait_ge(ot_kept, 8)
            for p in range(2):
                ins = nc.tensor.matmul(ps[:, p, :], w_al[:, P * p:P * p + P], al[0:16, :], start=True, stop=True)
            ins.then_inc(gz_done, 1)
            pe.wait_ge(gla_qk, 3)
            for i in range(TT):
                for p in range(2):
                    ins = nc.tensor.transpose(ps[:, 2 + i // 2, 256 * (i % 2) + P * p:256 * (i % 2) + P * p + P],
                                              ks[:, p, P * i:P * i + P], ident[:, :])
            ins.then_inc(kst_done, 1)
            pe.wait_ge(kst_ready, 1)

            def gla_head(hh):
                p, r = hh // 2, slice(HD * (hh % 2), HD * (hh % 2) + HD)
                e = slice(P * hh, P * hh + P)
                if hh == 0:
                    pe.wait_ge(st_ready, 1)
                pe.wait_ge(att_ready, hh + 1)
                if hh >= 2:
                    pe.wait_ge(go_t, hh - 1)
                o = ps[:, 6 + hh % 2, :]
                for i in range(TT):
                    nc.tensor.matmul(o[:, P * i:P * i + P], vb[:, i, e], att[hh % 2][:, i, :], start=(i == 0),
                                     stop=False, skip_group_check=True)
                for c in range(1, NCH):
                    t = slice(CHUNK * c, CHUNK * c + CHUNK)
                    ins = nc.tensor.matmul(o[:, t], st[r, p, c, :], qd[r, p, t], start=False, stop=True,
                                           skip_group_check=True)
                ins.then_inc(go_done, 1)
                pe.wait_ge(go_sq, hh + 1)
                if hh >= 2:
                    pe.wait_ge(go_root, hh - 1)
                nc.tensor.matmul(ps[:, hh % 2, :], ones[:, :], gt[:, hh % 2, :], start=True, stop=True)\
                  .then_inc(go_sum, 1)

            for c in range(NCH - 1):
                for hh in range(4):
                    p, half = hh // 2, hh % 2
                    r = slice(CHUNK * (c % 2), CHUNK * (c % 2) + CHUNK)
                    ins = nc.tensor.matmul(ps[HD * half:HD * half + HD, 2 * p + c % 2, P * (c // 2):P * (c // 2) + P],
                                           kst[r, c // 2, HD * hh:HD * hh + HD], vb[r, c // 2, P * hh:P * hh + P],
                                           start=True, stop=True)
            ins.then_inc(inc_done, 1)
            for hh in range(4):
                p, r = hh // 2, slice(HD * (hh % 2), HD * (hh % 2) + HD)
                if hh == 0:
                    pe.wait_ge(gla_qk, 3)
                if hh >= 2:
                    pe.wait_ge(att_ready, hh - 1)
                for i in range(TT):
                    ins = nc.tensor.matmul(ps[:, 4 + hh % 2, P * i:P * i + P], kd[r, p, P * i:P * i + P],
                                           qd[r, p, P * i:P * i + P], start=True, stop=True)
                ins.then_inc(att_done, 1)
                if hh >= 1:
                    gla_head(hh - 1)
            gla_head(3)
            pe.wait_ge(go_ready, 4)

            for j in range(4):
                gemm(f"mg{j}", by_feature(u))
            for j in range(2):
                gemm(f"bn{j}", by_feature(lambda k: (on_hi[:, k, :], on_lo[:, k, :])))
                gemm(f"bg{j}", by_feature(lambda k: (og_hi[:, k, :], og_lo[:, k, :])))
            for j in range(2):
                gemm(f"ow{j}", by_feature(u), (lambda k: pe.wait_ge(mix_ready, k + 1)) if j == 0 else None,
                     norm_next=XAT if j == 1 else None)

            norm_sum(XAT, KT // 2)
            pe.wait_ge(root_ready, XAT + 1)
            gemm("xq", by_feature(u), when_normed(XAT))
            after_groups(pe, "xq")

            def xa_scores(n):
                hh, i = n // TT, n % TT
                if n >= 2:
                    pe.wait_ge(xa_exp, n - 1)
                nc.tensor.matmul(ps[:, n % 2, 0:L], xq_t[:, hh, P * i:P * i + P], xk[:, hh, :],
                                 start=True, stop=True).then_inc(xa_s, 1)

            def xa_turn(n):
                pe.wait_ge(xa_exp, n + 1)
                if n >= 2:
                    pe.wait_ge(xa_pt, n - 1)
                for j in range(LT):
                    ins = nc.tensor.transpose(ps[:, 2 + n % 2, P * j:P * j + P], p_x[n % 2][:, P * j:P * j + P],
                                              ident[:, :])
                ins.then_inc(xa_t, 1)

            def xa_values(n):
                hh = n // TT
                pe.wait_ge(xa_pt, n + 1)
                if n >= 2:
                    pe.wait_ge(xa_o, n - 1)
                for j in range(LT):
                    ins = nc.tensor.matmul(ps[:, 4 + n % 2, 0:P], pt_x[n % 2][:, j, :], xv[:, j, P * hh:P * hh + P],
                                           start=(j == 0), stop=(j == LT - 1))
                ins.then_inc(xa_pv, 1)

            xa_scores(0)
            xa_scores(1)
            for n in range(4 * TT):
                if n + 2 < 4 * TT:
                    xa_scores(n + 2)
                xa_turn(n)
                if n:
                    xa_values(n - 1)
            xa_values(4 * TT - 1)
            pe.wait_ge(xa_o, 4 * TT)
            turn_out(o_x)
            pe.wait_ge(ot_kept, 12)
            for j in range(2):
                gemm(f"xo{j}", by_feature(lambda k: (xo_hi[:, k, :], xo_lo[:, k, :])),
                     norm_next=FF if j == 1 else None)

            norm_sum(FF, KT // 2)
            pe.wait_ge(root_ready, FF + 1)
            for c, nt in enumerate(FC):
                gemm(f"fu{c}", by_feature(u), when_normed(FF) if c == 0 else None)
                gemm(f"fg{c}", by_feature(u))
                for j in range(2):
                    gemm(f"fd{c}{j}", by_feature(lambda k, c=c: (a_hi[c % 2][:, k, :], a_lo[c % 2][:, k, :])),
                         (lambda k, c=c: pe.wait_ge(f_pair, 4 * c + k + 1)) if j == 0 else None,
                         norm_next=FIN if (c, j) == (len(FC) - 1, 1) else None)
            norm_sum(FIN, KT // 2)
            pe.wait_ge(n_ready, N_READY[FIN] + 8)
            after_groups(pe, "fd51")
            for n in range(2 * TT):
                i, half = n // 2, n % 2
                if n >= 4:
                    pe.wait_ge(out_kept, n - 3)
                for j in range(4):
                    ins = nc.tensor.transpose(ps[:, n % 4, P * j:P * j + P], y[:, 4 * half + j, P * i:P * i + P],
                                              ident[:, :])
                ins.then_inc(out_turned, 1)

        @block.scalar
        def _(act):
            chain = [0]

            def link(ins):
                chain[0] += 1
                ins.then_inc(act_chain, 1)
                act.wait_ge(act_chain, chain[0])

            def split(n):
                if n >= NPAN:
                    return
                act.wait_ge(w_loaded[n % 3], 16 * LOADS[n])
                if n >= 2:
                    after_panel(act, n - 2)
                nc.scalar.copy(part_panel(w_hi, n), raw_panel(n)).then_inc(w_hi_ready, 1)

            after_root = []

            def squares(n, first=0, last=KT, ready=None):
                t = ncols.get(n, S)
                for k in range(first, last):
                    if ready:
                        ready(k)
                    else:
                        residual_tile(act, n, k)
                    if n or k >= 2:
                        act.wait_ge(sq_used, 8 * n + k - 1)
                    nc.scalar.activation(sq[:, k % 2, 0:t], source(n, k), ACT.Square).then_inc(sq_ready, 1)

            def group(name, evacuate=None, norm_next=None):
                g = G[name]
                for i, n in enumerate(g["panels"]):
                    if i == len(g["panels"]) - 1 and norm_next is not None:
                        squares(norm_next, 0, KT // 2)
                    if i == len(g["panels"]) - 1 and evacuate:
                        for m in range(g["tiles"]):
                            if g["by"] == "a":
                                act.wait_ge(tile_done, g["tile0"] + m + 1)
                            evacuate(m, ps[:, g["bank0"] + m, :])
                    if RELEASER[n] == name:
                        if i == len(g["panels"]) - 1 and norm_next is not None:
                            after_root.append(n + 2)
                        else:
                            split(n + 2)

            def copy_to(dst, t=S, scale=None):
                def evacuate(m, src):
                    if scale is None:
                        nc.scalar.copy(dst(m), src[:, 0:t]).then_inc(free_a, 1)
                    else:
                        nc.scalar.mul(dst(m), src[:, 0:t], scale).then_inc(free_a, 1)
                return evacuate

            def norm(n, free=None, first=KT // 2, ready=None):
                t = ncols.get(n, S)
                squares(n, first, KT, ready)
                act.wait_ge(sq_used, 8 * n + 8)
                if n:
                    act.wait_ge(rstd_ready, n)
                nc.scalar.activation(root[:, 0:t], ps[:, SUM_BANK[n], 0:t], ACT.Sqrt, bias=eps[:, :], scale=1.0 / D)\
                  .then_inc(root_ready, 1)
                while after_root:
                    split(after_root.pop())
                if n not in PAIRED:
                    return
                if free:
                    computed(act, free)
                for k in range(KT):
                    act.wait_ge(t_ready, PAIRED[n] + k + 1)
                    if n in (MEM, MIX, XAT, FF):
                        ins = nc.scalar.copy(pair(n, k)[0], tmp[:, k % 2, 0:t])
                    else:
                        ins = nc.scalar.activation(pair(n, k)[0], tmp[:, k % 2, 0:t], ACT.Identity, bias=shift(n, k))
                    ins.then_inc(n_hi_ready, 1)

            def scale_mod(y):
                w, k, loaded, acc, summed = mod_tile(1, y)
                act.wait_ge(*loaded)
                if k == 0 and summed > 0:
                    act.wait_ge(mod_summed, summed)
                if y >= 2:
                    act.wait_ge(mod_pooled, y - 1)
                vector = 1 if y < FIRST_K else 0
                nc.scalar.mul(acc if k == 0 else mod_product(y), w, silu[:, k, vector:vector + 1])\
                  .then_inc(mod_scaled, 1)

            act.wait_ge(ones_set, 1)
            act.wait_ge(col_ready, 1)
            for i, name in enumerate(("c", "c_ctx")):
                nc.scalar.activation(silu[:, :, i], col[:, COL[name]:COL[name] + KT], ACT.Silu)\
                  .then_inc(silu_ready, 1)
            split(0)
            split(1)
            norm(MEM, None, 0, lambda k: act.wait_ge(tok_kept, 4))
            act.wait_ge(silu_ready, 2)
            for mk in range(FIRST_K // 2):
                scale_mod(mk)
            group("xk", copy_to(lambda m: xk[:, m, :], L))
            for mk in range(FIRST_K // 2, FIRST_K):
                scale_mod(mk)
            group("xv", copy_to(lambda m: xv[:, m, :]))
            norm(CTX, "xv", 0, lambda k: act.wait_ge(tok_kept, 8))
            norm(X1, None, 0, lambda k: act.wait_ge(tok_kept, 16))
            group("f", copy_to(lambda m: f_t[:, m, :]))
            group("q", copy_to(lambda m: q_t[:, m, :]))
            group("k", copy_to(lambda m: k_t[:, m, :]))
            group("kc", copy_to(lambda m: kc_t[:, m, :], L))
            group("v", copy_to(lambda m: v[:, m, :]))
            group("vc", copy_to(lambda m: vc[:, m, :]))

            act.wait_ge(free_a, G["vc"]["a"])

            def head_square(n):
                src = q_t[:, n, :] if n < 4 else k_t[:, n - 4, :] if n < 8 else kc_t[:, 2 * n - 16:2 * n - 14, :]
                if n >= 2:
                    act.wait_ge(hn_sum, n - 1)
                dst = sq[:, n % 2, :]
                if n >= 8:
                    dst = dst.rearrange("p (a b) -> p a b", a=2)
                nc.scalar.activation(dst, src, ACT.Square).then_inc(hn_sq, 1)

            def head_root(n):
                act.wait_ge(hn_sum, n + 1)
                if n >= 2:
                    act.wait_ge(qk_ready, n - 1)
                nc.scalar.activation(ga[:, n % 2, :], ps[:, 6 + n % 2, :], ACT.Sqrt, bias=eps[:, :], scale=1.0 / HD)\
                  .then_inc(hn_root, 1)

            def fourier_out(g):
                act.wait_ge(four_done, g + 1)
                nc.scalar.copy(u_hi[:, g, :], ps[:, 4 + g % 2, :]).then_inc(four_hi, 1)

            for n in range(2):
                head_square(n)
                head_root(n)
            for g in range(4):
                for x in range(2):
                    act.wait_ge(z_done, 2 * g + x + 1)
                    if g >= 2:
                        act.wait_ge(four_done, g - 1)
                    nc.scalar.copy(z[g % 2][:, 2 * x:2 * x + 2, :],
                                   ps[:, 2 + x, :].rearrange("p (a b) -> p a b", a=2)).then_inc(z_ready, 1)
                for n in range(2 * g + 2, 2 * g + 4):
                    head_square(n)
                    head_root(n)
                if g:
                    fourier_out(g - 1)
            fourier_out(3)

            def na_exp_of(n):
                act.wait_ge(na_max, n + 1)
                nc.scalar.activation(p_na[n % 2][:, 0:S], p_na[n % 2][:, 0:S], ACT.Exp, bias=stats[:, 4, n:n + 1],
                                     accum_out=stats[:, 2, n:n + 1])
                nc.scalar.activation(p_na[n % 2][:, S:S + L], ps[:, 2 * (n % 2) + 1, 0:L], ACT.Exp,
                                     bias=stats[:, 4, n:n + 1], accum_out=stats[:, 3, n:n + 1]).then_inc(na_exp, 1)

            def na_keep(n):
                act.wait_ge(na_t, n + 1)
                if n >= 2:
                    act.wait_ge(na_pv, n - 1)
                nc.scalar.copy(pt_na[n % 2][:, :, :].rearrange("p a b -> p (a b)"),
                               ps[:, 4:6, :].rearrange("p a b -> p (a b)")[:, 0:768]).then_inc(na_pt, 1)

            act.wait_ge(four_kept, 4)
            act.wait_ge(z_ready, 8)
            act.wait_ge(qk_ready, 10)
            na_exp_of(0)
            for n in range(NUNIT):
                if n + 1 < NUNIT:
                    na_exp_of(n + 1)
                na_keep(n)
                for x in pieces_after(n):
                    for mk in (2 * x, 2 * x + 1):
                        scale_mod(FIRST_K + mk)

            def turned_hi(which, dst, free):
                if free:
                    computed(act, free)
                for j in range(4):
                    act.wait_ge(ot_turned, 4 * which + j + 1)
                    nc.scalar.copy(dst(j), ps[:, j, :]).then_inc(ot_hi, 1)

            turned_hi(0, lambda j: u_hi[:, 4 + j, :], None)
            group("o0")
            group("o1", norm_next=X2)

            def mlp(l, n):
                prev = "o1" if l == 0 else "p1"
                norm(n, prev, KT // 2 if l == 0 else 0)

                def hidden(c):
                    g = G[f"m{l}a{c}"]

                    def evacuate(m, src):
                        t = 32 * l + 4 * c + m
                        if t >= 2:
                            act.wait_ge(a_ready, t - 1)
                        nc.scalar.activation(tmp[:, m % 2, :], src, ACT.Relu).then_inc(free_a, 1)
                        act.wait_ge(free_a, g["a"] - 4 + m + 1)
                        if m == 0 and c >= 2:
                            computed(act, f"m{l}b{c - 2}1")
                        nc.scalar.activation(a_hi[c % 2][:, m, :], tmp[:, m % 2, :], ACT.Square).then_inc(a_hi_ready, 1)
                    return evacuate

                group(f"m{l}a0", hidden(0))
                for c in range(8):
                    if c < 7:
                        group(f"m{l}a{c + 1}", hidden(c + 1))
                    group(f"m{l}b{c}0")
                    group(f"m{l}b{c}1", norm_next=(Y1, MIX)[l] if c == 7 else None)
            mlp(0, X2)
            norm(Y1)
            computed(act, "m0a7")
            for g in range(4):
                act.wait_ge(pooled, g + 1)
                nc.scalar.copy(u_hi[:, 2 * g:2 * g + 2, :], tmp[:, :, :]).then_inc(pooled_hi, 1)
            group("p0")
            group("p1")
            mlp(1, Y2)
            norm(MIX, "m1a7")
            group("qa", copy_to(lambda m: qa_t[:, m, :], scale=HD ** -0.5))
            group("kv1", copy_to(lambda m: (kcv_t[:, 0, :], kcv_t[:, 1, :], ks_t[:, :],
                                            v_t[:, 0, :])[m]))

            def window_and_gates(m, src):
                if m < 2:
                    nc.scalar.copy((kw_t[:, :], v_t[:, 1, :])[m], src).then_inc(free_a, 1)
                else:
                    act.wait_ge(gate_loaded, 16)
                    nc.scalar.activation(gate_t[:, :], src[0:3 * NH, :], ACT.Sigmoid, bias=gate_b[:, :])\
                      .then_inc(free_a, 1)
            group("kv2", window_and_gates)
            group("qkb", copy_to(lambda m: qkb[:, m, :]))
            group("vb", copy_to(lambda m: vb[:, m, :]))
            group("rb", lambda m, src: nc.scalar.activation(rb[:, m, :], src, ACT.Silu).then_inc(free_a, 1))
            group("al", copy_to(lambda m: al[:, :]))
            for j in range(4):
                act.wait_ge(hid_done, j + 1)
                nc.scalar.activation(ghid[:, j, 0:NCMP], ps[:, j, 0:NCMP], ACT.Gelu_apprx_tanh).then_inc(hid_ready, 1)

            def parts(i):
                ws, ww = P * (i + 1), P * min(i + 1, 3)
                return (slice(896, 896 + NCMP), slice(0, ws), slice(S, S + ww))

            def ns_exp_of(n):
                act.wait_ge(ns_max, n + 1)
                pr = p_nsa[n % 2]
                for x, c in enumerate(parts(n % TT)):
                    ins = nc.scalar.activation(pr[:, c], pr[:, c], ACT.Exp, bias=stats[:, x, n:n + 1],
                                               accum_out=stats[:, 3 + x, n:n + 1])
                ins.then_inc(ns_exp, 1)

            def ns_keep(n):
                i = n % TT
                act.wait_ge(ns_t, n + 1)
                if n >= 2:
                    act.wait_ge(ns_pv, n - 1)
                pt = pt_nsa[n % 2][:, :, :].rearrange("p a b -> p (a b)")
                ws, ww = P * (i + 1), P * min(i + 1, 3)
                nc.scalar.copy(pt[:, 0:ws], ps[:, 4, 0:ws])
                nc.scalar.copy(pt[:, 512:512 + ww], ps[:, 5, 0:ww])
                nc.scalar.copy(pt[0:NCMP, 896:1024], ps[0:NCMP, 5, 384:512]).then_inc(ns_pt, 1)

            ns_exp_of(0)
            for n in range(NUNIT):
                if n + 1 < NUNIT:
                    ns_exp_of(n + 1)
                ns_keep(n)
            turned_hi(1, lambda j: on_hi[:, j, :], None)

            act.wait_ge(gz_done, 1)
            act.wait_ge(tab_ready, 8)
            for p in range(2):
                nc.scalar.activation(gt[:, p, :], ps[:, p, :], ACT.Abs,
                                     bias=col[:, COL["b_alpha"] + p:COL["b_alpha"] + p + 1]).then_inc(act_chain, 1)
            chain[0] += 2
            act.wait_ge(act_chain, chain[0])
            link(nc.scalar.activation(gt[:, :, :], gt[:, :, :], ACT.Exp, scale=-1.0))
            nc.scalar.activation(gt[:, :, :], gt[:, :, :], ACT.Ln, bias=ones[:, 0:1]).then_inc(gz_log, 1)
            act.wait_ge(gla_b, 1)
            nc.scalar.activation(ga[:, :, :], la[0][:, :, :], ACT.Exp, scale=1.0 / 16).then_inc(gla_e, 1)
            nc.scalar.activation(gt[:, :, :], la[0][:, :, :], ACT.Exp, scale=-1.0 / 16).then_inc(gla_e, 1)
            act.wait_ge(gla_b, 2)
            act.wait_ge(gla_qk, 1)
            nc.scalar.activation(ga[:, :, :], la[1][:, :, :], ACT.Exp, scale=1.0 / 16).then_inc(gla_e, 1)
            nc.scalar.activation(dec[:, :, :], la[0][:, :, CHUNK - 1::CHUNK], ACT.Exp, scale=1.0 / 16)\
              .then_inc(gla_e, 1)
            act.wait_ge(gla_qk, 3)
            for hh in range(4):
                act.wait_ge(go_done, hh + 1)
                if hh >= 2:
                    act.wait_ge(go_sum, hh - 1)
                nc.scalar.activation(gt[:, hh % 2, :], ps[:, 6 + hh % 2, :], ACT.Square).then_inc(go_sq, 1)
                act.wait_ge(go_sum, hh + 1)
                if hh:
                    act.wait_ge(go_t, hh)
                nc.scalar.activation(root[:, :], ps[:, hh % 2, :], ACT.Sqrt, bias=eps[:, :], scale=1.0 / P)\
                  .then_inc(go_root, 1)
                act.wait_ge(go_t, hh + 1)
                nc.scalar.copy(og_hi[:, hh, :], tmp[:, hh % 2, :]).then_inc(go_hi, 1)

            act.wait_ge(go_ready, 4)
            for j in range(4):
                group(f"mg{j}", lambda m, src, j=j: nc.scalar.activation(mg[4 * j + m][:, :], src, ACT.Sigmoid)
                      .then_inc(free_a, 1))

            def mixed(j):
                def evacuate(m, src):
                    act.wait_ge(mix_t, 4 * j + m + 1)
                    nc.scalar.copy(u_hi[:, 4 * j + m, :], tmp[:, m % 2, :]).then_inc(mix_hi, 1)
                return evacuate
            for j in range(2):
                group(f"bn{j}")
                group(f"bg{j}", mixed(j))
            group("ow0")
            group("ow1", norm_next=XAT)

            norm(XAT, "ow1")
            group("xq", copy_to(lambda m: xq_t[:, m, :], scale=float(np.float32(P ** -0.5))))

            def xa_exp_of(n):
                act.wait_ge(xa_max, n + 1)
                if n >= 2:
                    act.wait_ge(xa_t, n - 1)
                nc.scalar.activation(p_x[n % 2][:, :], ps[:, n % 2, 0:L], ACT.Exp, bias=stats[:, 1, n:n + 1],
                                     accum_out=stats[:, 2, n:n + 1]).then_inc(xa_exp, 1)

            def xa_keep(n):
                act.wait_ge(xa_t, n + 1)
                if n >= 2:
                    act.wait_ge(xa_pv, n - 1)
                nc.scalar.copy(pt_x[n % 2][:, :, :].rearrange("p a b -> p (a b)"), ps[:, 2 + n % 2, 0:L])\
                  .then_inc(xa_pt, 1)

            xa_exp_of(0)
            for n in range(4 * TT):
                if n + 1 < 4 * TT:
                    xa_exp_of(n + 1)
                xa_keep(n)
            turned_hi(2, lambda j: xo_hi[:, j, :], None)
            group("xo0")
            group("xo1", norm_next=FF)

            norm(FF, "xq")
            for c, nt in enumerate(FC):
                def conv(m, src, c=c):
                    t = 4 * c + m
                    act.wait_ge(tile_done, G[f"fu{c}"]["tile0"] + m + 1)
                    w0 = COL["conv_w"] + 2 * FT + t
                    nc.scalar.activation(cv[:, m, :], src, ACT.Identity, scale=col[:, w0:w0 + 1],
                                         bias=col[:, COL["conv_b"] + t:COL["conv_b"] + t + 1]).then_inc(c_ready, 1)

                group(f"fu{c}", conv)
                for m in range(nt):
                    act.wait_ge(free_d, G[f"fu{c}"]["d"] - nt + m + 1)
                    nc.scalar.activation(ub[:, m, :], cv[:, m, :], ACT.Gelu_apprx_tanh).then_inc(c_gelu, 1)

                def gated(m, src, c=c, nt=nt):
                    act.wait_ge(free_d, G[f"fg{c}"]["d"] - nt + m + 1)
                    if m == 0 and c >= 2:
                        computed(act, f"fd{c - 2}1")
                    nc.scalar.copy(a_hi[c % 2][:, m, :], tmp[:, m % 2, :]).then_inc(f_hi, 1)
                group(f"fg{c}", gated)
                group(f"fd{c}0")
                group(f"fd{c}1", norm_next=FIN if c == len(FC) - 1 else None)
            norm(FIN)

        @block.gpsimd
        def _(pool):
            nc.gpsimd.memset(eps[:, :], EPS)
            nc.gpsimd.memset(ones[:, :], 1.0).then_inc(ones_set, 1)

            def split(n):
                pool.wait_ge(w_hi_ready, n + 1)
                nc.gpsimd.tensor_tensor(part_panel(w_lo, n), raw_panel(n), part_panel(w_hi, n).bitcast(F32),
                                        ALU.subtract).then_inc(w_lo_ready, 1)

            def through(name, n0):
                n1 = min(G[name]["panels"][-1] + 3, NPAN)
                for n in range(n0, n1):
                    split(n)
                return n1

            def pool_mod(y):
                _, k, _, acc, _ = mod_tile(1, y)
                pool.wait_ge(mod_scaled, y + 1)
                if k == 0:
                    pool.sem_inc(mod_pooled, 1)
                else:
                    nc.gpsimd.tensor_tensor(acc, acc, mod_product(y), ALU.add).then_inc(mod_pooled, 1)
                    pool.wait_ge(mod_pooled, y + 1)

            split(0)
            split(1)
            for mk in range(FIRST_K // 2):
                pool_mod(mk)
            split(2)
            split(3)
            for mk in range(FIRST_K // 2, FIRST_K):
                pool_mod(mk)
            n0 = through("vc", 4)
            pool.wait_ge(ones_set, 1)
            nc.gpsimd.memset(pad[:, :], 0.0).then_inc(pad_set, 1)
            for mk in range(FIRST_K, FIRST_K + 2 * PIECES):
                pool_mod(mk)
            n0 = through("m0b71", n0)
            n0 = through("p1", n0)
            n0 = through("m1b71", n0)
            n0 = through("al", n0)
            pool.wait_ge(hid_done, 4)
            pool.wait_ge(free_a, G["kv2"]["a"])
            pool.wait_ge(w_lo_ready, n0)
            for x, (own, other) in enumerate(((ks_t, ks_o), (kw_t, kw_o))):
                nc.gpsimd.memset(other[0:HD, :], 0.0).then_inc(keys_apart, 1)
                pool.wait_ge(keys_apart, 3 * x + 1)
                nc.gpsimd.tensor_copy(other[HD:P, :], own[HD:P, :]).then_inc(keys_apart, 1)
                pool.wait_ge(keys_apart, 3 * x + 2)
                nc.gpsimd.memset(own[HD:P, :], 0.0).then_inc(keys_apart, 1)
                pool.wait_ge(keys_apart, 3 * x + 3)
            pool.wait_ge(tab_loaded, 32)
            for hh in range(NH):
                if hh >= 2:
                    pool.wait_ge(ns_max, 4 * (hh - 1))
                nc.gpsimd.tensor_scalar(ntab[hh % 2][:, :], tab[:, :], SLOPES[hh], 1.0, ALU.mult, ALU.mult)\
                  .then_inc(tab_ready, 1)
            pool.wait_ge(ot_turned, 8)
            for i in range(2):
                nc.gpsimd.memset(att[i][:, :, :], 0.0).then_inc(att_zero, 1)
            through("fd51", n0)

        @block.vector
        def _(dve):
            chain = [0]

            def link(ins):
                chain[0] += 1
                ins.then_inc(dve_chain, 1)
                dve.wait_ge(dve_chain, chain[0])

            for n in range(16):
                i, half = n // 2, n % 2
                dve.wait_ge(tok_turned, n + 1)
                dst, t = ((mem_t, i) if i < 2 else (ctx_t, i - 2) if i < 4 else (h, i - 4))
                nc.vector.tensor_copy(dst[:, 4 * half:4 * half + 4, P * t:P * t + P],
                                      ps[:, n % 4, :].rearrange("p (a b) -> p a b", a=4)).then_inc(tok_kept, 1)
                if n == 3:
                    dve.wait_ge(rows_turned, 1)
                    nc.vector.tensor_copy(col[:, :], ps[:, 4, 0:NCOL]).then_inc(col_ready, 1)
            dve.wait_ge(col_ready, 1)
            dve.wait_ge(tok_kept, 16)

            def norm(n, dst=None):
                t = ncols.get(n, S)
                dve.wait_ge(root_ready, n + 1)
                nc.vector.reciprocal(rstd[:, 0:t], root[:, 0:t]).then_inc(rstd_ready, 1)
                dve.wait_ge(rstd_ready, n + 1)

                def lower(k):
                    hi, lo = pair(n, k)
                    dve.wait_ge(n_hi_ready, PAIRED[n] + k + 1)
                    if n in (MEM, MIX, XAT, FF):
                        ins = nc.vector.tensor_tensor(lo, tmp[:, k % 2, 0:t], hi.bitcast(F32), ALU.subtract)
                    else:
                        ins = nc.vector.scalar_tensor_tensor(lo, tmp[:, k % 2, 0:t], shift(n, k), hi.bitcast(F32),
                                                             ALU.add, ALU.subtract)
                    ins.then_inc(n_ready, 1)

                if n == FIN:
                    for k in range(KT):
                        nc.vector.scalar_tensor_tensor(y[:, k, :], h[:, k, :], gain(n, k), rstd[:, :], ALU.mult,
                                                       ALU.mult).then_inc(n_ready, 1)
                    return
                if n == Y1:
                    return
                for k in range(KT):
                    if k >= 2:
                        dve.wait_ge(n_ready, 8 * n + k - 1)
                    nc.vector.scalar_tensor_tensor(tmp[:, k % 2, 0:t], source(n, k), gain(n, k), rstd[:, 0:t],
                                                   ALU.mult, ALU.mult).then_inc(t_ready, 1)
                    if k:
                        lower(k - 1)
                lower(KT - 1)

            def add_mod(y):
                w, k, loaded, acc, summed = mod_tile(0, y)
                dve.wait_ge(*loaded)
                if k == 0 and summed > 0:
                    dve.wait_ge(mod_summed, summed)
                if k == 0:
                    ins = nc.vector.tensor_scalar(acc, w, silu[:, k, 0:1], None, ALU.mult)
                else:
                    ins = nc.vector.scalar_tensor_tensor(acc, w, silu[:, k, 0:1], acc, ALU.mult, ALU.add)
                ins.then_inc(mod_added, 1)
                dve.wait_ge(mod_added, y + 1)

            def modulation(stage):
                b0, n0 = COL["b_mod"], 4 * MOD_FIRST
                if stage == 0:
                    dve.wait_ge(mod_summed, MOD_FIRST)
                    link(nc.vector.tensor_tensor(modc[:, 0, 0:n0, :],
                                                 ps[:, 6, 0:2 * n0].rearrange("p (a b) -> p a b", b=2),
                                                 col[:, b0:b0 + n0].unsqueeze(2).broadcast_to([P, n0, 2]), ALU.add))
                    jobs = [(CTX, 8, 1, 0, "norm1"), (X1, 8, 0, 0, "norm1")]
                elif stage == 1:
                    dve.wait_ge(mod_summed, MOD_PARTS)
                    link(nc.vector.tensor_tensor(modc[:, 0, n0:48, 0], ps[:, 7, 0:48 - n0], col[:, b0 + n0:b0 + 48],
                                                 ALU.add))
                    jobs = [(X2, 32, 0, 0, "norm2")]
                else:
                    dve.wait_ge(free_d, G["mc2"]["d"])
                    link(nc.vector.tensor_tensor(modc[:, 1, :, 0], modc[:, 1, :, 0], col[:, b0 + 48:b0 + 96], ALU.add))
                    jobs = [(Y1, 8, 0, 1, "norm1"), (Y2, 32, 0, 1, "norm2")]
                for n, t0, src, l, name in jobs:
                    c0 = COL[name] + 8 * l
                    ins = nc.vector.scalar_tensor_tensor(gcol[:, n, :], modc[:, l, t0:t0 + 8, src], 1.0,
                                                         col[:, c0:c0 + 8], ALU.add, ALU.mult)
                if stage == 2:
                    c0 = COL["pool_scale"]
                    ins = nc.vector.tensor_tensor(gcol[:, 6, :], modc[:, 1, 16:24, 0], col[:, c0:c0 + 8], ALU.mult)
                ins.then_inc(mod_ready, 1)
                dve.wait_ge(mod_ready, stage + 1)

            def residual(name, j, gate_of=None):
                g = G[name]
                if g["d"] > 4:
                    dve.wait_ge(free_d, g["d"] - 4)
                for m in range(4):
                    dve.wait_ge(tile_done, g["tile0"] + m + 1)
                    k = 4 * j + m
                    src = ps[:, g["bank0"] + m, :]
                    if gate_of:
                        ins = nc.vector.scalar_tensor_tensor(h[:, k, :], src, gate_of(k), h[:, k, :], ALU.mult, ALU.add)
                    else:
                        ins = nc.vector.tensor_tensor(h[:, k, :], src, h[:, k, :], ALU.add)
                    ins.then_inc(free_d, 1)

            norm(MEM)
            dve.wait_ge(silu_ready, 2)
            for mk in range(FIRST_K):
                add_mod(mk)
            modulation(0)
            norm(CTX)
            norm(X1)

            for x in range(2):
                ins = nc.vector.scalar_tensor_tensor(gcol[:, 7, x:x + 1], col[:, COL["qg"]:COL["qg"] + 1], HD ** -0.5,
                                                     halves[:, HD * x:HD * x + 1], ALU.mult, ALU.mult)
            link(ins)
            def head_norm(n):
                dve.wait_ge(hn_root, n + 1)
                if n >= 2:
                    dve.wait_ge(qk_ready, n - 1)
                link(nc.vector.reciprocal(tmp[:, n % 2, :], ga[:, n % 2, :]))
                x = q_t[:, n, :] if n < 4 else k_t[:, n - 4, :] if n < 8 else kc_t[:, 2 * n - 16:2 * n - 14, :]
                g = gcol[:, 7, 0:1] if n < 4 else col[:, COL["kg"]:COL["kg"] + 1]
                r = tmp[:, n % 2, :]
                if n >= 8:
                    r = r.rearrange("p (a b) -> p a b", a=2)
                if n < 4:
                    link(nc.vector.scalar_tensor_tensor(q_o[:, n, :], x, gcol[:, 7, 1:2], r, ALU.mult, ALU.mult))
                nc.vector.scalar_tensor_tensor(x, x, g, r, ALU.mult, ALU.mult).then_inc(qk_ready, 1)

            def fourier_lower(g):
                dve.wait_ge(four_hi, g + 1)
                nc.vector.tensor_tensor(u_lo[:, g, :], ps[:, 4 + g % 2, :], u_hi[:, g, :].bitcast(F32), ALU.subtract)\
                   .then_inc(four_kept, 1)

            head_norm(0)
            head_norm(1)
            dve.wait_ge(cw_done, 1)
            nc.vector.tensor_copy(cw[:, :, :].rearrange("p a b -> p (a b)"),
                                  ps[:, 0:2, :].rearrange("p a b -> p (a b)")).then_inc(cw_ready, 1)
            for g in range(4):
                head_norm(2 * g + 2)
                head_norm(2 * g + 3)
                if g:
                    fourier_lower(g - 1)
            fourier_lower(3)

            dve.wait_ge(pad_loaded, 32)
            dve.wait_ge(pad_set, 1)
            nc.vector.tensor_copy(pad[:, 48:79], rpb_in[:, ::-1]).then_inc(pad_set, 1)

            def bias_ready(hh):
                dve.wait_ge(gb_loaded[hh % 2], 32 * (hh // 2 + 1))
                nc.vector.tensor_tensor(gb[hh % 2][:, :, :], gb[hh % 2][:, :, :],
                                        near[:, :].unsqueeze(1).broadcast_to([P, 14, GRID]), ALU.add)\
                   .then_inc(gb_ready, 1)

            def na_scores(n):
                hh, i, b = n // TT, n % TT, 2 * (n % 2)
                dve.wait_ge(na_s, n + 1)
                dve.wait_ge(gb_ready, hh + 1)
                if n >= 2:
                    dve.wait_ge(na_t, n - 1)
                nc.vector.tensor_tensor_reduce(p_na[n % 2][:, 0:S].rearrange("p (a b) -> p a b", b=GRID),
                                               ps[:, b, :].rearrange("p (a b) -> p a b", b=GRID),
                                               gb[hh % 2][:, 6 - 2 * i:14 - 2 * i, ::-1],
                                               1.0, NEG, ALU.add, ALU.max, stats[:, 0, n:n + 1])
                link(nc.vector.reduce_max(stats[:, 1, n:n + 1], ps[:, b + 1, 0:L], X))
                nc.vector.tensor_scalar(stats[:, 4, n:n + 1], stats[:, 0, n:n + 1], stats[:, 1, n:n + 1], -1.0,
                                        ALU.max, ALU.mult).then_inc(na_max, 1)

            def na_out(n):
                hh, i = n // TT, n % TT
                dve.wait_ge(na_pv, n + 1)
                link(nc.vector.tensor_tensor(stats[:, 5, n:n + 1], stats[:, 2, n:n + 1], stats[:, 3, n:n + 1], ALU.add))
                link(nc.vector.reciprocal(stats[:, 6, n:n + 1], stats[:, 5, n:n + 1]))
                nc.vector.tensor_scalar(o_na[:, i, HD * hh:HD * hh + HD], ps[:, 6 + n % 2, 256:256 + HD],
                                        stats[:, 6, n:n + 1], None, ALU.mult).then_inc(na_o, 1)

            bias_ready(0)
            na_scores(0)
            for n in range(NUNIT):
                if n + 1 < NUNIT:
                    na_scores(n + 1)
                if n % TT == 1 and n // TT + 1 < NH:
                    bias_ready(n // TT + 1)
                if n >= 2:
                    na_out(n - 2)
                for x in pieces_after(n):
                    for mk in (2 * x, 2 * x + 1):
                        add_mod(FIRST_K + mk)
            na_out(NUNIT - 2)
            na_out(NUNIT - 1)
            modulation(1)

            def turned_lo(which, hi, lo):
                for j in range(4):
                    dve.wait_ge(ot_hi, 4 * which + j + 1)
                    nc.vector.tensor_tensor(lo(j), ps[:, j, :], hi(j).bitcast(F32), ALU.subtract).then_inc(ot_kept, 1)

            turned_lo(0, lambda j: u_hi[:, 4 + j, :], lambda j: u_lo[:, 4 + j, :])
            for j in range(2):
                residual(f"o{j}", j, lambda k: g_mod(0, False, k))

            def add_mod1(i):
                dve.wait_ge(mod1_loaded[i % 2], 16 * (i // 2 + 1))
                acc = mod_sums[:, i // 2, :]
                for kk in range(4):
                    k = 4 * (i % 2) + kk
                    if k == 0:
                        ins = nc.vector.tensor_scalar(acc, mod_panels[i % 2][:, kk, :], silu[:, k, 0:1], None, ALU.mult)
                    else:
                        ins = nc.vector.scalar_tensor_tensor(acc, mod_panels[i % 2][:, kk, :], silu[:, k, 0:1], acc,
                                                             ALU.mult, ALU.add)
                    ins.then_inc(mod1_added, 1)
                    dve.wait_ge(mod1_added, 4 * i + kk + 1)

            def sum_mod(name):
                g, x = G[name], int(name[2])
                for m in range(4):
                    dve.wait_ge(tile_done, g["tile0"] + m + 1)
                    j = 4 * (4 * x + m)
                    nc.vector.reduce_sum(modc[:, 1, j:j + 4, 0],
                                         ps[:, g["bank0"] + m, :].rearrange("p (a b) -> p a b", a=4), X)\
                      .then_inc(free_d, 1)

            def mlp(l, n):
                norm(n)

                def hidden(c):
                    g = G[f"m{l}a{c}"]
                    for m in range(4):
                        t = 32 * l + 4 * c + m
                        dve.wait_ge(free_a, g["a"] - 4 + m + 1)
                        link(nc.vector.tensor_tensor(sq[:, m % 2, :], tmp[:, m % 2, :], tmp[:, m % 2, :], ALU.mult))
                        dve.wait_ge(a_hi_ready, t + 1)
                        nc.vector.tensor_tensor(a_lo[c % 2][:, m, :], sq[:, m % 2, :],
                                                a_hi[c % 2][:, m, :].bitcast(F32), ALU.subtract).then_inc(a_ready, 1)

                hidden(0)
                for c in range(8):
                    if c < 7:
                        hidden(c + 1)
                    here = l == 0 and c < 6
                    if here:
                        add_mod1(4 * c)
                    for j in range(2):
                        residual(f"m{l}b{c}{j}", j, lambda k: g_mod(l, True, k))
                        if here:
                            add_mod1(4 * c + 1 + j)
                    if here:
                        add_mod1(4 * c + 3)
                    if f"m{l}b{c}1" in MOD_AFTER:
                        sum_mod(MOD_AFTER[f"m{l}b{c}1"])

            mlp(0, X2)

            modulation(2)
            for k in range(KT):
                nc.vector.memset(up[:, k, 0:8], 0.0)
                nc.vector.memset(up[:, k, 8 + S:16 + S], 0.0)
            norm(Y1)
            dve.wait_ge(cnt_loaded, 16)
            for g in range(4):
                if g:
                    dve.wait_ge(pooled_ready, g)
                    dve.wait_ge(pooled_hi, g)
                for k in range(2 * g, 2 * g + 2):
                    link(nc.vector.scalar_tensor_tensor(tmp[:, k % 2, :], h[:, k, :], gain(Y1, k), rstd[:, :],
                                                        ALU.mult, ALU.mult))
                    nc.vector.tensor_scalar(up[:, k, 8:8 + S], tmp[:, k % 2, :], shift(Y1, k), None, ALU.add)\
                      .then_inc(n_ready, 1)
                dve.wait_ge(n_ready, 8 * Y1 + 2 * g + 2)
                src, reach = up[:, 2 * g:2 * g + 2, :], 1
                a0, a1 = 1, S + 16
                link(nc.vector.tensor_tensor(win[0][:, :, a0:a1], src[:, :, a0 - 1:a1 - 1], src[:, :, a0:a1], ALU.add))
                now = 0
                for _ in range(g):
                    a0, a1 = a0 + reach, a1 - reach
                    link(nc.vector.tensor_tensor(win[1 - now][:, :, a0:a1], win[now][:, :, a0 - reach:a1 - reach],
                                                 win[now][:, :, a0 + reach:a1 + reach], ALU.add))
                    now, reach = 1 - now, 2 * reach
                link(nc.vector.tensor_tensor(win[1 - now][:, :, 0:S], win[now][:, :, 8:8 + S],
                                             cnt[:, g:g + 1, :].broadcast_to([P, 2, S]), ALU.mult))
                nc.vector.tensor_tensor(tmp[:, :, :], win[1 - now][:, :, 0:S], src[:, :, 8:8 + S], ALU.subtract)\
                   .then_inc(pooled, 1)
                dve.wait_ge(pooled_hi, g + 1)
                nc.vector.tensor_tensor(u_lo[:, 2 * g:2 * g + 2, :], tmp[:, :, :],
                                        u_hi[:, 2 * g:2 * g + 2, :].bitcast(F32), ALU.subtract).then_inc(pooled_ready, 1)
            for j in range(2):
                residual(f"p{j}", j, lambda k: gcol[:, 6, k:k + 1])
            mlp(1, Y2)
            norm(MIX)

            dve.wait_ge(pos_turned, 1)
            link(nc.vector.tensor_copy(pos[:, :, :].rearrange("p a b -> p (a b)"), ps[:, 6, 0:64]))
            dve.wait_ge(free_a, G["al"]["a"])
            for x in range(2):
                for hh in range(2):
                    src = slice(HD * hh, HD * hh + HD)
                    for g in range(2):
                        ins = nc.vector.tensor_tensor(
                            kpos[x][HD * g:HD * g + HD, hh, 0:16 * NCMP].rearrange("p (n l) -> p n l", l=16),
                            kcv_t[src, x, 16 * g:16 * g + 16 * NCMP].rearrange("p (n l) -> p n l", l=16),
                            pos[src, x, 16 * g:16 * g + 16].unsqueeze(1).broadcast_to([HD, NCMP, 16]), ALU.add)
                    ins.then_inc(kpos_ready, 1)
            dve.wait_ge(v_turned, 1)
            for x in range(2):
                nc.vector.tensor_copy((vs, vw)[x][:, :, :].rearrange("p a b -> p (a b)"), ps[:, (7, 4)[x], :])
            nc.vector.tensor_copy(gate[:, :, :].rearrange("p a b -> p (a b)"), ps[:, 5, 0:96]).then_inc(v_kept, 1)
            dve.wait_ge(v_kept, 1)
            dve.wait_ge(cmp_done, 1)
            lower, upper = slice(0, HD), slice(HD, P)
            nc.vector.memset(kcm[upper, :], 0.0)
            nc.vector.memset(kcm_o[lower, :], 0.0)
            nc.vector.tensor_copy(kcm[lower, 0:NCMP], ps[lower, 4, 0:NCMP])
            nc.vector.tensor_copy(kcm_o[upper, 0:NCMP], ps[upper, 4, 0:NCMP])
            nc.vector.tensor_copy(vcm[:, :, :].rearrange("p a b -> p (a b)"), ps[0:NCMP, 5, 0:P])
            dve.wait_ge(tab_loaded, 32)
            for i in range(TT):
                ins = nc.vector.tensor_scalar(gate[:, i, 0:24:3], gate[:, i, 0:24:3], valid[:, i:i + 1], None, ALU.mult)
            ins.then_inc(cmp_ready, 1)
            dve.wait_ge(cmp_ready, 1)

            def ns_scores(n):
                hh, i, b = n // TT, n % TT, 2 * (n % 2)
                ws, ww = P * (i + 1), P * min(i + 1, 3)
                t = ntab[hh % 2]
                pr = p_nsa[n % 2]
                dve.wait_ge(ns_s, n + 1)
                dve.wait_ge(tab_ready, hh + 1)
                if n >= 2:
                    dve.wait_ge(ns_t, n - 1)
                for x, (dst, src, bias) in enumerate((
                        (pr[:, 896:896 + NCMP], ps[:, b + 1, 384:384 + NCMP],
                         t[:, 896 + NCMP * i:896 + NCMP * i + NCMP]),
                        (pr[:, 0:ws], ps[:, b, 0:ws], t[:, S - ws:S]),
                        (pr[:, S:S + ww], ps[:, b + 1, 0:ww], t[:, 896 - ww:896]))):
                    ins = nc.vector.tensor_tensor_reduce(dst, src, bias, 1.0, 3.0e38 * -1, ALU.add, ALU.max,
                                                         stats[:, x, n:n + 1])
                link(ins)
                nc.vector.tensor_scalar(stats[:, 0:3, n], stats[:, 0:3, n], -1.0, None, ALU.mult).then_inc(ns_max, 1)

            def ns_out(n):
                hh, i, b = n // TT, n % TT, 6 + n % 2
                dve.wait_ge(ns_pv, n + 1)
                c = stats[:, 3:6, n]
                link(nc.vector.reciprocal(c, c))
                link(nc.vector.tensor_tensor(c, c, gate[:, i, 3 * hh:3 * hh + 3], ALU.mult))
                o = o_nsa[:, i, HD * hh:HD * hh + HD]
                link(nc.vector.tensor_scalar(o, ps[:, b, 0:HD], stats[:, 4, n:n + 1], None, ALU.mult))
                link(nc.vector.scalar_tensor_tensor(o, ps[:, b, HD:2 * HD], stats[:, 5, n:n + 1], o, ALU.mult, ALU.add))
                nc.vector.scalar_tensor_tensor(o, ps[:, b, 2 * HD:3 * HD], stats[:, 3, n:n + 1], o, ALU.mult, ALU.add)\
                   .then_inc(ns_o, 1)

            ns_scores(0)
            for n in range(NUNIT):
                if n + 1 < NUNIT:
                    ns_scores(n + 1)
                if n >= 2:
                    ns_out(n - 2)
            ns_out(NUNIT - 2)
            ns_out(NUNIT - 1)
            turned_lo(1, lambda j: on_hi[:, j, :], lambda j: on_lo[:, j, :])

            dve.wait_ge(gz_log, 1)
            for p in range(2):
                ins = nc.vector.tensor_scalar(ga[:, p, :], ps[:, p, :],
                                              col[:, COL["b_alpha"] + p:COL["b_alpha"] + p + 1], 0.0, ALU.add, ALU.min)
            link(ins)
            link(nc.vector.tensor_tensor(la[0][:, :, :], ga[:, :, :], gt[:, :, :], ALU.subtract))

            def chunks(t):
                return t[:, :, :].rearrange("p a (c j) -> p (a c) j", j=CHUNK)

            now, reach = 0, 1
            while reach < CHUNK:
                x, y_ = chunks(la[now]), chunks(la[1 - now])
                nc.vector.tensor_copy(y_[:, :, 0:reach], x[:, :, 0:reach])
                ins = nc.vector.tensor_tensor(y_[:, :, reach:], x[:, :, reach:], x[:, :, :CHUNK - reach], ALU.add)
                now, reach = 1 - now, 2 * reach
                if reach < CHUNK:
                    link(ins)
            ins.then_inc(gla_b, 1)
            dve.wait_ge(gla_b, 1)
            b = chunks(la[0])
            nc.vector.tensor_tensor(chunks(la[1]), b[:, :, CHUNK - 1:CHUNK].broadcast_to([P, 2 * NCH, CHUNK]), b,
                                    ALU.subtract).then_inc(gla_b, 1)
            dve.wait_ge(gla_e, 1)
            nc.vector.scalar_tensor_tensor(qd[:, :, :], qkb[:, 0:2, :], HD ** -0.5, ga[:, :, :], ALU.mult, ALU.mult)\
               .then_inc(gla_qk, 1)
            dve.wait_ge(gla_e, 2)
            nc.vector.tensor_tensor(kd[:, :, :], qkb[:, 2:4, :], gt[:, :, :], ALU.mult).then_inc(gla_qk, 1)
            dve.wait_ge(gla_e, 3)
            nc.vector.tensor_tensor(ks[:, :, :], qkb[:, 2:4, :], ga[:, :, :], ALU.mult).then_inc(gla_qk, 1)
            dve.wait_ge(kst_done, 1)
            nc.vector.tensor_copy(kst[:, :, :].rearrange("p a b -> p (a b)"),
                                  ps[:, 2:4, :].rearrange("p a b -> p (a b)")).then_inc(kst_ready, 1)
            dve.wait_ge(inc_done, 1)
            dve.wait_ge(gla_e, 4)
            for c in range(NCH - 1):
                for p in range(2):
                    inc = ps[:, 2 * p + c % 2, P * (c // 2):P * (c // 2) + P]
                    if c == 0:
                        ins = nc.vector.tensor_copy(st[:, p, 1, :], inc)
                    else:
                        ins = nc.vector.scalar_tensor_tensor(st[:, p, c + 1, :], st[:, p, c, :], dec[:, p, c:c + 1],
                                                             inc, ALU.mult, ALU.add)
                if c < NCH - 2:
                    link(ins)
            ins.then_inc(st_ready, 1)
            dve.wait_ge(att_zero, 2)
            dve.wait_ge(gmask_loaded, 16)

            def gla_attention(hh):
                dve.wait_ge(att_done, hh + 1)
                if hh >= 2:
                    dve.wait_ge(go_done, hh - 1)
                nc.vector.copy_predicated(att[hh % 2][:, :, :], gmask[:, :].unsqueeze(1).broadcast_to([P, TT, P]),
                                          ps[:, 4 + hh % 2, :].rearrange("p (a b) -> p a b", a=TT))\
                   .then_inc(att_ready, 1)

            def gla_norm(hh):
                o = ps[:, 6 + hh % 2, :]
                t = tmp[:, hh % 2, :]
                dve.wait_ge(go_root, hh + 1)
                link(nc.vector.reciprocal(rstd[:, :], root[:, :]))
                link(nc.vector.scalar_tensor_tensor(t, o, col[:, COL["gla_norm"]:COL["gla_norm"] + 1], rstd[:, :],
                                                    ALU.mult, ALU.mult))
                nc.vector.tensor_tensor(t, t, rb[:, hh, :], ALU.mult).then_inc(go_t, 1)
                dve.wait_ge(go_hi, hh + 1)
                nc.vector.tensor_tensor(og_lo[:, hh, :], t, og_hi[:, hh, :].bitcast(F32), ALU.subtract)\
                   .then_inc(go_ready, 1)

            gla_attention(0)
            for hh in range(4):
                if hh < 3:
                    gla_attention(hh + 1)
                gla_norm(hh)

            for j in range(2):
                gn, gg = G[f"bn{j}"], G[f"bg{j}"]
                for m in range(4):
                    dve.wait_ge(tile_done, gn["tile0"] + m + 1)
                    nc.vector.tensor_tensor(mixn[:, m, :], ps[:, gn["bank0"] + m, :], mg[4 * j + m][:, :], ALU.mult)\
                       .then_inc(free_d, 1)
                for m in range(4):
                    dve.wait_ge(tile_done, gg["tile0"] + m + 1)
                    k = 4 * j + m
                    nc.vector.tensor_tensor(tmp[:, m % 2, :], ps[:, gg["bank0"] + m, :], mg[8 + k][:, :], ALU.mult)\
                       .then_inc(free_d, 1)
                    dve.wait_ge(free_d, gg["d"] - 4 + m + 1)
                    nc.vector.tensor_tensor(tmp[:, m % 2, :], tmp[:, m % 2, :], mixn[:, m, :], ALU.add)\
                       .then_inc(mix_t, 1)
                    dve.wait_ge(mix_hi, k + 1)
                    nc.vector.tensor_tensor(u_lo[:, k, :], tmp[:, m % 2, :], u_hi[:, k, :].bitcast(F32), ALU.subtract)\
                       .then_inc(mix_ready, 1)
            for j in range(2):
                residual(f"ow{j}", j)
            norm(XAT)

            def xa_max_of(n):
                dve.wait_ge(xa_s, n + 1)
                link(nc.vector.reduce_max(stats[:, 0, n:n + 1], ps[:, n % 2, 0:L], X))
                nc.vector.tensor_scalar(stats[:, 1, n:n + 1], stats[:, 0, n:n + 1], -1.0, None, ALU.mult)\
                   .then_inc(xa_max, 1)

            def xa_out(n):
                hh, i = n // TT, n % TT
                dve.wait_ge(xa_pv, n + 1)
                link(nc.vector.reciprocal(stats[:, 3, n:n + 1], stats[:, 2, n:n + 1]))
                nc.vector.tensor_scalar(o_x[:, i, P * hh:P * hh + P], ps[:, 4 + n % 2, 0:P], stats[:, 3, n:n + 1],
                                        None, ALU.mult).then_inc(xa_o, 1)

            xa_max_of(0)
            for n in range(4 * TT):
                if n + 1 < 4 * TT:
                    xa_max_of(n + 1)
                if n >= 2:
                    xa_out(n - 2)
            xa_out(4 * TT - 2)
            xa_out(4 * TT - 1)
            turned_lo(2, lambda j: xo_hi[:, j, :], lambda j: xo_lo[:, j, :])
            for j in range(2):
                residual(f"xo{j}", j)

            norm(FF)
            for c, nt in enumerate(FC):
                gu, gg = G[f"fu{c}"], G[f"fg{c}"]
                for m in range(nt):
                    t = 4 * c + m
                    src = ps[:, gu["bank0"] + m, :]
                    w0 = COL["conv_w"] + t
                    dve.wait_ge(c_ready, t + 1)
                    link(nc.vector.scalar_tensor_tensor(cv[:, m, 1:], src[:, :S - 1], col[:, w0 + FT:w0 + FT + 1],
                                                        cv[:, m, 1:], ALU.mult, ALU.add))
                    nc.vector.scalar_tensor_tensor(cv[:, m, 2:], src[:, :S - 2], col[:, w0:w0 + 1], cv[:, m, 2:],
                                                   ALU.mult, ALU.add).then_inc(free_d, 1)
                for m in range(nt):
                    t = 4 * c + m
                    dve.wait_ge(tile_done, gg["tile0"] + m + 1)
                    dve.wait_ge(c_gelu, t + 1)
                    nc.vector.tensor_tensor(tmp[:, m % 2, :], ps[:, gg["bank0"] + m, :], ub[:, m, :], ALU.mult)\
                       .then_inc(free_d, 1)
                    dve.wait_ge(f_hi, t + 1)
                    nc.vector.tensor_tensor(a_lo[c % 2][:, m, :], tmp[:, m % 2, :],
                                            a_hi[c % 2][:, m, :].bitcast(F32), ALU.subtract).then_inc(f_pair, 1)
                for j in range(2):
                    residual(f"fd{c}{j}", j)
            norm(FIN)
            for n in range(2 * TT):
                i, half = n // 2, n % 2
                dve.wait_ge(out_turned, n + 1)
                if i >= 2 and half == 0:
                    dve.wait_ge(out_stored[i % 2], 16 * (i // 2))
                nc.vector.tensor_copy(y_out[i % 2][:, 512 * half:512 * half + 512], ps[:, n % 4, :]).then_inc(out_kept, 1)


_OUT = (1, S, D)


def kernel(**inputs):
    import concourse.bacc as _bacc
    from concourse.bass_utils import run_bass_kernel_spmd as _run

    nc = _bacc.Bacc("TRN2", target_bir_lowering=False, num_devices=1)
    arrays, aps = {}, {}
    for name, value in {**inputs, **host_constants()}.items():
        value = np.ascontiguousarray(value)
        arrays[f"in_{name}"] = value
        aps[name] = nc.dram_tensor(f"in_{name}", value.shape, mybir.dt.from_np(value.dtype), kind="ExternalInput").ap()
    out = nc.dram_tensor("out_y", _OUT, F32, kind="ExternalOutput").ap()
    build(nc, aps, out)
    r = _run(nc, [arrays], core_ids=[0])
    return r.results[0]["out_y"]
```
